# Optimizing a Trainium2 kernel written in Bass

```python
import math
import numpy as np
import jax
import jax.numpy as jnp
from jax import lax

"""One inference step (DEPTH layers) of a conditioned hybrid decoder trunk, run for a prompt group and a sample group with shared weights.

Layer: adaLN-modulated RMSNorm -> single combined input projection whose columns are partitioned among
  branch A: gated linear attention (GLA, low-rank data-dependent forget gate, chunked exact per-token recurrence), and
  branch B: dilated sliding-window attention, head groups (window,dilation) = (128,1),(512,4),(2048,16), keys gathered by stride,
            shared T5 relative bias, group outputs combined with weights proportional to their softmax denominators,
  plus two per-channel branch gates; each branch projected to D_MODEL, sigmoid-gated sum, one output projection, adaLN-gated residual;
  then adaLN-modulated RMSNorm -> gated ConvFFN (causal depthwise conv width 3 on the activation branch) -> adaLN-gated residual.
Final RMSNorm.

Inputs: x_prompt (BATCH,SEQ,D_MODEL); x_sample (DEC_BATCH,DEC_SEQ,D_MODEL);
  state_gla (DEPTH,DEC_BATCH,GLA_HEADS,GLA_DK,GLA_DV);
  cache_win1/2/3 (DEPTH,DEC_BATCH,min(W_g,PAST_LEN),2,ATT_HEADS_PER_GROUP,ATT_HEAD_DIM): K (index 0) / V (index 1) of the last positions;
  state_conv (DEPTH,DEC_BATCH,CONV_W-1,FFN_HIDDEN); c_prompt (BATCH,D_MODEL); c_sample (DEC_BATCH,D_MODEL); weights.
Returns (y_prompt (BATCH,SEQ,D_MODEL), y_sample (DEC_BATCH,DEC_SEQ,D_MODEL),
  state_gla_prompt (DEPTH,BATCH,4,128,256), state_gla_sample (DEPTH,DEC_BATCH,4,128,256),
  cache_win1_prompt (DEPTH,BATCH,min(128,SEQ),2,8,64), cache_win1_sample (DEPTH,DEC_BATCH,min(128,PAST_LEN),2,8,64),
  cache_win2_prompt (DEPTH,BATCH,min(512,SEQ),2,8,64), cache_win2_sample (DEPTH,DEC_BATCH,min(512,PAST_LEN),2,8,64),
  cache_win3_prompt (DEPTH,BATCH,min(2048,SEQ),2,8,64), cache_win3_sample (DEPTH,DEC_BATCH,min(2048,PAST_LEN),2,8,64),
  state_conv_prompt (DEPTH,BATCH,2,FFN_HIDDEN), state_conv_sample (DEPTH,DEC_BATCH,2,FFN_HIDDEN)).
"""

D_MODEL = 1024
BATCH = 1
SEQ = 512
DEPTH = 1
DEC_BATCH = 8
DEC_SEQ = 1
PAST_LEN = 1024
PAGE_SIZE = 128

GLA_HEADS = 4
GLA_DK = D_MODEL // 2 // GLA_HEADS
GLA_DV = D_MODEL // GLA_HEADS
GLA_QK_W = GLA_HEADS * GLA_DK
GLA_V_W = GLA_HEADS * GLA_DV
GLA_GATE_RANK = 16
GLA_GATE_NORM = 16.0
GLA_CHUNK = 64
ATT_GROUPS = ((128, 1), (512, 4), (2048, 16))
ATT_HEADS_PER_GROUP = 8
ATT_HEAD_DIM = 64
ATT_HEADS = ATT_HEADS_PER_GROUP * len(ATT_GROUPS)
ATT_W = ATT_HEADS * ATT_HEAD_DIM
ATT_OUT_W = ATT_HEADS_PER_GROUP * ATT_HEAD_DIM
ATT_BLOCK = 128
REL_BUCKETS = 32
REL_MAX_DIST = 2048
FFN_HIDDEN = 2816
CONV_W = 3
N_ADA = 6
EPS = 1e-6

SPLIT_SIZES = (GLA_QK_W, GLA_QK_W, GLA_V_W, GLA_V_W, GLA_GATE_RANK, ATT_W, ATT_W, ATT_W, D_MODEL, D_MODEL)
SPLIT_IDX = [int(s) for s in np.cumsum(SPLIT_SIZES)[:-1]]

kernel_name = 'hybrid_gla_dilated_adaln_step'

def _rmsnorm(x, g):
    xf = x.astype(jnp.float32)
    y = xf * lax.rsqrt(jnp.mean(xf * xf, axis=-1, keepdims=True) + EPS)
    return (y * g.astype(jnp.float32)).astype(x.dtype)

def _modulate(h, shift, scale):
    return h * (1 + scale[:, None]) + shift[:, None]

def _t5_bucket(dist):
    max_exact = REL_BUCKETS // 2
    d = np.maximum(dist, 1).astype(np.float32)
    large = max_exact + (np.log(d / max_exact) / np.log(REL_MAX_DIST / max_exact) * (REL_BUCKETS - max_exact)).astype(np.int32)
    large = np.minimum(large, REL_BUCKETS - 1)
    return np.where(dist < max_exact, dist, large).astype(np.int32)

def _gla(q, k, v, logg, s0):
    B, T, H, _ = q.shape
    C = min(GLA_CHUNK, T)
    n = -(-T // C)
    pad = n * C - T

    def blocks(t):
        t = jnp.pad(t, ((0, 0), (0, pad), (0, 0), (0, 0)))
        return jnp.moveaxis(t.reshape(B, n, C, H, t.shape[-1]), 1, 0)

    mask = jnp.tril(jnp.ones((C, C), dtype=bool))

    def step(S, inp):
        qc, kc, vc, gc = inp
        b = jnp.cumsum(gc, axis=1)
        ref = b[:, C // 2:C // 2 + 1]
        a = jnp.einsum('bihd,bjhd->bhij', qc * jnp.exp(b - ref), kc * jnp.exp(ref - b))
        a = jnp.where(mask, a, 0.0)
        o = jnp.einsum('bhij,bjhv->bihv', a, vc) + jnp.einsum('bihd,bhdv->bihv', qc * jnp.exp(b), S)
        blast = b[:, -1]
        kd = kc * jnp.exp(blast[:, None] - b)
        S = S * jnp.exp(blast)[..., None] + jnp.einsum('bjhd,bjhv->bhdv', kd, vc)
        return S, o

    S, o = lax.scan(step, s0, (blocks(q), blocks(k), blocks(v), blocks(logg)))
    o = jnp.moveaxis(o, 0, 1).reshape(B, n * C, H, v.shape[-1])[:, :T]
    return o, S

def _softmax_lse(s, axis=-1):
    m = jnp.max(s, axis=axis, keepdims=True)
    p = jnp.exp(s - m)
    den = jnp.sum(p, axis=axis, keepdims=True)
    return p / den, (m + jnp.log(den))

def _dilated_prompt(q, k, v, rel_bias_g, window, dil):
    B, T, H, E = q.shape
    span = window // dil
    L = T // dil
    nb = -(-L // ATT_BLOCK)
    Lp = nb * ATT_BLOCK

    def to_blocks(t):
        t = t.reshape(B, L, dil, H, E).transpose(0, 2, 1, 3, 4)
        t = jnp.pad(t, ((0, 0), (0, 0), (0, Lp - L), (0, 0), (0, 0)))
        return t.reshape(B, dil, nb, ATT_BLOCK, H, E)

    def with_prev(t):
        prev = jnp.pad(t, ((0, 0), (0, 0), (1, 0), (0, 0), (0, 0), (0, 0)))[:, :, :-1]
        return jnp.concatenate([prev, t], axis=3)

    qb = to_blocks(q)
    kk = with_prev(to_blocks(k))
    vv = with_prev(to_blocks(v))
    i = np.arange(ATT_BLOCK)[:, None]
    j = np.arange(2 * ATT_BLOCK)[None, :]
    off = ATT_BLOCK + i - j
    valid = (off >= 0) & (off <= span)
    bucket = _t5_bucket(np.clip(off, 0, span) * dil)
    bias = jnp.transpose(rel_bias_g[bucket], (2, 0, 1))
    first_blk = (np.arange(nb)[:, None, None] == 0) & (j[None] < ATT_BLOCK)
    mask = valid[None] & ~first_blk
    s = jnp.einsum('brnihe,brnjhe->brnhij', qb, kk) * (E ** -0.5) + bias[None, None, None]
    s = jnp.where(mask[None, None, :, None], s, -jnp.inf)
    p, lse = _softmax_lse(s)
    o = jnp.einsum('brnhij,brnjhe->brnihe', p, vv)
    o = o.reshape(B, dil, Lp, H, E)[:, :, :L].transpose(0, 2, 1, 3, 4).reshape(B, T, H, E)
    lse = lse[..., 0].transpose(0, 1, 2, 4, 3).reshape(B, dil, Lp, H)[:, :, :L]
    lse = lse.transpose(0, 2, 1, 3).reshape(B, T, H)
    return o, lse

def _dilated_sample(q, k, v, buf, rel_bias_g, window, dil):
    B, Tn, H, E = q.shape
    Lb = buf.shape[1]
    span = window // dil
    kall = jnp.concatenate([buf[:, :, 0].astype(jnp.float32), k], axis=1)
    vall = jnp.concatenate([buf[:, :, 1].astype(jnp.float32), v], axis=1)
    mstep = np.arange(span + 1)
    idx = Lb + np.arange(Tn)[:, None] - mstep[None, :] * dil
    valid = idx >= 0
    idx = np.maximum(idx, 0)
    kg = kall[:, idx]
    vg = vall[:, idx]
    bias = jnp.transpose(rel_bias_g[_t5_bucket(mstep * dil)], (1, 0))
    s = jnp.einsum('bthe,btshe->bths', q, kg) * (E ** -0.5) + bias[None, None]
    s = jnp.where(valid[None, :, None, :], s, -jnp.inf)
    p, lse = _softmax_lse(s)
    o = jnp.einsum('bths,btshe->bthe', p, vg)
    new_buf = jnp.stack([kall, vall], axis=2)[:, kall.shape[1] - Lb:].astype(buf.dtype)
    return o, lse[..., 0], new_buf

def _conv_ffn(h, conv_state, w_up, conv_w, conv_b, w_down):
    T = h.shape[1]
    a, b = jnp.split(h @ w_up, 2, axis=-1)
    a_ext = jnp.concatenate([conv_state.astype(a.dtype), a], axis=1)
    a_conv = conv_b + sum(conv_w[j] * a_ext[:, j:j + T] for j in range(CONV_W))
    y = (jax.nn.silu(a_conv) * b) @ w_down
    return y, a_ext[:, T:]

def _layer(x, c, gla_state, win_bufs, conv_state, rel_bias,
           w_ada, b_ada, norm1_g, w_in, gla_wg2, gla_bg, gla_norm_g,
           w_branch_a, w_branch_b, w_out, norm2_g, w_up, conv_w, conv_b, w_down):
    B, T, _ = x.shape
    f32 = jnp.float32
    shift1, scale1, gate1, shift2, scale2, gate2 = jnp.split(jax.nn.silu(c) @ w_ada + b_ada, N_ADA, axis=-1)
    h = _modulate(_rmsnorm(x, norm1_g), shift1, scale1)
    gq, gk, gv, gr, glr, aq, ak, av, ga, gb = jnp.split(h @ w_in, SPLIT_IDX, axis=-1)

    q = gq.reshape(B, T, GLA_HEADS, GLA_DK).astype(f32) * (GLA_DK ** -0.5)
    k = gk.reshape(B, T, GLA_HEADS, GLA_DK).astype(f32)
    v = gv.reshape(B, T, GLA_HEADS, GLA_DV).astype(f32)
    logg = jax.nn.log_sigmoid((glr @ gla_wg2 + gla_bg).astype(f32)).reshape(B, T, GLA_HEADS, GLA_DK) / GLA_GATE_NORM
    s0 = jnp.zeros((B, GLA_HEADS, GLA_DK, GLA_DV), f32) if gla_state is None else gla_state.astype(f32)
    o_gla, s_gla = _gla(q, k, v, logg, s0)
    o_gla = _rmsnorm(o_gla, gla_norm_g) * jax.nn.silu(gr.astype(f32)).reshape(B, T, GLA_HEADS, GLA_DV)
    y_a = o_gla.reshape(B, T, GLA_V_W).astype(x.dtype) @ w_branch_a

    aq = aq.reshape(B, T, ATT_HEADS, ATT_HEAD_DIM).astype(f32)
    ak = ak.reshape(B, T, ATT_HEADS, ATT_HEAD_DIM).astype(f32)
    av = av.reshape(B, T, ATT_HEADS, ATT_HEAD_DIM).astype(f32)
    outs, lses, new_bufs = [], [], []
    for g, (window, dil) in enumerate(ATT_GROUPS):
        hs = slice(g * ATT_HEADS_PER_GROUP, (g + 1) * ATT_HEADS_PER_GROUP)
        bias_g = rel_bias[:, hs].astype(f32)
        if win_bufs is None:
            o, lse = _dilated_prompt(aq[:, :, hs], ak[:, :, hs], av[:, :, hs], bias_g, window, dil)
            nbuf = jnp.stack([ak[:, :, hs], av[:, :, hs]], axis=2)[:, T - min(window, T):].astype(x.dtype)
        else:
            o, lse, nbuf = _dilated_sample(aq[:, :, hs], ak[:, :, hs], av[:, :, hs], win_bufs[g], bias_g, window, dil)
        outs.append(o)
        lses.append(lse)
        new_bufs.append(nbuf)
    w_grp = jax.nn.softmax(jnp.stack(lses), axis=0)
    o_att = jnp.sum(w_grp[..., None] * jnp.stack(outs), axis=0)
    y_b = o_att.reshape(B, T, ATT_OUT_W).astype(x.dtype) @ w_branch_b

    mix = (jax.nn.sigmoid(ga) * y_a + jax.nn.sigmoid(gb) * y_b) @ w_out
    x = x + gate1[:, None] * mix

    h2 = _modulate(_rmsnorm(x, norm2_g), shift2, scale2)
    if conv_state is None:
        conv_state = jnp.zeros((B, CONV_W - 1, FFN_HIDDEN), x.dtype)
    y_f, new_conv = _conv_ffn(h2, conv_state, w_up, conv_w, conv_b, w_down)
    x = x + gate2[:, None] * y_f
    return x, s_gla, new_bufs[0], new_bufs[1], new_bufs[2], new_conv

def setup_inputs(seed: int = 0) -> dict:
    key = jax.random.key(seed)
    ks = iter(jax.random.split(key, 32))

    def nrm(shape, scale):
        return jax.random.normal(next(ks), shape, jnp.float32) * scale

    in_w = int(sum(SPLIT_SIZES))
    wl = [min(w, PAST_LEN) for w, _ in ATT_GROUPS]
    return {
        'x_prompt': nrm((BATCH, SEQ, D_MODEL), 1.0),
        'x_sample': nrm((DEC_BATCH, DEC_SEQ, D_MODEL), 1.0),
        'state_gla': nrm((DEPTH, DEC_BATCH, GLA_HEADS, GLA_DK, GLA_DV), 0.5),
        'cache_win1': nrm((DEPTH, DEC_BATCH, wl[0], 2, ATT_HEADS_PER_GROUP, ATT_HEAD_DIM), 1.0),
        'cache_win2': nrm((DEPTH, DEC_BATCH, wl[1], 2, ATT_HEADS_PER_GROUP, ATT_HEAD_DIM), 1.0),
        'cache_win3': nrm((DEPTH, DEC_BATCH, wl[2], 2, ATT_HEADS_PER_GROUP, ATT_HEAD_DIM), 1.0),
        'state_conv': nrm((DEPTH, DEC_BATCH, CONV_W - 1, FFN_HIDDEN), 1.0),
        'c_prompt': nrm((BATCH, D_MODEL), 1.0),
        'c_sample': nrm((DEC_BATCH, D_MODEL), 1.0),
        'w_ada': nrm((DEPTH, D_MODEL, N_ADA * D_MODEL), 0.5 * D_MODEL ** -0.5),
        'b_ada': nrm((DEPTH, N_ADA * D_MODEL), 0.02),
        'norm1_g': 1.0 + nrm((DEPTH, D_MODEL), 0.02),
        'w_in': nrm((DEPTH, D_MODEL, in_w), D_MODEL ** -0.5),
        'gla_wg2': nrm((DEPTH, GLA_GATE_RANK, GLA_QK_W), GLA_GATE_RANK ** -0.5),
        'gla_bg': nrm((DEPTH, GLA_QK_W), 0.1),
        'gla_norm_g': 1.0 + nrm((DEPTH, GLA_DV), 0.02),
        'w_branch_a': nrm((DEPTH, GLA_V_W, D_MODEL), GLA_V_W ** -0.5),
        'w_branch_b': nrm((DEPTH, ATT_OUT_W, D_MODEL), ATT_OUT_W ** -0.5),
        'w_out': nrm((DEPTH, D_MODEL, D_MODEL), D_MODEL ** -0.5),
        'rel_bias': nrm((REL_BUCKETS, ATT_HEADS), 0.5),
        'norm2_g': 1.0 + nrm((DEPTH, D_MODEL), 0.02),
        'w_up': nrm((DEPTH, D_MODEL, 2 * FFN_HIDDEN), D_MODEL ** -0.5),
        'conv_w': nrm((DEPTH, CONV_W, FFN_HIDDEN), CONV_W ** -0.5),
        'conv_b': nrm((DEPTH, FFN_HIDDEN), 0.02),
        'w_down': nrm((DEPTH, FFN_HIDDEN, D_MODEL), FFN_HIDDEN ** -0.5),
        'normf_g': 1.0 + nrm((D_MODEL,), 0.02),
    }

def reference(x_prompt, x_sample, state_gla, cache_win1, cache_win2, cache_win3, state_conv,
              c_prompt, c_sample, w_ada, b_ada, norm1_g, w_in, gla_wg2, gla_bg, gla_norm_g,
              w_branch_a, w_branch_b, w_out, rel_bias, norm2_g, w_up, conv_w, conv_b, w_down, normf_g):
    xp, xs = x_prompt, x_sample
    sp = [[] for _ in range(5)]
    ss = [[] for _ in range(5)]
    for l in range(DEPTH):
        lw = (w_ada[l], b_ada[l], norm1_g[l], w_in[l], gla_wg2[l], gla_bg[l], gla_norm_g[l],
              w_branch_a[l], w_branch_b[l], w_out[l], norm2_g[l], w_up[l], conv_w[l], conv_b[l], w_down[l])
        xp, *new_p = _layer(xp, c_prompt, None, None, None, rel_bias, *lw)
        xs, *new_s = _layer(xs, c_sample, state_gla[l], (cache_win1[l], cache_win2[l], cache_win3[l]),
                            state_conv[l], rel_bias, *lw)
        for i in range(5):
            sp[i].append(new_p[i])
            ss[i].append(new_s[i])
    y_prompt = _rmsnorm(xp, normf_g)
    y_sample = _rmsnorm(xs, normf_g)
    gla_p, w1_p, w2_p, w3_p, conv_p = [jnp.stack(t) for t in sp]
    gla_s, w1_s, w2_s, w3_s, conv_s = [jnp.stack(t) for t in ss]
    return (y_prompt, y_sample, gla_p, gla_s, w1_p, w1_s, w2_p, w2_s, w3_p, w3_s, conv_p, conv_s)


_drawn_inputs = setup_inputs


def setup_inputs(seed=0):
    import zlib

    import numpy as np

    out = dict(_drawn_inputs(seed))
    spreads = {}
    factors = {'gla_norm_g': 8.0, 'rel_bias': 4.499, 'norm2_g': 2.986, 'conv_b': 8.0, 'normf_g': 2.799}
    for name, (base, spread) in spreads.items():
        noise = np.random.default_rng([zlib.crc32(name.encode()), seed]).standard_normal(out[name].shape)
        drawn = base * np.exp(spread * noise) if base else spread * noise
        out[name] = jnp.asarray(drawn.astype(out[name].dtype))
    for name, factor in factors.items():
        out[name] = (out[name] * factor).astype(out[name].dtype)
    return out
```

```python
import concourse.bass as bass
from concourse import mybir
from contextlib import ExitStack
import numpy as np

F32 = mybir.dt.float32
R32 = mybir.dt.float32r
ACT = mybir.ActivationFunctionType
ALU = mybir.AluOpType
AX = mybir.AxisListType

P = 128
D = 1024
KD = D // P
TP = 512
NS = 8
T = TP + NS
HT = T // 2
NC = 1 + NS
GH, GDK, GDV = 4, 128, 256
GR = 16
CH = 64
NCH = TP // CH
AH, AE = 8, 64
NG = 3
AG = AH * AE
FH = 2816
KF = FH // P
EPS = 1e-6
UW = 16 * P
NEG = -1e30
BND = AE + 2
BW = 384
SK = P + 1
WIN = (128, 512, 1024)
DIL = (1, 4, 16)
SCALE = AE ** -0.5

C_GQ, C_GK, C_GV, C_GR, C_LR = 0, 512, 1024, 2048, 3072
C_AQ = C_LR + GR
C_AK = C_AQ + NG * AG
C_AV = C_AK + NG * AG
C_GA = C_AV + NG * AG
C_GB = C_GA + D

V_N1, V_N2, V_NF, V_GN, V_BA = 0, KD, 2 * KD, 3 * KD, 3 * KD + 2
NV1 = V_BA + 6 * KD
V_CB, V_CW = NV1, NV1 + KF
NV2 = 4 * KF


def up_sources(w, col):
    v = w["w_up"].rearrange("(k p) n -> p k n", p=P)
    return [(i * KD, v[:, :, bass.ds(FH * i + col, P)]) for i in range(2)]


def down_sources(w, half, col):
    v = w["w_down"].rearrange("(k p) n -> p k n", p=P)
    k0, k1, k2 = (half * (KF // 2) + k for k in (0, 6, KF // 2))
    return [(0, v[:, k0:k1, bass.ds(col, P)]), (6, v[:, k1:k2, bass.ds(col, P)])]


def stream(w):
    out = []

    def cols(kind, src, c0, m, kt=KD, k0=0):
        v = src[k0 * P:(k0 + kt) * P, c0:c0 + m * P].rearrange("(k p) n -> p k n", p=P)
        out.append(dict(kind=kind, src=[(0, v)], kt=kt, mt=m, block=lambda k, j: k * m + j))

    def ada(u):
        cols("ada", w["w_ada"], 256 * u, 2)

    for u in range(8):
        ada(u)
    for kind, c, n in (("gk", C_GK, 2), ("gq", C_GQ, 2), ("gv", C_GV, 4)):
        for u in range(n):
            cols(kind, w["w_in"], c + 256 * u, 2)
    cols("lr", w["w_in"], C_LR, 1)
    n_ada = 8
    for g in range(NG):
        for kind, c in (("aq", C_AQ), ("ak", C_AK), ("av", C_AV)):
            for u in range(2):
                cols(f"{kind}{g}", w["w_in"], c + AG * g + 256 * u, 2)
                if n_ada < 24:
                    ada(n_ada)
                    n_ada += 1
    for u in range(2):
        cols("bb", w["w_branch_b"], 512 * u, 4, kt=4)
    for kind, src, c in (("gr", "w_in", C_GR), ("ba", "w_branch_a", 0), ("ga", "w_in", C_GA),
                         ("gb", "w_in", C_GB), ("wo", "w_out", 0)):
        for u in range(4):
            cols(kind, w[src], c + 256 * u, 2)
    for u in range(KF):
        out.append(dict(kind="up", src=up_sources(w, u * P), kt=KD, mt=2, block=lambda k, j: KD * j + k))
    for m in range(KD):
        for half in range(2):
            out.append(dict(kind="dn", src=down_sources(w, half, m * P), kt=KF // 2, mt=1, half=half,
                            block=lambda k, j: k))
    n = {"mm": 0, "ada": 0}
    tile = done = 0
    arrived = [0, 0]
    for u, x in enumerate(out):
        sort = "ada" if x["kind"] == "ada" else "mm"
        x["i"] = n[sort]
        n[sort] += 1
        arrived[u % 2] += 16 * len(x["src"])
        x["arrived"] = arrived[u % 2]
        x["words"] = x["kt"] * x["mt"] * P
        x["tile0"], x["pass0"] = tile, done
        if sort == "mm":
            done += x["mt"]
            tile += 0 if x.get("half") == 0 else x["mt"]
    return out


def program(nc, w, o, con):
    U = stream(w)
    MM = [u for u, x in enumerate(U) if x["kind"] != "ada"]
    ADA = [u for u, x in enumerate(U) if x["kind"] == "ada"]
    LAST = {"gr": "dve", "wo": "dve", "up": "dve", "dn": "dve"}
    owner, freed, passes = [], [], []
    count = {"act": 0, "dve": 0}
    for u in MM:
        x = U[u]
        if x.get("half") == 0:
            continue
        for m in range(x["mt"]):
            who = LAST.get(x["kind"], "act") if not (x["kind"] == "up" and m == 0) else "act"
            count[who] += 1
            owner.append(who)
            freed.append(count[who])
            passes.append(x["pass0"] + m + 1)

    def units(kind):
        return [u for u, x in enumerate(U) if x["kind"] == kind]

    ctx = ExitStack()
    with ctx:
        def sb(name, shape, dt=F32):
            return ctx.enter_context(nc.sbuf_tensor(name, shape, dt))

        def sem(name):
            return ctx.enter_context(nc.semaphore(name))

        actH = sb("actH", [P, KD, T], R32)
        actL = sb("actL", [P, KD, T], R32)
        wraw = sb("wraw", [P, 2, UW])
        whi = sb("whi", [P, 2, UW], R32)
        wlo = sb("wlo", [P, 2, UW], R32)
        cst = sb("cst", [P, 5 * P])
        mod = sb("mod", [P, 6 * KD, NC])
        vec = sb("vec", [P, NV1 + NV2])
        stT = sb("stT", [P, KF, NS * 2])
        modA = sb("modA", [P, KD, NC])
        scT = sb("scT", [P, NC * KD])
        ident, tri, gmask, flip, ones = (cst[:, P * i:P * i + P] for i in range(5))
        AW = 30208
        FX = 2 * KF * T
        FT = FX + KD * T
        with ExitStack() as e:
            e.enter_context(nc.sbuf_tensor("below_a2", [P, KD * T], F32))
            a2H = e.enter_context(nc.sbuf_tensor("a2H", [P, KD, T], R32))
            a2L = e.enter_context(nc.sbuf_tensor("a2L", [P, KD, T], R32))
        with ExitStack() as e:
            gH = e.enter_context(nc.sbuf_tensor("gH", [P, KF, T], R32))
            gL = e.enter_context(nc.sbuf_tensor("gL", [P, KF, T], R32))
        arena = sb("arena", [P, AW])
        ps = ctx.enter_context(nc.psum_tensor("ps", [P, 8, 512], F32))

        def at(off, *shape, parts=P):
            n = int(np.prod(shape))
            assert off + n <= AW, (off, shape)
            v = arena[0:parts, off:off + n]
            if len(shape) == 2:
                v = v.rearrange("p (a b) -> p a b", b=shape[1])
            return v

        def norm_temps(off):
            return dict(sq=at(off, 2, T), v=at(off + 2 * T, T), y=at(off + 3 * T, T), t=at(off + 4 * T, T),
                        r=at(off + 5 * T, T), hf=at(off + 6 * T, 2, T))

        def dram(name, *shape):
            return nc.dram_tensor(name, shape, F32, kind="Internal").ap()

        xd = dram("x_feature_major", P, KD * T)
        od = dram("gla_out", P, KD * T)
        bd = dram("bias_by_distance", NG * AH, BW)
        gd = [dram(f"group_out{g}", TP, AH * BND) for g in range(NG)]

        w_dma = [sem("w_dma0"), sem("w_dma1")]
        hi_ready, lo_ready, pass_done = sem("hi_ready"), sem("lo_ready"), sem("pass_done")
        ada_done, ada_read = sem("ada_done"), sem("ada_read")
        tile_read = {"act": sem("tile_read_act"), "dve": sem("tile_read_dve")}
        outs, outs_pool = sem("outs"), sem("outs_pool")
        n_outs, n_outs_pool = [0], [0]
        S = {}

        def s(name):
            if name not in S:
                S[name] = sem(name)
            return S[name]

        class Chain:

            def __init__(self, name):
                self.sem, self.n = sem(name), 0

            def link(self, eng, ins):
                self.n += 1
                ins.then_inc(self.sem, 1)
                eng.wait_ge(self.sem, self.n)

        dch, ach, pch = Chain("dve_chain"), Chain("act_chain"), Chain("pool_chain")

        def issue(sp, u):
            if u >= len(U):
                return
            x = U[u]
            if u >= 2:
                y = U[u - 2]
                sp.wait_ge(ada_done if y["kind"] == "ada" else lo_ready, y["i"] + 1)
            load(sp, u % 2, x["src"])

        def load(sp, slot, sources):
            for block, src in sources:
                k, n = src.shape[1], src.shape[2]
                dst = wraw[:, slot, P * block:P * block + k * n].rearrange("p (k n) -> p k n", k=k)
                sp.dma_start(dst, src).then_inc(w_dma[slot], 16)

        def split_hi(act, v):
            if v >= len(MM):
                return
            u = MM[v]
            act.wait_ge(w_dma[u % 2], U[u]["arrived"])
            if v >= 2:
                y = U[MM[v - 2]]
                act.wait_ge(pass_done, y["pass0"] + y["mt"])
            n = U[u]["words"]
            act.activation(whi[:, v % 2, 0:n], wraw[:, u % 2, 0:n], ACT.Copy).then_inc(hi_ready, 1)

        def split_lo(dve, v):
            if v >= len(MM):
                return
            u = MM[v]
            n = U[u]["words"]
            dve.wait_ge(hi_ready, v + 1)
            dve.tensor_tensor(wlo[:, v % 2, 0:n], wraw[:, u % 2, 0:n], whi[:, v % 2, 0:n].bitcast(F32),
                              ALU.subtract).then_inc(lo_ready, 1)

        def banks(n):
            return ps[:, 2 * (n % 2):2 * (n % 2) + 2, 0:HT]

        def halves(v):
            return v.rearrange("p (a b) -> p a b", a=2)

        def three_pass(pe, n, slot, blocks, H, L, k0=0, begin=True, end=True):
            last = None
            for j, b in enumerate(blocks):
                hi, lo = whi[:, slot, b * P:b * P + P], wlo[:, slot, b * P:b * P + P]
                for a, wt, X in ((0, hi, H), (1, hi, H), (0, hi, L), (1, hi, L), (0, lo, H), (1, lo, H)):
                    last = pe.matmul(ps[:, 2 * (n % 2) + a, 0:HT], wt, X[:, k0 + j, a * HT:a * HT + HT],
                                     start=begin and j == 0 and wt is hi and X is H,
                                     stop=end and j == len(blocks) - 1 and wt is lo)
            return last

        def multiply(pe, u, H, L):
            x = U[u]
            pe.wait_ge(lo_ready, x["i"] + 1)
            for m in range(x["mt"]):
                n = x["tile0"] + m
                if n >= 2:
                    pe.wait_ge(tile_read[owner[n - 2]], freed[n - 2])
                three_pass(pe, n, x["i"] % 2, [x["block"](k, m) for k in range(x["kt"])], H, L)\
                    .then_inc(pass_done, 1)

        def copy_tiles(act, u, dst, m0):
            x = U[u]
            split_hi(act, x["i"] + 1)
            for m in range(x["mt"]):
                n = x["tile0"] + m
                act.wait_ge(pass_done, passes[n])
                act.activation(halves(dst[:, m0 + m, :]), banks(n), ACT.Copy).then_inc(tile_read["act"], 1)

        def wait_copied(eng, u):
            n = U[u]["tile0"] + U[u]["mt"] - 1
            eng.wait_ge(tile_read["act"], freed[n])

        def ada_pe(pe, a):
            u = ADA[a]
            pe.wait_ge(w_dma[u % 2], U[u]["arrived"])
            if a >= 1:
                pe.wait_ge(ada_read, a)
            for m in range(2):
                for k in range(KD):
                    last = pe.matmul(ps[:, 7, 480 + NC * m:480 + NC * m + NC],
                                     wraw[:, u % 2, (2 * k + m) * P:(2 * k + m) * P + P],
                                     scT[:, k:NC * KD:KD], start=k == 0, stop=k == KD - 1)
            last.then_inc(ada_done, 1)

        def ada_dve(dve, a):
            dve.wait_ge(ada_done, a + 1)
            dve.tensor_tensor(mod[:, 2 * a:2 * a + 2, :],
                              ps[:, 7, 480:480 + 2 * NC].rearrange("p (m c) -> p m c", m=2),
                              vec[:, V_BA + 2 * a:V_BA + 2 * a + 2].unsqueeze(2).to_broadcast([P, 2, NC]),
                              ALU.add).then_inc(ada_read, 1)

        def norm_pe(pe, i, tmp):
            for k in range(KD):
                pe.wait_ge(s("sq_ready"), KD * i + k + 1)
                for a in range(2):
                    last = pe.matmul(ps[:, 4 + a, 0:HT], ones, tmp["sq"][:, k % 2, a * HT:a * HT + HT],
                                     start=k == 0, stop=k == KD - 1)
                last.then_inc(s("sq_summed"), 1)

        def newton(dve, v, y, t, r):
            dch.link(dve, dve.tensor_tensor(t, y, y, ALU.mult))
            dch.link(dve, dve.scalar_tensor_tensor(t, t, -0.5, v, ALU.mult, ALU.mult))
            return dve.scalar_tensor_tensor(r, t, 1.5, y, ALU.add, ALU.mult)

        def norm_sum_dve(dve, i, X, tmp):
            for k in range(KD):
                if k >= 2:
                    dve.wait_ge(s("sq_summed"), KD * i + k - 1)
                dve.tensor_tensor(tmp["sq"][:, k % 2, :], X[:, k, :], X[:, k, :], ALU.mult).then_inc(s("sq_ready"), 1)
            dve.wait_ge(s("sq_summed"), KD * i + KD)
            dve.tensor_scalar(halves(tmp["v"]), ps[:, 4:6, 0:HT], 1.0 / D, EPS, ALU.mult, ALU.add)\
               .then_inc(s("ms_ready"), 1)
            dve.wait_ge(s("rs_ready"), i + 1)
            dch.link(dve, newton(dve, tmp["v"], tmp["y"], tmp["t"], tmp["r"]))

        def norm_act(act, i, tmp):
            act.wait_ge(s("ms_ready"), i + 1)
            ach.link(act, act.activation(tmp["y"], tmp["v"], ACT.Ln))
            act.activation(tmp["y"], tmp["y"], ACT.Exp, scale=-0.5).then_inc(s("rs_ready"), 1)

        def modulate_dve(dve, i, X, tmp, gcol, shift, scale):
            g = vec[:, gcol:gcol + KD].unsqueeze(2).to_broadcast([P, KD, NC])
            dch.link(dve, dve.scalar_tensor_tensor(modA[:, :, :], mod[:, scale:scale + KD, :], 1.0, g, ALU.add, ALU.mult))

            def low(k):
                dve.wait_ge(s("h_hi"), KD * i + k + 1)
                dve.tensor_tensor(actL[:, k, :], tmp["hf"][:, k % 2, :], actH[:, k, :].bitcast(F32), ALU.subtract)\
                   .then_inc(s("h_split"), 1)

            for k in range(KD):
                h = tmp["hf"][:, k % 2, :]
                if k >= 2:
                    dve.wait_ge(s("h_split"), KD * i + k - 1)
                dch.link(dve, dve.tensor_tensor(h, X[:, k, :], tmp["r"], ALU.mult))
                dve.tensor_scalar(h[:, 0:TP], h[:, 0:TP], modA[:, k, 0:1], mod[:, shift + k, 0:1], ALU.mult, ALU.add)
                dch.link(dve, dve.tensor_tensor(h[:, TP:T], h[:, TP:T], modA[:, k, 1:NC], ALU.mult))
                dve.tensor_tensor(h[:, TP:T], h[:, TP:T], mod[:, shift + k, 1:NC], ALU.add).then_inc(s("h_ready"), 1)
                if k >= 1:
                    low(k - 1)
            low(KD - 1)

        def modulate_act(act, i, tmp):
            for k in range(KD):
                act.wait_ge(s("h_ready"), KD * i + k + 1)
                act.activation(actH[:, k, :], tmp["hf"][:, k % 2, :], ACT.Copy).then_inc(s("h_hi"), 1)

        xT1 = at(0, KD, T)
        xin = at(4160, 4, D)
        n1 = norm_temps(8256)
        csrow = at(12416, FH, parts=2 * NS)
        crow = at(15232, P, parts=NC * KD)
        v1row = at(15360, P, parts=NV1)
        v2row = at(15488, P, parts=NV2)
        xsin = at(15616, D, parts=NS)
        sig1 = at(16640, NC * KD)

        with nc.Block() as block:
            @block.sync
            def _(sp):
                sp.dma_start(cst[:, 0:4 * P], con["cst"]).then_inc(s("early_in"), 16)
                sp.dma_start(crow[0:KD, :], w["c_prompt"].rearrange("b (k p) -> (b k) p", p=P)).then_inc(s("early_in"), 16)
                sp.dma_start(crow[KD:NC * KD, :], w["c_sample"].rearrange("b (k p) -> (b k) p", p=P)).then_inc(s("early_in"), 16)
                for name, r0, n in (("norm1_g", V_N1, KD), ("norm2_g", V_N2, KD), ("normf_g", V_NF, KD),
                                    ("gla_norm_g", V_GN, 2), ("b_ada", V_BA, 6 * KD)):
                    sp.dma_start(v1row[r0:r0 + n, :], w[name].rearrange("(k p) -> k p", p=P)).then_inc(s("early_in"), 16)
                issue(sp, 0)
                issue(sp, 1)
                for t in range(4):
                    sp.dma_start(xin[:, t, :], w["x_prompt"][P * t:P * t + P, :]).then_inc(s("x_in"), 16)
                sp.dma_start(xsin, w["x_sample"]).then_inc(s("x_in"), 16)
                sp.dma_start(v2row[0:KF, :], w["conv_b"].rearrange("(k p) -> k p", p=P)).then_inc(s("late_in"), 16)
                sp.dma_start(v2row[KF:NV2, :], w["conv_w"].rearrange("j (k p) -> (j k) p", p=P)).then_inc(s("late_in"), 16)
                sp.dma_start(csrow, w["state_conv"].rearrange("b j n -> (b j) n")).then_inc(s("late_in"), 16)
                for u in range(2, 8 + 2):
                    issue(sp, u)
                sp.wait_ge(s("x_all"), 1)
                sp.dma_start(xd, xT1.rearrange("p k t -> p (k t)")).then_inc(s("x_spilled"), 16)
                sp.wait_ge(s("x_spilled"), 16)

            @block.gpsimd
            def _(pool):
                for g in range(NG):
                    for b in range(NS):
                        n = (WIN[g] - 1) * D // P
                        src = w[f"cache_win{g + 1}"][b].rearrange("t n -> (t n)")[D:WIN[g] * D]
                        dst = o[f"win{g + 1}_s"][b].rearrange("t n -> (t n)")[0:(WIN[g] - 1) * D]
                        pool.dma_start(dst.rearrange("(p n) -> p n", n=n), src.rearrange("(p n) -> p n", n=n))\
                            .then_inc(outs_pool, 16)
                        n_outs_pool[0] += 16
                pool.dma_start(o["conv_s"][:, 0, :], w["state_conv"][:, 1, :]).then_inc(outs_pool, 16)
                n_outs_pool[0] += 16
                pool.memset(ones, 1.0).then_inc(s("ones_ready"), 1)

            @block.scalar
            def _(act):
                act.wait_ge(s("prep_T"), 1)
                act.activation(sig1, ps[:, 4, 0:NC * KD], ACT.Sigmoid).then_inc(s("c_sig"), 1)
                for k in range(KD):
                    act.wait_ge(s("x_T"), k + 1)
                    act.activation(xT1[:, k, 0:TP], ps[:, k % 4, :], ACT.Copy).then_inc(s("x_evac"), 1)
                act.wait_ge(s("prep_T"), 3)
                act.activation(xT1[:, :, TP:T], ps[:, 5, 0:NS * KD].rearrange("p (k b) -> p k b", b=NS), ACT.Copy)\
                   .then_inc(s("x_all"), 1)
                norm_act(act, 0, n1)
                modulate_act(act, 0, n1)
                split_hi(act, 0)

            @block.vector
            def _(dve):
                dve.wait_ge(s("c_sig"), 1)
                dve.tensor_tensor(scT[:, :], ps[:, 4, 0:NC * KD], sig1, ALU.mult).then_inc(s("c_silu"), 1)
                dve.wait_ge(s("prep_T"), 2)
                dve.tensor_copy(vec[:, 0:NV1], ps[:, 6, 0:NV1]).then_inc(s("vec_ready"), 1)
                dve.wait_ge(s("prep_T"), 4)
                dve.tensor_copy(vec[:, NV1:NV1 + NV2], ps[:, 6, NV1:NV1 + NV2])
                dve.wait_ge(s("prep_T"), 5)
                dve.tensor_copy(stT[:, :, :], ps[:, 7, 0:KF * 16].rearrange("p (k b) -> p k b", b=16))\
                   .then_inc(s("vec_ready"), 1)
                dve.wait_ge(s("x_all"), 1)
                dve.wait_ge(s("vec_ready"), 2)
                norm_sum_dve(dve, 0, xT1, n1)
                for a in range(8):
                    ada_dve(dve, a)
                dve.wait_ge(ada_read, 8)
                modulate_dve(dve, 0, xT1, n1, V_N1, 0, KD)
                split_lo(dve, 0)

            @block.tensor
            def _(pe):
                pe.wait_ge(s("early_in"), 128)
                pe.transpose(ps[:, 4, 0:NC * KD], crow, ident[0:NC * KD, 0:NC * KD]).then_inc(s("prep_T"), 1)
                pe.transpose(ps[:, 6, 0:NV1], v1row, ident[0:NV1, 0:NV1]).then_inc(s("prep_T"), 1)
                for k in range(KD):
                    if k >= 4:
                        pe.wait_ge(s("x_evac"), k - 3)
                    for t in range(4):
                        if k == 0 and t == 0:
                            pe.wait_ge(s("x_in"), 80)
                        last = pe.transpose(ps[:, k % 4, P * t:P * t + P], xin[:, t, P * k:P * k + P], ident)
                    last.then_inc(s("x_T"), 1)
                    if k == 0:
                        for j in range(KD):
                            last = pe.transpose(ps[:, 5, NS * j:NS * j + NS], xsin[:, P * j:P * j + P], ident[0:NS, 0:NS])
                        last.then_inc(s("prep_T"), 1)
                pe.wait_ge(s("late_in"), 48)
                pe.wait_ge(s("vec_ready"), 1)
                pe.transpose(ps[:, 6, NV1:NV1 + NV2], v2row, ident[0:NV2, 0:NV2]).then_inc(s("prep_T"), 1)
                for j in range(KF):
                    last = pe.transpose(ps[:, 7, 16 * j:16 * j + 16], csrow[:, P * j:P * j + P], ident[0:16, 0:16])
                last.then_inc(s("prep_T"), 1)
                pe.wait_ge(s("c_silu"), 1)
                pe.wait_ge(s("vec_ready"), 2)
                pe.wait_ge(s("ones_ready"), 1)
                norm_pe(pe, 0, n1)
                for a in range(8):
                    ada_pe(pe, a)

        gk, gq, gv = at(0, 4, T), at(2080, 4, T), at(4160, KD, T)
        vtok = at(10400, 4, D)
        oT2 = at(14496, KD, T)
        gtok = at(18656, 4, 512)
        Bt, X1, X2, X3, X4, X5, kdtok, aTm = (at(20704 + 512 * i, 512) for i in range(8))
        Sall = at(24800, 8, GDV)
        sq2 = at(26848, 2, 512)
        lrT = at(27872, T)
        wg2 = at(28392, 512, parts=GR + 1)
        ebS = at(28904, 4, NS)
        za, zb = Bt, X1
        ktS, vtS = at(28940 - 28940 + 10400, 512, parts=NS), at(10912, D, parts=NS)
        Sring = at(18656, 2, 4 * GDV)
        kmask = at(11936, 2, 512, parts=NS)
        qS, gS, oS = at(20704, 4, NS), at(20736, 4 * NS), at(20768, 8, NS)
        sqS, rsS, rsT, rsV, rsR = at(20832, 8, NS), at(20896, 4 * NS), at(20928, 4 * NS), at(20960, 4 * NS), at(20992, 4 * NS)
        QSC = GDK ** -0.5
        U_K, U_Q, U_V, U_LR = units("gk"), units("gq"), units("gv"), units("lr")
        AQKV = [at(4160, 12, T), at(10400, 12, T)]

        def update_bank(c):
            return ps[:, 4 + 2 * (c % 2) + c // 4, GDV * (c // 2 % 2):GDV * (c // 2 % 2) + GDV]

        def group_units(g):
            return [u for k in ("aq", "ak", "av") for u in units(f"{k}{g}")]

        def logsig_act(act, z, ta, tb, name, i):
            ach.link(act, act.activation(ta, z, ACT.Abs))
            ach.link(act, act.activation(ta, ta, ACT.Exp, scale=-1.0))
            act.activation(tb, ta, ACT.Ln, bias=1.0).then_inc(s(name), 1)

        with nc.Block() as block:
            @block.sync
            def _(sp):
                sp.dma_start(wg2[0:GR, :], w["gla_wg2"]).then_inc(s("wg2_in"), 16)
                sp.dma_start(wg2[GR:GR + 1, :], w["gla_bg"].rearrange("(a n) -> a n", a=1)).then_inc(s("wg2_in"), 16)
                for u in range(10, U_LR[0] + 3):
                    issue(sp, u)
                for h in range(GH):
                    sp.wait_ge(s("gla_state"), 8 * (h + 1))
                    sp.dma_start(o["gla_p"][h], Sall[:, 7, :]).then_inc(s("gla_p_out"), 16)
                    sp.wait_ge(s("gla_p_out"), 16 * (h + 1))
                for b in range(NS):
                    if b == 0:
                        sp.wait_ge(s("o_done"), GH)
                    if b >= 2:
                        sp.wait_ge(s(f"gs_out{b % 2}"), 16 * (b // 2))
                        sp.wait_ge(s("gs_read"), b - 1)
                    sp.dma_start(Sring[:, b % 2, :].rearrange("p (h v) -> p h v", h=GH),
                                 w["state_gla"][b].rearrange("h p v -> p h v")).then_inc(s(f"gs_in{b % 2}"), 16)
                    if b >= 1:
                        sp.wait_ge(s("gs_new"), b)
                        sp.dma_start(o["gla_s"][b - 1].rearrange("h p v -> p h v"),
                                     Sring[:, (b - 1) % 2, :].rearrange("p (h v) -> p h v", h=GH))\
                            .then_inc(s(f"gs_out{(b - 1) % 2}"), 16)
                sp.wait_ge(s("gs_new"), NS)
                sp.dma_start(o["gla_s"][NS - 1].rearrange("h p v -> p h v"),
                             Sring[:, (NS - 1) % 2, :].rearrange("p (h v) -> p h v", h=GH)).then_inc(s("gs_out1"), 16)
                for d in range(2):
                    sp.wait_ge(s(f"gs_out{d}"), 16 * (NS // 2))
                sp.wait_ge(s("o_all"), 1)
                sp.dma_start(od, oT2.rearrange("p k t -> p (k t)")).then_inc(s("o_spilled"), 16)
                sp.wait_ge(s("o_spilled"), 16)
                last_u = group_units(0)[-1]
                for u in range(U_LR[0] + 3, last_u + 4):
                    issue(sp, u)

            @block.scalar
            def _(act):
                for us, dst in ((U_K, gk), (U_Q, gq), (U_V, gv)):
                    for j, u in enumerate(us):
                        copy_tiles(act, u, dst, 2 * j)
                x = U[U_LR[0]]
                split_hi(act, x["i"] + 1)
                act.wait_ge(s("lr_ones"), 1)
                act.wait_ge(pass_done, passes[x["tile0"]])
                act.activation(halves(lrT[0:GR, :]), ps[0:GR, 2 * (x["tile0"] % 2):2 * (x["tile0"] % 2) + 2, 0:HT], ACT.Copy).then_inc(tile_read["act"], 1)
                for t in range(4):
                    act.wait_ge(s("z_ready"), t + 1)
                    if t >= 1:
                        act.wait_ge(s("g_ready"), t)
                    logsig_act(act, ps[:, 4 + t, :], za, zb, "ln_ready", t)
                for t in range(4):
                    act.wait_ge(s("v_T"), t + 1)
                    act.activation(vtok[:, t, :].rearrange("p (a b) -> p a b", a=2),
                                   ps[:, 4 + 2 * (t % 2):6 + 2 * (t % 2), :], ACT.Copy).then_inc(s("v_tok"), 1)
                for h in range(GH):
                    act.wait_ge(s("b_ready"), 2 * h + 1)
                    act.activation(X3, Bt, ACT.Exp)
                    act.wait_ge(s("b_ready"), 2 * h + 2)
                    act.activation(X2, X1, ACT.Exp, scale=-1.0)
                    act.activation(X4, X4, ACT.Exp).then_inc(s("e24"), 1)
                    act.activation(X5, X1, ACT.Exp).then_inc(s("e5"), 1)
                    act.wait_ge(s("kd_T"), h + 1)
                    act.activation(kdtok, ps[:, 6, :], ACT.Copy).then_inc(s("kd_tok"), 1)
                    act.wait_ge(s("o_ready"), h + 1)
                    act.activation(oT2[:, 2 * h:2 * h + 2, 0:TP], ps[:, 4:6, :], ACT.Copy)
                    act.activation(sq2, ps[:, 4:6, :], ACT.Square).then_inc(s("o_sq"), 1)
                    act.wait_ge(s("o_v"), h + 1)
                    ach.link(act, act.activation(Bt, aTm, ACT.Ln))
                    act.activation(Bt, Bt, ACT.Exp, scale=-0.5).then_inc(s("o_rs"), 1)
                act.wait_ge(s("z_ready"), 5)
                logsig_act(act, ps[:, 4, 0:32], gS, rsS, "ln_ready", 0)
                act.wait_ge(s("g_ready"), 5)
                act.activation(ebS.rearrange("p h b -> p (h b)"), gS, ACT.Exp, scale=1.0 / 16).then_inc(s("ebs"), 1)
                act.wait_ge(s("kvs_T"), 1)
                ach.link(act, act.activation(ktS, ps[0:NS, 5, :], ACT.Copy))
                act.activation(vtS.rearrange("p (a b) -> p a b", a=2), ps[0:NS, 6:8, :], ACT.Copy).then_inc(s("kvs"), 1)
                act.wait_ge(s("o_v"), 5)
                ach.link(act, act.activation(rsT, rsV, ACT.Ln))
                act.activation(rsT, rsT, ACT.Exp, scale=-0.5).then_inc(s("o_rs"), 1)
                act.wait_ge(s("o_all"), 1)
                for j, u in enumerate(group_units(0)):
                    copy_tiles(act, u, AQKV[0], 2 * j)

            @block.vector
            def _(dve):
                dve.memset(lrT[0:32, :], 1.0).then_inc(s("lr_ones"), 1)
                for v in range(1, U[U_LR[0]]["i"] + 2):
                    split_lo(dve, v)
                for t in range(4):
                    dve.wait_ge(s("ln_ready"), t + 1)
                    dve.scalar_tensor_tensor(gtok[:, t, :], ps[:, 4 + t, :], 0.0, zb, ALU.min, ALU.subtract)\
                       .then_inc(s("g_ready"), 1)
                for h in range(GH):
                    dve.wait_ge(s("B_ready"), h + 1)
                    if h >= 1:
                        dve.wait_ge(s("o_done"), h)
                    dve.tensor_copy(Bt, ps[:, 4, :]).then_inc(s("b_ready"), 1)
                    dve.wait_ge(s("b_ready"), 2 * h + 1)
                    B3 = Bt.rearrange("p (c i) -> p c i", i=CH)
                    dve.tensor_tensor(X1.rearrange("p (c i) -> p c i", i=CH), B3,
                                      B3[:, :, CH // 2:CH // 2 + 1].to_broadcast([P, NCH, CH]), ALU.subtract)
                    dve.tensor_tensor(X4.rearrange("p (c i) -> p c i", i=CH),
                                      B3[:, :, CH - 1:CH].to_broadcast([P, NCH, CH]), B3, ALU.subtract)\
                       .then_inc(s("b_ready"), 1)
                    dve.wait_ge(s("e24"), h + 1)
                    dve.tensor_tensor(X2, gk[:, h, 0:TP], X2, ALU.mult)
                    dve.tensor_tensor(X4, gk[:, h, 0:TP], X4, ALU.mult).then_inc(s("kd"), 1)
                    dve.wait_ge(s("e5"), h + 1)
                    dve.scalar_tensor_tensor(X1, gq[:, h, 0:TP], QSC, X5, ALU.mult, ALU.mult).then_inc(s("qe"), 1)
                    dve.wait_ge(s("qe"), h + 1)
                    dve.scalar_tensor_tensor(X5, gq[:, h, 0:TP], QSC, X3, ALU.mult, ALU.mult).then_inc(s("qb"), 1)
                    dve.wait_ge(s("A_ready"), h + 1)
                    dve.tensor_tensor(aTm.rearrange("p (t i) -> p t i", i=P), ps[:, 5, :].rearrange("p (t i) -> p t i", i=P),
                                      gmask.unsqueeze(1).to_broadcast([P, 4, P]), ALU.mult).then_inc(s("aT"), 1)
                    dve.wait_ge(s("U_ready"), h + 1)
                    if h >= 1:
                        dve.wait_ge(s("gla_p_out"), 16 * h)
                    for c in range(NCH):
                        add = update_bank(c)
                        if c == 0:
                            ins = dve.tensor_copy(Sall[:, 0, :], add)
                        else:
                            ins = dve.scalar_tensor_tensor(Sall[:, c, :], Sall[:, c - 1, :],
                                                           X3[:, CH * c + CH - 1:CH * c + CH], add, ALU.mult, ALU.add)
                        ins.then_inc(s("gla_state"), 1)
                        dve.wait_ge(s("gla_state"), NCH * h + c + 1)
                    dve.wait_ge(s("o_summed"), h + 1)
                    dve.tensor_scalar(aTm, ps[:, 6, :], 1.0 / GDV, EPS, ALU.mult, ALU.add).then_inc(s("o_v"), 1)
                    dve.wait_ge(s("o_rs"), h + 1)
                    dch.link(dve, newton(dve, aTm, Bt, X2, X4))
                    for vt in range(2):
                        last = dve.scalar_tensor_tensor(oT2[:, 2 * h + vt, 0:TP], oT2[:, 2 * h + vt, 0:TP],
                                                        vec[:, V_GN + vt:V_GN + vt + 1], X4, ALU.mult, ALU.mult)
                    last.then_inc(s("o_done"), 1)
                dve.wait_ge(s("o_done"), GH)
                dve.tensor_scalar(qS, gq[:, :, TP:T], QSC, None, ALU.mult)
                dve.wait_ge(s("ln_ready"), 5)
                dve.scalar_tensor_tensor(gS, ps[:, 4, 0:32], 0.0, rsS, ALU.min, ALU.subtract).then_inc(s("g_ready"), 1)
                dve.wait_ge(s("kvs"), 1)
                dve.wait_ge(s("ebs"), 1)
                for b in range(NS):
                    if b >= 2:
                        dve.wait_ge(s("kv_outer"), b - 1)
                    dve.tensor_scalar(kmask[:, b % 2, :], ktS, ident[0:NS, b:b + 1], None, ALU.mult).then_inc(s("kmask"), 1)
                    dve.wait_ge(s("kv_outer"), b + 1)
                    dve.wait_ge(s(f"gs_in{b % 2}"), 16 * (b // 2 + 1))
                    for h in range(GH):
                        st = Sring[:, b % 2, GDV * h:GDV * h + GDV]
                        last = dve.scalar_tensor_tensor(st, st, ebS[:, h, b:b + 1],
                                                        ps[:, 4 + h // 2, GDV * (h % 2):GDV * (h % 2) + GDV], ALU.mult, ALU.add)
                    last.then_inc(s("gs_new"), 1)
                dve.wait_ge(s("gs_read"), NS)
                dch.link(dve, dve.tensor_copy(oS.rearrange("p a b -> p (a b)"), ps[:, 6, 0:64]))
                dve.tensor_tensor(sqS.rearrange("p a b -> p (a b)"), oS.rearrange("p a b -> p (a b)"),
                                  oS.rearrange("p a b -> p (a b)"), ALU.mult).then_inc(s("o_sq"), 1)
                dve.wait_ge(s("o_summed"), 5)
                dve.tensor_scalar(rsV, ps[:, 7, 0:32], 1.0 / GDV, EPS, ALU.mult, ALU.add).then_inc(s("o_v"), 1)
                dve.wait_ge(s("o_rs"), 5)
                dch.link(dve, newton(dve, rsV, rsT, rsS, rsR))
                for vt in range(2):
                    last = dve.scalar_tensor_tensor(oT2[:, vt:KD:2, TP:T], oS[:, vt:KD:2, :],
                                                    vec[:, V_GN + vt:V_GN + vt + 1],
                                                    rsR.rearrange("p (h b) -> p h b", b=NS), ALU.mult, ALU.mult)
                last.then_inc(s("o_all"), 1)
                for j, u in enumerate(group_units(0)):
                    split_lo(dve, U[u]["i"] + 1)
                    ada_dve(dve, 8 + j)

            @block.tensor
            def _(pe):
                pe.wait_ge(s("h_split"), KD)
                for u in U_K + U_Q + U_V + U_LR:
                    multiply(pe, u, actH, actL)
                pe.wait_ge(s("wg2_in"), 32)
                wait_copied(pe, U_LR[0])
                for t in range(4):
                    pe.matmul(ps[:, 4 + t, :], lrT[0:GR + 1, P * t:P * t + P], wg2, start=True, stop=True)\
                      .then_inc(s("z_ready"), 1)
                for t in range(4):
                    pe.wait_ge(s("g_ready"), 2 * (t % 2) + 2)
                    if t >= 2:
                        pe.wait_ge(s("v_tok"), t - 1)
                    for m in range(KD):
                        last = pe.transpose(ps[:, 4 + 2 * (t % 2) + m // 4, P * (m % 4):P * (m % 4) + P],
                                            gv[:, m, P * t:P * t + P], ident)
                    last.then_inc(s("v_T"), 1)
                pe.wait_ge(s("v_tok"), 4)
                for h in range(GH):
                    if h >= 1:
                        pe.wait_ge(s("o_v"), h)
                        pe.wait_ge(s("o_sq"), h)
                    for t in range(4):
                        last = pe.matmul(ps[:, 4, P * t:P * t + P], gtok[:, t, GDK * h:GDK * h + GDK], tri, start=True, stop=True)
                    last.then_inc(s("B_ready"), 1)
                    pe.wait_ge(s("kd"), h + 1)
                    for t in range(4):
                        last = pe.transpose(ps[:, 6, P * t:P * t + P], X4[:, P * t:P * t + P], ident)
                    last.then_inc(s("kd_T"), 1)
                    pe.wait_ge(s("qe"), h + 1)
                    for t in range(4):
                        last = pe.matmul(ps[:, 5, P * t:P * t + P], X2[:, P * t:P * t + P], X1[:, P * t:P * t + P],
                                         start=True, stop=True)
                    last.then_inc(s("A_ready"), 1)
                    pe.wait_ge(s("kd_tok"), h + 1)
                    pe.wait_ge(s("aT"), h + 1)
                    for c in range(NCH):
                        t, r = c // 2, CH * (c % 2)
                        last = pe.matmul(update_bank(c), kdtok[r:r + CH, P * t:P * t + P], vtok[r:r + CH, t, GDV * h:GDV * h + GDV],
                                         start=True, stop=True)
                    last.then_inc(s("U_ready"), 1)
                    pe.wait_ge(s("gla_state"), NCH * (h + 1))
                    pe.wait_ge(s("qb"), h + 1)
                    for vt in range(2):
                        for t in range(4):
                            col = GDV * h + P * vt
                            last = pe.matmul(ps[:, 4 + vt, P * t:P * t + P], vtok[:, t, col:col + P],
                                             aTm[:, P * t:P * t + P], start=True, stop=False)
                            for c in (2 * t, 2 * t + 1):
                                if c >= 1:
                                    last = pe.matmul(ps[:, 4 + vt, CH * c:CH * c + CH], Sall[:, c - 1, P * vt:P * vt + P],
                                                     X5[:, CH * c:CH * c + CH], start=False, stop=c % 2 == 1)
                    last.then_inc(s("o_ready"), 1)
                    pe.wait_ge(s("o_sq"), h + 1)
                    for vt in range(2):
                        last = pe.matmul(ps[:, 6, :], ones, sq2[:, vt, :], start=vt == 0, stop=vt == 1)
                    last.then_inc(s("o_summed"), 1)
                pe.wait_ge(s("o_done"), GH)
                for h in range(GH):
                    last = pe.matmul(ps[:, 4, NS * h:NS * h + NS], wg2[:, GDK * h:GDK * h + GDK], lrT[0:GR + 1, TP:T],
                                     start=True, stop=True)
                last.then_inc(s("z_ready"), 1)
                for m in range(4):
                    last = pe.transpose(ps[0:NS, 5, P * m:P * m + P], gk[:, m, TP:T], ident)
                for m in range(KD):
                    last = pe.transpose(ps[0:NS, 6 + m // 4, P * (m % 4):P * (m % 4) + P], gv[:, m, TP:T], ident)
                last.then_inc(s("kvs_T"), 1)
                pe.wait_ge(s("g_ready"), 5)
                pe.wait_ge(s("kvs"), 1)
                for b in range(NS):
                    pe.wait_ge(s("kmask"), b + 1)
                    if b >= 1:
                        pe.wait_ge(s("gs_new"), b)
                    for h in range(GH):
                        last = pe.matmul(ps[:, 4 + h // 2, GDV * (h % 2):GDV * (h % 2) + GDV],
                                         kmask[:, b % 2, GDK * h:GDK * h + GDK], vtS[:, GDV * h:GDV * h + GDV],
                                         start=True, stop=True)
                    last.then_inc(s("kv_outer"), 1)
                    pe.wait_ge(s("gs_new"), b + 1)
                    for h in range(GH):
                        for vt in range(2):
                            col = (2 * h + vt) * NS + b
                            last = pe.matmul(ps[:, 6, col:col + 1], Sring[:, b % 2, GDV * h + P * vt:GDV * h + P * vt + P],
                                             qS[:, h, b:b + 1], start=True, stop=True)
                    last.then_inc(s("gs_read"), 1)
                pe.wait_ge(s("o_sq"), 5)
                for vt in range(2):
                    last = pe.matmul(ps[:, 7, 0:32], ones, sqS[:, vt:KD:2, :], start=vt == 0, stop=vt == 1)
                last.then_inc(s("o_summed"), 1)
                pe.wait_ge(s("o_v"), GH + 1)
                for j, u in enumerate(group_units(0)):
                    multiply(pe, u, actH, actL)
                    ada_pe(pe, 8 + j)


        hank = at(0, AH, 512)
        qkS = at(0, NG, AG, parts=NS)
        vnew = at(1536, NG, AG, parts=NS)
        kring = at(3072, 2, AG)
        biasT = at(16640, AH, 512)
        avt = at(20736, 4, AG)
        kst = at(22784, 2, AG)
        sq_ = at(23808, 2, 512)
        PT = at(24832, 2, 512)
        bnd = at(25856, 2, AH * BND)
        sc = at(26912, NG, NS * AH)
        snew = at(27104, NG, AH, parts=NS)
        SS = at(27128, NG, SK, parts=NS * AH)
        sbias = at(27515, NG, SK, parts=NS * AH)
        pT = at(27902, NG, NS * AH)
        small = at(28094, 32)
        snd = at(28126, NG, AH, parts=NS * AH)
        snr = at(28150, NG, 1, parts=NS * AH)
        prod = at(28190, AG)
        relb = at(28702, NG * AH, parts=33)
        relbS = at(28726, NG, NS * AH, parts=33)
        onehot = at(23808, NG * (BW + SK), parts=33)
        bvec = at(20736, NG, BW, parts=AH)
        NB = NG * (BW + SK)
        BC = ((0, 2 * P), (2 * P, 3 * P), (3 * P, 4 * P))

        def rows(g, c):
            return slice(P * c, P * c + P) if g == 0 else slice(c, TP, 4)

        def steps(g):
            if g == 0:
                return [(c, slice(h, h + 3, 2), [c] if c == 0 else [c - 1, c]) for c in range(4) for h in (0, 4, 1, 5)]
            return [(c, slice(h, AH, 2), [c]) for c in range(4) for h in (0, 1)]

        J0 = [0, 16, 24]
        KOUT = [[3], [0, 1, 2, 3], [0, 1, 2, 3]]
        K0 = [0, 1, 5]
        NK = (P, P, P // 2)

        def win_rows(g, c, kv):
            v = o[f"win{g + 1}_p"]
            v = v[:, :] if g == 0 else v.rearrange("(i c) n -> c i n", c=4)[c]
            return v[:, AG * kv:AG * kv + AG]

        def cache_rows(g, b, kv):
            v = w[f"cache_win{g + 1}"][b].rearrange("(i c) n -> c i n", c=DIL[g])[0]
            return v[:, AG * kv:AG * kv + AG]

        def bias_sp(sp):
            sp.dma_start(relb[0:32, :], w["rel_bias"]).then_inc(s("relb_in"), 16)
            sp.dma_start(onehot, con["onehot"]).then_inc(s("relb_in"), 16)
            sp.wait_ge(s("bvec_ready"), NG)
            sp.dma_start(bd.rearrange("(g h) n -> h g n", g=NG), bvec).then_inc(s("bias_spilled"), 16)
            sp.wait_ge(s("bias_spilled"), 16)
            for g in range(NG):
                lo, hi = BC[g]
                src = bass.AP(bd.tensor, g * AH * BW, [[1, P], [BW, AH], [1, hi - lo]])
                sp.dma_start(hank[:, :, lo:hi], src).then_inc(s("hank_in"), 16)

        def bias_pe(pe):
            pe.wait_ge(s("relb_in"), 32)
            pe.wait_ge(s("relb_ready"), 1)
            for g in range(NG):
                pe.matmul(ps[0:AH, 4 + g, 0:BW], relb[:, AH * g:AH * g + AH], onehot[:, BW * g:BW * g + BW],
                          start=True, stop=True).then_inc(s("bvec_T"), 1)
                last = pe.matmul(ps[0:NS * AH, 7, SK * g:SK * g + SK], relbS[:, g, :],
                                 onehot[:, NG * BW + SK * g:NG * BW + SK * g + SK], start=True, stop=True)
            last.then_inc(s("sbias_T"), 1)
            pe.wait_ge(s("hank_in"), 16 * NG)
            pe.wait_ge(s("bvec_ready"), NG)
            for h in range(AH):
                if h >= 2:
                    pe.wait_ge(s("bias_ready"), h - 1)
                pe.matmul(ps[:, 4 + h % 2, :], flip, hank[:, h, :], start=True, stop=True).then_inc(s("flipped"), 1)

        def bias_act(act):
            for h in range(AH):
                act.wait_ge(s("flipped"), h + 1)
                act.activation(biasT[:, h, :], ps[:, 4 + h % 2, :], ACT.Copy).then_inc(s("bias_ready"), 1)

        def bias_dve(dve):
            dve.memset(relb[32:33, :], 1.0)
            dve.memset(sc[:, NG - 1, :], 0.0)
            dve.wait_ge(s("relb_in"), 32)
            dch.link(dve, dve.memset(prod[:, 0:1], 0.0))
            for g in range(NG):
                last = dve.tensor_copy(relbS[:, g, :].rearrange("p (b h) -> p b h", h=AH),
                                       relb[:, AH * g:AH * g + AH].unsqueeze(1).to_broadcast([33, NS, AH]))
            last.then_inc(s("relb_ready"), 1)
            for g in range(NG):
                dve.wait_ge(s("bvec_T"), g + 1)
                dve.tensor_copy(bvec[:, g, :], ps[0:AH, 4 + g, 0:BW]).then_inc(s("bvec_ready"), 1)
            dve.wait_ge(s("sbias_T"), 1)
            dve.tensor_copy(sbias.rearrange("p g n -> p (g n)"), ps[0:NS * AH, 7, 0:NG * SK]).then_inc(s("sbias"), 1)

        def heads_tok_pe(pe, g, A):
            if g == 0:
                pe.wait_ge(s("bias_ready"), AH)
                pe.wait_ge(s("sbias"), 1)
            for c in range(4):
                if c >= 2:
                    pe.wait_ge(s("av_tok"), 4 * g + c - 1)
                for m in range(4):
                    last = pe.transpose(ps[:, 4 + c % 2, P * m:P * m + P], A[:, 8 + m, rows(g, c)], ident)
                last.then_inc(s("av_T"), 1)
            for i, c in enumerate(KOUT[g]):
                if i >= 2:
                    pe.wait_ge(s("k_tok"), K0[g] + i - 1)
                for m in range(4):
                    last = pe.transpose(ps[:, 6 + i % 2, P * m:P * m + P], A[:, 4 + m, rows(g, c)], ident)
                last.then_inc(s("ak_T"), 1)
            pe.wait_ge(s("av_tok"), 4 * g + 4)
            pe.wait_ge(s("k_tok"), K0[g] + len(KOUT[g]))
            for a in range(3):
                for m in range(4):
                    last = pe.transpose(ps[0:NS, 4 + a, P * m:P * m + P], A[:, 4 * a + m, TP:T], ident)
            last.then_inc(s("new_T"), 1)

        def heads_tok_act(act, g):
            for c in range(4):
                act.wait_ge(s("av_T"), 4 * g + c + 1)
                act.activation(avt[:, c, :], ps[:, 4 + c % 2, :], ACT.Copy).then_inc(s("av_tok"), 1)
            act.wait_ge(s("new_T"), g + 1)
            act.activation(qkS[:, 0:2, :], ps[0:NS, 4:6, :], ACT.Copy)
            act.activation(vnew[:, g, :], ps[0:NS, 6, :], ACT.Copy).then_inc(s("new_tok"), 1)

        def heads_tok_dve(dve, g):
            for i in range(len(KOUT[g])):
                n = K0[g] + i
                dve.wait_ge(s("ak_T"), n + 1)
                if n >= 2:
                    dve.wait_ge(s(f"k_out{n % 2}"), 16 * (n // 2))
                dve.tensor_copy(kst[:, n % 2, :], ps[:, 6 + i % 2, :]).then_inc(s("k_tok"), 1)
            dve.wait_ge(s("new_tok"), g + 1)
            dch.link(dve, dve.tensor_tensor(qkS[:, 2, :], qkS[:, 0, :], qkS[:, 1, :], ALU.mult))
            dve.tensor_reduce(snew[:, g, :], qkS[:, 2, :].rearrange("p (h e) -> p h e", e=AE), AX.X, ALU.add)

        def heads_tok_sp(sp, g):
            for i, c in enumerate(KOUT[g]):
                n = K0[g] + i
                sp.wait_ge(s("k_tok"), n + 1)
                sp.dma_start(win_rows(g, c, 0), kst[:, n % 2, :]).then_inc(s(f"k_out{n % 2}"), 16)
                sp.wait_ge(s("av_tok"), 4 * g + c + 1)
                sp.dma_start(win_rows(g, c, 1), avt[:, c, :]).then_inc(outs, 16)
                n_outs[0] += 16
            sp.wait_ge(s("new_tok"), g + 1)
            last = WIN[g] - 1
            sp.dma_start(o[f"win{g + 1}_s"][:, last, 0:AG], qkS[:, 1, :]).then_inc(outs, 16)
            sp.dma_start(o[f"win{g + 1}_s"][:, last, AG:2 * AG], vnew[:, g, :]).then_inc(outs, 16)
            n_outs[0] += 32

        def attend_pe(pe, g, A):
            st = steps(g)
            pe.wait_ge(s("new_tok"), g + 1)
            for j in range(len(st) + 2):
                if j < len(st):
                    c, hs, keys = st[j]
                    nh, h0 = AH // 4 if g == 0 else AH // 2, hs.start
                    n = J0[g] + j
                    J = P * len(keys)
                    if n >= 2:
                        pe.wait_ge(s("s_read"), n - 1)
                    for i in range(nh):
                        h = h0 + 2 * i
                        r = AE * (h % 2)
                        kt = slice(P * keys[0], P * keys[0] + J) if g == 0 else rows(g, c)
                        last = pe.matmul(ps[:, 4 + n % 2, J * i:J * i + J], A[r:r + AE, h // 2, rows(g, c)],
                                         A[r:r + AE, 4 + h // 2, kt], start=True, stop=True)
                    last.then_inc(s("s_ready"), 1)
                if 1 <= j <= len(st):
                    c, hs, keys = st[j - 1]
                    nh, h0 = AH // 4 if g == 0 else AH // 2, hs.start
                    n = J0[g] + j - 1
                    pe.wait_ge(s("p_ready"), n + 1)
                    if n >= 1:
                        pe.wait_ge(s("pT_ready"), n)
                    for i in range(nh * len(keys)):
                        last = pe.transpose(ps[:, 6, P * i:P * i + P], sq_[:, n % 2, P * i:P * i + P], ident)
                    last.then_inc(s("p_T"), 1)
                if j >= 2:
                    c, hs, keys = st[j - 2]
                    nh, h0 = AH // 4 if g == 0 else AH // 2, hs.start
                    n = J0[g] + j - 2
                    pe.wait_ge(s("pT_ready"), n + 1)
                    if h0 == 0 and 4 * g + c >= 1:
                        pe.wait_ge(s("o_read"), 4 * g + c)
                    for i in range(nh):
                        h = h0 + 2 * i
                        for kb, kt in enumerate(keys):
                            x = i * len(keys) + kb
                            last = pe.matmul(ps[:, 7, AE * h:AE * h + AE], PT[:, n % 2, P * x:P * x + P],
                                             avt[:, kt, AE * h:AE * h + AE], start=kb == 0, stop=kb == len(keys) - 1)
                    last.then_inc(s("pv"), 1)

        def attend_dve(dve, g):
            st = steps(g)

            def gather(c, n):
                dve.wait_ge(s("pv"), n + 1)
                out = bnd[:, c % 2, :].rearrange("p (h f) -> p h f", f=BND)[:, :, 0:AE]
                dve.tensor_copy(out, ps[:, 7, :].rearrange("p (h e) -> p h e", e=AE)).then_inc(s("o_read"), 1)

            due = []
            for j, (c, hs, keys) in enumerate(st):
                nh, h0 = AH // 4 if g == 0 else AH // 2, hs.start
                n = J0[g] + j
                J = P * len(keys)
                lo, hi = BC[g]
                lo = hi - J
                dve.wait_ge(s("s_ready"), n + 1)
                if n >= 2:
                    dve.wait_ge(s("p_T"), n - 1)
                sv = sq_[:, n % 2, 0:nh * J].rearrange("p (h k) -> p h k", k=J)
                dve.scalar_tensor_tensor(sv, ps[:, 4 + n % 2, 0:nh * J].rearrange("p (h k) -> p h k", k=J), SCALE,
                                         biasT[:, hs, lo:hi], ALU.mult, ALU.add).then_inc(s("s_read"), 1)
                dve.wait_ge(s("s_read"), n + 1)
                if h0 == 0 and 4 * g + c >= 2:
                    dve.wait_ge(s(f"g_out{c % 2}"), 16 * ((4 * g + c) // 2))
                nm = bnd[:, c % 2, :].rearrange("p (h f) -> p h f", f=BND)[:, hs, AE]
                dve.tensor_reduce(nm, sv, AX.X, ALU.max, negate=True).then_inc(s("m_ready"), 1)
                if due and due[0][0] == j:
                    gather(*due.pop(0)[1:])
                if j + 1 == len(st) or st[j + 1][0] != c:
                    due.append((j + 2, c, n))
            for _, c, n in due:
                gather(c, n)

        def attend_act(act, g):
            st = steps(g)
            for j in range(len(st) + 1):
                if j < len(st):
                    c, hs, keys = st[j]
                    nh, h0 = AH // 4 if g == 0 else AH // 2, hs.start
                    n = J0[g] + j
                    J = P * len(keys)
                    act.wait_ge(s("m_ready"), n + 1)
                    for i in range(nh):
                        b0 = BND * (h0 + 2 * i)
                        sv = sq_[:, n % 2, J * i:J * i + J]
                        last = act.activation(sv, sv, ACT.Exp, bias=bnd[:, c % 2, b0 + AE:b0 + AE + 1],
                                              accum_out=bnd[:, c % 2, b0 + AE + 1:b0 + AE + 2])
                    last.then_inc(s("p_ready"), 1)
                if j >= 1:
                    c, hs, keys = st[j - 1]
                    nh, h0 = AH // 4 if g == 0 else AH // 2, hs.start
                    n = J0[g] + j - 1
                    act.wait_ge(s("p_T"), n + 1)
                    if n >= 2:
                        act.wait_ge(s("pv"), n - 1)
                    k = P * nh * len(keys)
                    act.activation(PT[:, n % 2, 0:k], ps[:, 6, 0:k], ACT.Copy).then_inc(s("pT_ready"), 1)

        def attend_sp(sp, g):
            for c in range(4):
                sp.wait_ge(s("o_read"), 4 * g + c + 1)
                sp.wait_ge(s("p_ready"), J0[g] + (4 if g == 0 else 2) * (c + 1))
                dst = gd[g][P * c:P * c + P, :] if g == 0 else gd[g].rearrange("(i c) n -> c i n", c=4)[c]
                sp.dma_start(dst, bnd[:, c % 2, :]).then_inc(s(f"g_out{c % 2}"), 16)

        def sample_sp(sp, g):
            for b in range(NS):
                n = NS * g + b
                if n >= 2:
                    sp.wait_ge(s("sc_mul"), n - 1)
                sp.dma_start(kring[0:NK[g], b % 2, :], cache_rows(g, b, 0)).then_inc(s(f"kc_in{b % 2}"), 16)

        def sample_pe(pe, g):
            for b in range(NS):
                n = NS * g + b
                if b == 0:
                    pe.wait_ge(s("s_read"), J0[g] + len(steps(g)))
                if n >= 2:
                    pe.wait_ge(s("sc_mul"), n - 1)
                pe.matmul(ps[:, 4 + b % 2, :], ident[0:NS, b:b + 1].to_broadcast([NS, P]), qkS[:, 0, :],
                          start=True, stop=True).then_inc(s("q_wide"), 1)

        def sample_dve(dve, g):
            k = NK[g]
            for b in range(NS):
                n = NS * g + b
                dve.wait_ge(s("q_wide"), n + 1)
                dve.wait_ge(s(f"kc_in{b % 2}"), 16 * (n // 2 + 1))
                dve.tensor_tensor(prod[0:k, :], kring[0:k, b % 2, :], ps[0:k, 4 + b % 2, :], ALU.mult)\
                   .then_inc(s("sc_mul"), 1)
                dve.wait_ge(s("sc_mul"), n + 1)
                dch.link(dve, dve.tensor_reduce(sc[0:k, g, AH * b:AH * b + AH],
                                                prod[0:k, :].rearrange("p (h e) -> p h e", e=AE), AX.X, ALU.add))

        for g in range(NG):
            A = AQKV[g % 2]
            nxt = group_units(g + 1) if g + 1 < NG else []
            B = AQKV[(g + 1) % 2]
            ada0 = 14 + 6 * g

            with nc.Block() as block:
                @block.sync
                def _(sp):
                    if g == 0:
                        bias_sp(sp)
                    heads_tok_sp(sp, g)
                    attend_sp(sp, g)
                    sample_sp(sp, g)
                    if nxt:
                        after = nxt[-1] + 1 + (U[nxt[-1] + 1]["kind"] == "ada")
                        for u in range(nxt[0] + 2, after + 2):
                            issue(sp, u)
                    nk = K0[g] + len(KOUT[g])
                    for d in range(2):
                        sp.wait_ge(s(f"g_out{d}"), 32 * (g + 1))
                        sp.wait_ge(s(f"k_out{d}"), 16 * ((nk + 1 - d) // 2)) if nk > d else None

                @block.scalar
                def _(act):
                    if g == 0:
                        bias_act(act)
                    heads_tok_act(act, g)
                    attend_act(act, g)
                    for j, u in enumerate(nxt):
                        copy_tiles(act, u, B, 2 * j)

                @block.vector
                def _(dve):
                    if g == 0:
                        bias_dve(dve)
                    heads_tok_dve(dve, g)
                    attend_dve(dve, g)
                    sample_dve(dve, g)
                    for j, u in enumerate(nxt):
                        split_lo(dve, U[u]["i"] + 1)
                        if ada0 + j < len(ADA):
                            ada_dve(dve, ada0 + j)

                @block.tensor
                def _(pe):
                    if g == 0:
                        bias_pe(pe)
                    heads_tok_pe(pe, g, A)
                    attend_pe(pe, g, A)
                    sample_pe(pe, g)
                    for j, u in enumerate(nxt):
                        multiply(pe, u, actH, actL)
                        if ada0 + j < len(ADA):
                            ada_pe(pe, ada0 + j)

        cmb = at(12480, 2, NG * AH * BND)
        of = at(15648, 2, AG)
        cw = [at(20736 + 32 * i, NG, AH) for i in range(4)]
        cw8 = [at(20864 + 8 * i, AH) for i in range(4)]
        diag = at(23808, NG, NS * AH, parts=NS * AH)
        pn = at(24000, NG, NS * AH, parts=NS)
        sel8 = at(24192, NS * AH, parts=NS)
        sel64 = at(24256, NS, parts=NS * AH)
        hmask = at(24264, AH, parts=NS * AH)
        NR = NS * AH

        with nc.Block() as block:
            @block.sync
            def _(sp):
                sp.dma_start(sel8, con["sel8"]).then_inc(s("relb_in"), 16)
                sp.dma_start(sel64, con["sel64"]).then_inc(s("relb_in"), 16)
                sp.dma_start(hmask, con["hmask"]).then_inc(s("relb_in"), 16)
                for c in range(4):
                    if c >= 2:
                        sp.wait_ge(s("joined"), c - 1)
                    for g in range(NG):
                        sp.dma_start(cmb[:, c % 2, AH * BND * g:AH * BND * (g + 1)],
                                     gd[g].rearrange("(i c) n -> c i n", c=4)[c]).then_inc(s(f"cmb_in{c % 2}"), 16)
                for n in range(NG * NS):
                    g, b = n // NS, n % NS
                    if n >= 2:
                        sp.wait_ge(s("vc_used"), n - 1)
                    sp.dma_start(kring[0:NK[g], n % 2, :], cache_rows(g, b, 1)).then_inc(s(f"kc_in{n % 2}"), 16)

            @block.vector
            def _(dve):
                d, e, wd, al = cw
                mn, den, rd, _ = cw8
                for c in range(4):
                    dve.wait_ge(s(f"cmb_in{c % 2}"), 48 * (c // 2 + 1))
                    C = cmb[:, c % 2, :].rearrange("p (g h f) -> p g h f", g=NG, f=BND)
                    dch.link(dve, dve.tensor_tensor(mn, C[:, 0, :, AE], C[:, 1, :, AE], ALU.min))
                    dch.link(dve, dve.tensor_tensor(mn, mn, C[:, 2, :, AE], ALU.min))
                    dve.tensor_tensor(d, mn.unsqueeze(1).to_broadcast([P, NG, AH]), C[:, :, :, AE], ALU.subtract)\
                       .then_inc(s("join_d"), 1)
                    dve.wait_ge(s("join_e"), c + 1)
                    dch.link(dve, dve.tensor_tensor(wd, e, C[:, :, :, AE + 1], ALU.mult))
                    dch.link(dve, dve.tensor_tensor(den, wd[:, 0, :], wd[:, 1, :], ALU.add))
                    dch.link(dve, dve.tensor_tensor(den, den, wd[:, 2, :], ALU.add))
                    dch.link(dve, dve.reciprocal(rd, den))
                    dch.link(dve, dve.tensor_tensor(al, e, rd.unsqueeze(1).to_broadcast([P, NG, AH]), ALU.mult))
                    for g in range(NG):
                        ins = dve.tensor_tensor(C[:, g, :, 0:AE], C[:, g, :, 0:AE],
                                                al[:, g, :].unsqueeze(2).to_broadcast([P, AH, AE]), ALU.mult)
                    dch.link(dve, ins)
                    if c >= 2:
                        dve.wait_ge(s("oj_T"), c - 1)
                    ov = of[:, c % 2, :].rearrange("p (h e) -> p h e", e=AE)
                    dch.link(dve, dve.tensor_tensor(ov, C[:, 0, :, 0:AE], C[:, 1, :, 0:AE], ALU.add))
                    dve.tensor_tensor(ov, ov, C[:, 2, :, 0:AE], ALU.add).then_inc(s("joined"), 1)
                    dve.wait_ge(s("oj_hi"), c + 1)
                    dve.tensor_tensor(a2L[:, 0:4, c:TP:4], ps[:, 4 + c % 2, :].rearrange("p (f i) -> p f i", f=4),
                                      a2H[:, 0:4, c:TP:4].bitcast(F32), ALU.subtract).then_inc(s("oj_lo"), 1)
                dve.wait_ge(s("sn_T"), 1)
                dve.wait_ge(s("relb_in"), 80)
                dch.link(dve, dve.tensor_tensor(snd, ps[0:NR, 7, 0:NG * AH].rearrange("p (g h) -> p g h", g=NG),
                                                hmask.unsqueeze(1).to_broadcast([NR, NG, AH]), ALU.mult))
                dch.link(dve, dve.tensor_reduce(snr[:, :, 0], snd, AX.X, ALU.add))
                dve.scalar_tensor_tensor(SS[:, :, 0:P], ps[0:NR, 6, 0:NG * P].rearrange("p (g k) -> p g k", g=NG), SCALE,
                                         sbias[:, :, 0:P], ALU.mult, ALU.add)
                dch.link(dve, dve.scalar_tensor_tensor(SS[:, :, P:SK], snr, SCALE, sbias[:, :, P:SK], ALU.mult, ALU.add))
                dve.tensor_reduce(small[0:NR, 0:1], SS, AX.XY, ALU.max, negate=True).then_inc(s("sm_m"), 1)
                dve.wait_ge(s("sm_p"), 1)
                dch.link(dve, dve.reciprocal(small[0:NR, 2:3], small[0:NR, 1:2]))
                dve.tensor_scalar(SS, SS, small[0:NR, 2:3], None, ALU.mult).then_inc(s("sm_m"), 1)
                dve.wait_ge(s("sm_m"), 2)
                dve.tensor_tensor(diag, ident[0:NR, 0:NR].unsqueeze(1).to_broadcast([NR, NG, NR]),
                                  SS[:, :, P:SK].to_broadcast([NR, NG, NR]), ALU.mult).then_inc(s("sm_m"), 1)
                dve.wait_ge(s("sn_T"), 2)
                dve.tensor_copy(pT.rearrange("p g n -> p (g n)"), ps[:, 6, 0:NG * NR]).then_inc(s("spT"), 1)
                dve.wait_ge(s("sn_T"), 3)
                dve.tensor_copy(pn.rearrange("p g n -> p (g n)"), ps[0:NS, 7, 0:NG * NR]).then_inc(s("spT"), 1)
                dve.wait_ge(s("os_hi"), 1)
                for r in range(2):
                    q = slice(AE * r, AE * r + AE)
                    last = dve.tensor_tensor(a2L[q, 0:4, TP:T],
                                             ps[q, 4, 0:NR].rearrange("p (f b r) -> p f b r", f=4, r=2)[:, :, :, r],
                                             a2H[q, 0:4, TP:T].bitcast(F32), ALU.subtract)
                last.then_inc(s("oj_lo"), 1)

            @block.scalar
            def _(act):
                for c in range(4):
                    act.wait_ge(s("join_d"), c + 1)
                    act.activation(cw[1], cw[0], ACT.Exp).then_inc(s("join_e"), 1)
                    act.wait_ge(s("oj_T"), c + 1)
                    act.activation(a2H[:, 0:4, c:TP:4], ps[:, 4 + c % 2, :].rearrange("p (f i) -> p f i", f=4), ACT.Copy)\
                       .then_inc(s("oj_hi"), 1)
                act.wait_ge(s("sm_m"), 1)
                act.activation(SS, SS, ACT.Exp, bias=small[0:NR, 0:1], accum_out=small[0:NR, 1:2]).then_inc(s("sm_p"), 1)
                act.wait_ge(s("vc_used"), NG * NS)
                for r in range(2):
                    q = slice(AE * r, AE * r + AE)
                    last = act.activation(a2H[q, 0:4, TP:T],
                                          ps[q, 4, 0:NR].rearrange("p (f b r) -> p f b r", f=4, r=2)[:, :, :, r], ACT.Copy)
                last.then_inc(s("os_hi"), 1)

            @block.tensor
            def _(pe):
                for c in range(4):
                    pe.wait_ge(s("joined"), c + 1)
                    if c >= 2:
                        pe.wait_ge(s("oj_lo"), c - 1)
                    for f in range(4):
                        last = pe.transpose(ps[:, 4 + c % 2, P * f:P * f + P], of[:, c % 2, P * f:P * f + P], ident)
                    last.then_inc(s("oj_T"), 1)
                pe.wait_ge(s("relb_in"), 80)
                for g in range(NG):
                    last = pe.transpose(ps[0:NR, 6, P * g:P * g + P], sc[:, g, :], ident)
                last = pe.matmul(ps[0:NR, 7, 0:NG * AH], sel8, snew.rearrange("p g h -> p (g h)"), start=True, stop=True)
                last.then_inc(s("sn_T"), 1)
                pe.wait_ge(s("sm_m"), 2)
                for g in range(NG):
                    last = pe.transpose(ps[:, 6, NR * g:NR * g + NR], SS[:, g, 0:P], ident[0:NR, 0:NR])
                last.then_inc(s("sn_T"), 1)
                pe.wait_ge(s("sm_m"), 3)
                pe.matmul(ps[0:NS, 7, 0:NG * NR], sel64, diag.rearrange("p g n -> p (g n)"), start=True, stop=True)\
                  .then_inc(s("sn_T"), 1)
                pe.wait_ge(s("spT"), 2)
                pe.wait_ge(s("oj_lo"), 4)
                for g in range(NG):
                    for f in range(4):
                        pe.matmul(ps[:, 4, 16 * f:16 * f + 16], vnew[:, g, P * f:P * f + P],
                                  pn[:, g, :].rearrange("p (b h) -> p b h", h=AH)[:, :, 2 * f:2 * f + 2],
                                  start=g == 0 and f == 0, stop=False, skip_group_check=True)
                for n in range(NG * NS):
                    g, b = n // NS, n % NS
                    k = NK[g]
                    pe.wait_ge(s(f"kc_in{n % 2}"), 16 * (NG * NS // 2 + n // 2 + 1))
                    for f in range(4):
                        last = pe.matmul(ps[:, 4, 16 * f + 2 * b:16 * f + 2 * b + 2], kring[0:k, n % 2, P * f:P * f + P],
                                         pT[0:k, g, AH * b + 2 * f:AH * b + 2 * f + 2], start=False,
                                         stop=n == NG * NS - 1 and f == 3, skip_group_check=True)
                    last.then_inc(s("vc_used"), 1)

        oT4 = at(0, KD, T)
        ya, yb = at(12480, KD, T), at(16640, KD, T)
        sg4 = at(20800, 2, T)
        f4 = at(FT, 4, T)
        xT = at(FX, KD, T)
        n2 = norm_temps(0)
        gated = at(FT + 2400, NS)
        G = {k: units(k) for k in ("bb", "gr", "ba", "ga", "gb", "wo", "up", "dn")}

        sg_free = [(s("a2_f"), q + 1) for q in range(KD)] + [(s("ga_used"), q + 1) for q in range(KD)] \
            + [(s("a2_f"), KD + q + 1) for q in range(KD)]

        def end_pass(us):
            return U[us[-1]]["pass0"] + U[us[-1]]["mt"]

        def residual_dve(dve, n, q, gate):
            a, b = ps[:, 2 * (n % 2), 0:HT], ps[:, 2 * (n % 2) + 1, 0:HT]
            g = mod[:, gate + q, 0:1]
            dve.scalar_tensor_tensor(xT[:, q, 0:HT], a, g, xT[:, q, 0:HT], ALU.mult, ALU.add)
            dve.scalar_tensor_tensor(xT[:, q, HT:TP], b[:, 0:TP - HT], g, xT[:, q, HT:TP], ALU.mult, ALU.add)
            dve.tensor_tensor(gated, b[:, TP - HT:HT], mod[:, gate + q, 1:NC], ALU.mult).then_inc(tile_read["dve"], 1)
            dve.wait_ge(tile_read["dve"], freed[n])
            dch.link(dve, dve.tensor_tensor(xT[:, q, TP:T], xT[:, q, TP:T], gated, ALU.add))

        with nc.Block() as block:
            @block.sync
            def _(sp):
                sp.dma_start(oT4.rearrange("p k t -> p (k t)"), od).then_inc(s("o_back"), 16)
                sp.dma_start(xT.rearrange("p k t -> p (k t)"), xd).then_inc(s("x_back"), 16)
                for u in range(G["bb"][0] + 2, G["up"][0] + 2):
                    issue(sp, u)

            @block.scalar
            def _(act):
                r = 0

                def sigmoid(n, inc):
                    nonlocal r
                    act.wait_ge(pass_done, passes[n])
                    if r >= 2:
                        act.wait_ge(*sg_free[r - 2])
                    act.activation(halves(sg4[:, r % 2, :]), banks(n), ACT.Sigmoid).then_inc(inc, 1)
                    r += 1

                def high(src, q, i):
                    act.wait_ge(s("a2_f"), i + 1)
                    act.activation(a2H[:, q, :], src, ACT.Copy).then_inc(s("a2_hi"), 1)

                for j, u in enumerate(G["bb"]):
                    copy_tiles(act, u, yb, 4 * j)
                for j, u in enumerate(G["gr"]):
                    split_hi(act, U[u]["i"] + 1)
                    for m in range(2):
                        sigmoid(U[u]["tile0"] + m, s("gr_sig"))
                    for q in (2 * j - 2, 2 * j - 1):
                        if q >= 0:
                            high(f4[:, q % 4, :], q, q)
                for q in (KD - 2, KD - 1):
                    high(f4[:, q % 4, :], q, q)
                for j, u in enumerate(G["ba"]):
                    copy_tiles(act, u, ya, 2 * j)
                for u in G["ga"]:
                    split_hi(act, U[u]["i"] + 1)
                    for m in range(2):
                        sigmoid(U[u]["tile0"] + m, tile_read["act"])
                for j, u in enumerate(G["gb"]):
                    split_hi(act, U[u]["i"] + 1)
                    for m in range(2):
                        sigmoid(U[u]["tile0"] + m, tile_read["act"])
                    for q in (2 * j - 2, 2 * j - 1):
                        if q >= 0:
                            high(ya[:, q, :], q, KD + q)
                for q in (KD - 2, KD - 1):
                    high(ya[:, q, :], q, KD + q)
                for u in G["wo"]:
                    split_hi(act, U[u]["i"] + 1)
                norm_act(act, 1, n2)
                modulate_act(act, 1, n2)

            @block.vector
            def _(dve):
                r = 0

                def low(src, q, i):
                    dve.wait_ge(s("a2_hi"), i + 1)
                    dve.tensor_tensor(a2L[:, q, :], src, a2H[:, q, :].bitcast(F32), ALU.subtract).then_inc(s("a2_lo"), 1)

                for u in G["bb"]:
                    split_lo(dve, U[u]["i"] + 1)
                dve.wait_ge(s("o_back"), 16)
                dve.wait_ge(pass_done, end_pass(G["bb"]))
                for j, u in enumerate(G["gr"]):
                    split_lo(dve, U[u]["i"] + 1)
                    for m in range(2):
                        q, n = 2 * j + m, U[u]["tile0"] + m
                        dve.wait_ge(s("gr_sig"), q + 1)
                        dve.tensor_tensor(halves(sg4[:, r % 2, :]), halves(sg4[:, r % 2, :]), banks(n), ALU.mult)\
                           .then_inc(tile_read["dve"], 1)
                        dve.wait_ge(tile_read["dve"], freed[n])
                        if q >= 4:
                            dve.wait_ge(s("a2_lo"), q - 3)
                        dve.tensor_tensor(f4[:, q % 4, :], sg4[:, r % 2, :], oT4[:, q, :], ALU.mult).then_inc(s("a2_f"), 1)
                        dve.wait_ge(s("a2_f"), q + 1)
                        r += 1
                    for q in (2 * j - 2, 2 * j - 1):
                        if q >= 0:
                            low(f4[:, q % 4, :], q, q)
                for q in (KD - 2, KD - 1):
                    low(f4[:, q % 4, :], q, q)
                for u in G["ba"]:
                    split_lo(dve, U[u]["i"] + 1)
                for j, u in enumerate(G["ga"]):
                    split_lo(dve, U[u]["i"] + 1)
                    for m in range(2):
                        q, n = 2 * j + m, U[u]["tile0"] + m
                        dve.wait_ge(tile_read["act"], freed[n])
                        dve.tensor_tensor(ya[:, q, :], ya[:, q, :], sg4[:, r % 2, :], ALU.mult).then_inc(s("ga_used"), 1)
                        r += 1
                for j, u in enumerate(G["gb"]):
                    split_lo(dve, U[u]["i"] + 1)
                    for m in range(2):
                        q, n = 2 * j + m, U[u]["tile0"] + m
                        dve.wait_ge(tile_read["act"], freed[n])
                        dch.link(dve, dve.tensor_tensor(yb[:, q, :], yb[:, q, :], sg4[:, r % 2, :], ALU.mult))
                        r += 1
                        dve.wait_ge(s("ga_used"), KD)
                        dve.tensor_tensor(ya[:, q, :], ya[:, q, :], yb[:, q, :], ALU.add).then_inc(s("a2_f"), 1)
                        dve.wait_ge(s("a2_f"), KD + q + 1)
                    for q in (2 * j - 2, 2 * j - 1):
                        if q >= 0:
                            low(ya[:, q, :], q, KD + q)
                for q in (KD - 2, KD - 1):
                    low(ya[:, q, :], q, KD + q)
                dve.wait_ge(s("x_back"), 16)
                for j, u in enumerate(G["wo"]):
                    split_lo(dve, U[u]["i"] + 1)
                    for m in range(2):
                        n = U[u]["tile0"] + m
                        dve.wait_ge(pass_done, passes[n])
                        residual_dve(dve, n, 2 * j + m, 2 * KD)
                norm_sum_dve(dve, 1, xT, n2)
                modulate_dve(dve, 1, xT, n2, V_N2, 3 * KD, 4 * KD)

            @block.tensor
            def _(pe):
                for u in G["bb"]:
                    multiply(pe, u, a2H, a2L)
                for u in G["gr"]:
                    multiply(pe, u, actH, actL)
                pe.wait_ge(s("a2_lo"), KD)
                for u in G["ba"]:
                    multiply(pe, u, a2H, a2L)
                for u in G["ga"] + G["gb"]:
                    multiply(pe, u, actH, actL)
                pe.wait_ge(s("a2_lo"), 2 * KD)
                for u in G["wo"]:
                    multiply(pe, u, a2H, a2L)
                norm_pe(pe, 1, n2)

        abuf = at(FT, 2, T + 2)
        acc, sg5 = at(FT + 1044, T), at(FT + 1564, T)
        ast = at(FT + 2084, 2, P, parts=NS + 2)
        n3 = norm_temps(0)
        yst = at(4160, 2, D)
        ysst = at(6208, D, parts=NS)
        up0, dn0 = G["up"][0], G["dn"][0]
        v0, vd0 = U[up0]["i"], U[dn0]["i"]
        p0, t0 = U[up0]["pass0"], U[up0]["tile0"]
        td0 = U[dn0]["tile0"]
        FA, FD = freed[t0], freed[t0 + 1]

        with nc.Block() as block:
            @block.sync
            def _(sp):
                with sp.Fori(0, KF // 2 - 1) as i:
                    for d in range(2):
                        u = up0 + 2 + d
                        sp.wait_ge(lo_ready, v0 + 1 + d + 2 * i)
                        load(sp, u % 2, up_sources(w, P * (2 + d) + 2 * P * i))
                with sp.Fori(0, KD) as m:
                    for half in range(2):
                        u = dn0 + half
                        sp.wait_ge(lo_ready, vd0 - 1 + half + 2 * m)
                        load(sp, u % 2, down_sources(w, half, P * m))
                for t in range(4):
                    sp.wait_ge(s("y_tok"), t + 1)
                    sp.dma_start(o["y_prompt"][P * t:P * t + P, :], yst[:, t % 2, :]).then_inc(s(f"y_out{t % 2}"), 16)
                sp.wait_ge(s("y_tok"), 5)
                sp.dma_start(o["y_sample"], ysst).then_inc(outs, 16)
                n_outs[0] += 16
                sp.wait_ge(s("y_out0"), 32)
                sp.wait_ge(s("y_out1"), 32)
                sp.wait_ge(outs, n_outs[0])

            @block.gpsimd
            def _(pool):
                pool.wait_ge(outs_pool, n_outs_pool[0])

                def store(u, col):
                    pool.wait_ge(s("tail_tok"), u + 1)
                    pool.dma_start(o["conv_p"][:, col], ast[0:2, store.slot, :]).then_inc(s(f"conv_out{store.slot}"), 16)
                    pool.dma_start(o["conv_s"][:, 1, col], ast[2:NS + 2, store.slot, :])\
                        .then_inc(s(f"conv_out{store.slot}"), 16)

                with pool.Fori(0, KF // 2) as i:
                    for d in range(2):
                        store.slot = d
                        store(2 * i + d, bass.ds(P * d + 2 * P * i, P))
                for d in range(2):
                    pool.wait_ge(s(f"conv_out{d}"), 32 * (KF // 2))

            @block.scalar
            def _(act):
                def unit(i, d, first):
                    vn = v0 + 1 + d
                    act.wait_ge(w_dma[(up0 + 1 + d) % 2], U[up0 + 1 + d]["arrived"] + 32 * i)
                    act.wait_ge(pass_done, p0 + 2 * d + 4 * i)
                    act.activation(whi[:, vn % 2, :], wraw[:, (up0 + 1 + d) % 2, :], ACT.Copy).then_inc(hi_ready, 1)
                    act.wait_ge(pass_done, p0 + 2 * d + 1 + 4 * i)
                    if not first:
                        act.wait_ge(s("conv_done"), 2 * i + d - 1)
                        act.wait_ge(s("tail_T"), 2 * i + d - 1)
                    act.activation(halves(abuf[:, d, 2:T + 2]), banks(t0), ACT.Copy).then_inc(tile_read["act"], 1)
                    act.wait_ge(s("conv_done"), 2 * i + d + 1)
                    act.activation(sg5, acc, ACT.Sigmoid).then_inc(s("ffn_sig"), 1)
                    act.wait_ge(tile_read["dve"], FD + d + 2 * i)
                    act.activation(gH[:, bass.ds(2 * i + d, 1), :].rearrange("p a t -> p (a t)"), acc, ACT.Copy)\
                       .then_inc(s("g_hi"), 1)

                for d in range(2):
                    unit(0, d, True)
                with act.Fori(1, KF // 2) as i:
                    for d in range(2):
                        unit(i, d, False)
                for v in range(vd0, vd0 + 2 * KD):
                    split_hi(act, v + 1)
                norm_act(act, 2, n3)
                for t in range(4):
                    act.wait_ge(s("y_T"), t + 1)
                    if t >= 2:
                        act.wait_ge(s(f"y_out{t % 2}"), 16)
                    act.activation(yst[:, t % 2, :].rearrange("p (a b) -> p a b", a=2),
                                   ps[:, 2 * (t % 2):2 * (t % 2) + 2, :], ACT.Copy).then_inc(s("y_tok"), 1)
                act.wait_ge(s("y_T"), 5)
                act.activation(ysst.rearrange("p (a b) -> p a b", a=2), ps[0:NS, 4:6, :], ACT.Copy).then_inc(s("y_tok"), 1)

            @block.vector
            def _(dve):
                dch.link(dve, dve.memset(abuf[:, :, 0:2], 0.0))
                conv = sem("conv_chain")
                one = lambda c, j: vec[:, bass.ds(c + j, 1)]

                def unit(i, d, first):
                    vn = v0 + 1 + d
                    f = 2 * i + d
                    dve.wait_ge(hi_ready, vn + 1 + 2 * i)
                    dve.tensor_tensor(wlo[:, vn % 2, :], wraw[:, (up0 + 1 + d) % 2, :], whi[:, vn % 2, :].bitcast(F32),
                                      ALU.subtract).then_inc(lo_ready, 1)
                    dve.wait_ge(tile_read["act"], FA + d + 2 * i)
                    ab = abuf[:, d, :]
                    carried = stT[:, bass.ds(f, 1), :].rearrange("p a (b j) -> p (a b) j", j=2)
                    wj = [one(V_CW + KF * j, f) for j in range(3)]
                    cb = one(V_CB, f)
                    if not (first and d == 0):
                        dve.wait_ge(s("g_lo"), f)
                    dve.tensor_scalar(acc[:, 0:TP], ab[:, 0:TP], wj[0], cb, ALU.mult, ALU.add)
                    dve.tensor_scalar(acc[:, TP:T], carried[:, :, 0], wj[0], cb, ALU.mult, ALU.add).then_inc(conv, 1)
                    dve.wait_ge(conv, 4 * i + 2 * d + 1)
                    dve.scalar_tensor_tensor(acc[:, 0:TP], ab[:, 1:TP + 1], wj[1], acc[:, 0:TP], ALU.mult, ALU.add)
                    dve.scalar_tensor_tensor(acc[:, TP:T], carried[:, :, 1], wj[1], acc[:, TP:T], ALU.mult, ALU.add)\
                       .then_inc(conv, 1)
                    dve.wait_ge(conv, 4 * i + 2 * d + 2)
                    dve.scalar_tensor_tensor(acc, ab[:, 2:T + 2], wj[2], acc, ALU.mult, ALU.add).then_inc(s("conv_done"), 1)
                    dve.wait_ge(s("ffn_sig"), f + 1)
                    dve.tensor_tensor(acc, acc, sg5, ALU.mult).then_inc(s("silu"), 1)
                    dve.wait_ge(s("silu"), f + 1)
                    dve.wait_ge(pass_done, p0 + 2 * d + 2 + 4 * i)
                    dve.tensor_tensor(halves(acc), halves(acc), banks(t0 + 1), ALU.mult).then_inc(tile_read["dve"], 1)
                    dve.wait_ge(s("g_hi"), f + 1)
                    dve.tensor_tensor(gL[:, bass.ds(f, 1), :].rearrange("p a t -> p (a t)"), acc,
                                      gH[:, bass.ds(f, 1), :].rearrange("p a t -> p (a t)").bitcast(F32), ALU.subtract)\
                       .then_inc(s("g_lo"), 1)

                def tail(i, d, first):
                    dve.wait_ge(s("tail_T"), 2 * i + d + 1)
                    if not first:
                        dve.wait_ge(s(f"conv_out{d}"), 32 * i)
                    dve.tensor_copy(ast[:, d, :], ps[0:NS + 2, 6 + d, 0:P]).then_inc(s("tail_tok"), 1)

                unit(0, 0, True)
                unit(0, 1, True)
                tail(0, 0, True)
                with dve.Fori(1, KF // 2) as i:
                    unit(i, 0, False)
                    dve.wait_ge(s("tail_T"), 2 * i)
                    dve.wait_ge(s("conv_out1"), 32 * i - 32)
                    dve.tensor_copy(ast[:, 1, :], ps[0:NS + 2, 7, 0:P]).then_inc(s("tail_tok"), 1)
                    unit(i, 1, False)
                    tail(i, 0, False)
                tail(KF // 2 - 1, 1, False)
                dve.wait_ge(s("g_lo"), KF)
                for m in range(KD):
                    for half in range(2):
                        split_lo(dve, vd0 + 2 * m + half + 1)
                    n = td0 + m
                    dve.wait_ge(pass_done, passes[n])
                    residual_dve(dve, n, m, 5 * KD)
                norm_sum_dve(dve, 2, xT, n3)
                for k in range(KD):
                    dve.scalar_tensor_tensor(xT[:, k, :], xT[:, k, :], vec[:, V_NF + k:V_NF + k + 1], n3["r"],
                                             ALU.mult, ALU.mult).then_inc(s("y_ready"), 1)

            @block.tensor
            def _(pe):
                def unit(i, d, first):
                    f = 2 * i + d
                    pe.wait_ge(lo_ready, v0 + d + 1 + 2 * i)
                    if first and d == 0:
                        pe.wait_ge(s("h_split"), 2 * KD)
                    for m in range(2):
                        n = t0 + 2 * d + m
                        if first:
                            pe.wait_ge(tile_read[owner[n - 2]], freed[n - 2])
                        else:
                            pe.wait_ge(tile_read["act" if m == 0 else "dve"], (FA if m == 0 else FD) + d - 1 + 2 * i)
                        three_pass(pe, n, (v0 + d) % 2, [KD * m + k for k in range(KD)], actH, actL).then_inc(pass_done, 1)

                def tail(i, d, first):
                    pe.wait_ge(tile_read["act"], FA + d + 2 * i)
                    if not first:
                        pe.wait_ge(s("tail_tok"), 2 * i + d - 1)
                    pe.transpose(ps[0:NS + 2, 6 + d, 0:P], abuf[:, d, TP:T + 2], ident).then_inc(s("tail_T"), 1)

                unit(0, 0, True)
                unit(0, 1, True)
                tail(0, 0, True)
                with pe.Fori(1, KF // 2) as i:
                    unit(i, 0, False)
                    pe.wait_ge(tile_read["act"], FA - 1 + 2 * i)
                    pe.wait_ge(s("tail_tok"), 2 * i - 1)
                    pe.transpose(ps[0:NS + 2, 7, 0:P], abuf[:, 1, TP:T + 2], ident).then_inc(s("tail_T"), 1)
                    unit(i, 1, False)
                    tail(i, 0, False)
                pe.wait_ge(tile_read["act"], FA + KF - 1)
                pe.wait_ge(s("tail_tok"), KF - 1)
                pe.transpose(ps[0:NS + 2, 7, 0:P], abuf[:, 1, TP:T + 2], ident).then_inc(s("tail_T"), 1)
                pe.wait_ge(s("g_lo"), KF)

                def down(m, i, first):
                    n = td0 + m
                    for half in range(2):
                        pe.wait_ge(lo_ready, vd0 + 2 * m + half + 1 + 4 * i)
                        if half == 0 and first:
                            pe.wait_ge(tile_read[owner[n - 2]], freed[n - 2])
                        elif half == 0:
                            pe.wait_ge(tile_read["dve"], freed[td0] + m - 2 + 2 * i)
                        three_pass(pe, n, (vd0 + half) % 2, list(range(KF // 2)), gH, gL, k0=half * (KF // 2),
                                   begin=half == 0, end=half == 1).then_inc(pass_done, 1)

                for m in range(2):
                    down(m, 0, True)
                with pe.Fori(0, KD // 2 - 1) as i:
                    for m in range(2):
                        down(2 + m, i, False)
                norm_pe(pe, 2, n3)
                pe.wait_ge(s("y_ready"), KD)
                for t in range(4):
                    if t >= 2:
                        pe.wait_ge(s("y_tok"), t - 1)
                    for k in range(KD):
                        last = pe.transpose(ps[:, 2 * (t % 2) + k // 4, P * (k % 4):P * (k % 4) + P],
                                            xT[:, k, P * t:P * t + P], ident)
                    last.then_inc(s("y_T"), 1)
                for k in range(KD):
                    last = pe.transpose(ps[0:NS, 4 + k // 4, P * (k % 4):P * (k % 4) + P], xT[:, k, TP:T], ident)
                last.then_inc(s("y_T"), 1)


def bucket(dist):
    d = np.maximum(dist, 1).astype(np.float32)
    large = 16 + (np.log(d / 16) / np.log(2048 / 16) * 16).astype(np.int32)
    return np.where(dist < 16, dist, np.minimum(large, 31)).astype(np.int32)


def constants():
    i = np.arange(P)
    same = (i[:, None] // CH == i[None, :] // CH) & (i[:, None] <= i[None, :])
    cst = np.concatenate([np.eye(P), same / 16.0, same, np.eye(P)[::-1]], axis=1).astype(np.float32)
    x = np.arange(BW)
    hot = np.zeros((33, NG * (BW + SK)), np.float32)

    def fill(c0, dist, valid):
        b = bucket(np.where(valid, dist, 0))
        cols = c0 + np.arange(len(dist))
        hot[b[valid], cols[valid]] = 1.0
        hot[32, cols[~valid]] = NEG

    d = 2 * P - 1 - x
    fill(0, d, (d >= 0) & (d <= P))
    d = P - 1 - x
    fill(BW, 4 * d, d >= 0)
    fill(2 * BW, 4 * d, (d >= 0) & (d % 4 == 0))
    r = np.arange(SK)
    for g, (dil, reach) in enumerate(((1, P), (4, P), (16, P // 2))):
        m = np.where(r == P, 0, reach - r)
        fill(NG * BW + SK * g, dil * m, m >= 0 if reach == P else (r == P) | (r < reach))
    rows = np.arange(NS * AH)
    sel64 = (rows[:, None] // AH == np.arange(NS)[None, :]).astype(np.float32)
    hmask = (rows[:, None] % AH == np.arange(AH)[None, :]).astype(np.float32)
    return {"cst": cst, "onehot": hot, "sel8": np.ascontiguousarray(sel64.T), "sel64": sel64, "hmask": hmask}


_INS = {
    "x_prompt": (TP, D), "x_sample": (NS, D), "state_gla": (NS, GH, GDK, GDV),
    "cache_win1": (NS, WIN[0], 2 * AG), "cache_win2": (NS, WIN[1], 2 * AG), "cache_win3": (NS, WIN[2], 2 * AG),
    "state_conv": (NS, 2, FH), "c_prompt": (1, D), "c_sample": (NS, D), "w_ada": (D, 6 * D), "b_ada": (6 * D,),
    "norm1_g": (D,), "w_in": (D, C_GB + D), "gla_wg2": (GR, GH * GDK), "gla_bg": (GH * GDK,), "gla_norm_g": (GDV,),
    "w_branch_a": (D, D), "w_branch_b": (AG, D), "w_out": (D, D), "rel_bias": (32, NG * AH), "norm2_g": (D,),
    "w_up": (D, 2 * FH), "conv_w": (3, FH), "conv_b": (FH,), "w_down": (FH, D), "normf_g": (D,),
}
_OUTS = {
    "y_prompt": ((TP, D), (1, TP, D)), "y_sample": ((NS, D), (NS, 1, D)),
    "gla_p": ((GH, GDK, GDV), (1, 1, GH, GDK, GDV)), "gla_s": ((NS, GH, GDK, GDV), (1, NS, GH, GDK, GDV)),
    "win1_p": ((P, 2 * AG), (1, 1, P, 2, AH, AE)), "win1_s": ((NS, WIN[0], 2 * AG), (1, NS, WIN[0], 2, AH, AE)),
    "win2_p": ((TP, 2 * AG), (1, 1, TP, 2, AH, AE)), "win2_s": ((NS, WIN[1], 2 * AG), (1, NS, WIN[1], 2, AH, AE)),
    "win3_p": ((TP, 2 * AG), (1, 1, TP, 2, AH, AE)), "win3_s": ((NS, WIN[2], 2 * AG), (1, NS, WIN[2], 2, AH, AE)),
    "conv_p": ((2, FH), (1, 1, 2, FH)), "conv_s": ((NS, 2, FH), (1, NS, 2, FH)),
}


def kernel(**inputs):
    import numpy as _np
    import concourse.bacc as _bacc
    from concourse.bass_utils import run_bass_kernel_spmd as _run

    nc = _bacc.Bacc("TRN2", target_bir_lowering=False, num_devices=1)
    arrays, w, con, o = {}, {}, {}, {}
    for name, shape in _INS.items():
        arrays[f"in_{name}"] = _np.ascontiguousarray(_np.asarray(inputs[name]).reshape(shape))
        w[name] = nc.dram_tensor(f"in_{name}", shape, F32, kind="ExternalInput").ap()
    for name, a in constants().items():
        arrays[f"in_{name}"] = a
        con[name] = nc.dram_tensor(f"in_{name}", a.shape, F32, kind="ExternalInput").ap()
    for name, (shape, _) in _OUTS.items():
        o[name] = nc.dram_tensor(f"out_{name}", shape, F32, kind="ExternalOutput").ap()
    program(nc, w, o, con)
    r = _run(nc, [arrays], core_ids=[0])
    return tuple(r.results[0][f"out_{name}"].reshape(full) for name, (_, full) in _OUTS.items())
```

```python
import concourse.bass as bass
from concourse import mybir
from contextlib import ExitStack
import numpy as np

F32 = mybir.dt.float32
R32 = mybir.dt.float32r
ACT = mybir.ActivationFunctionType
ALU = mybir.AluOpType
AX = mybir.AxisListType

P = 128
D = 1024
KD = D // P
TP = 512
NS = 8
T = TP + NS
HT = T // 2
NC = 1 + NS
GH, GDK, GDV = 4, 128, 256
GR = 16
CH = 64
NCH = TP // CH
AH, AE = 8, 64
NG = 3
AG = AH * AE
FH = 2816
KF = FH // P
EPS = 1e-6
UW = 16 * P
NEG = -1e30
BND = AE + 2
BW = 384
SK = P + 1
WIN = (128, 512, 1024)
DIL = (1, 4, 16)
SCALE = AE ** -0.5

C_GQ, C_GK, C_GV, C_GR, C_LR = 0, 512, 1024, 2048, 3072
C_AQ = C_LR + GR
C_AK = C_AQ + NG * AG
C_AV = C_AK + NG * AG
C_GA = C_AV + NG * AG
C_GB = C_GA + D

COLS = dict(gq=C_GQ, gk=C_GK, gv=C_GV, gr=C_GR, aq=C_AQ, ak=C_AK, av=C_AV, ga=C_GA, gb=C_GB)
SPILL = dict(gr=0, ga=KD, gb=2 * KD)

V_N1, V_N2, V_NF, V_GN, V_BA = 0, KD, 2 * KD, 3 * KD, 3 * KD + 2
NV1 = V_BA + 6 * KD
V_CB, V_CW = NV1, NV1 + KF
NV2 = 4 * KF


def up_sources(w, col):
    v = w["w_up"].rearrange("(k p) n -> p k n", p=P)
    return [(i * KD, v[:, :, bass.ds(FH * i + col, P)]) for i in range(2)]


def down_sources(w, half, col):
    v = w["w_down"].rearrange("(k p) n -> p k n", p=P)
    k0, k1, k2 = (half * (KF // 2) + k for k in (0, 6, KF // 2))
    return [(0, v[:, k0:k1, bass.ds(col, P)]), (6, v[:, k1:k2, bass.ds(col, P)])]


def stream(w):
    out = []

    def cols(kind, src, c0, m, kt=KD):
        v = src[0:kt * P, c0:c0 + m * P].rearrange("(k p) n -> p k n", p=P)
        out.append(dict(kind=kind, src=[(0, v)], kt=kt, mt=m, block=lambda k, j: k * m + j))

    def ada(u):
        cols("ada", w["w_ada"], 256 * u, 2)

    def add(names, phase):
        for name in names.split():
            first = 2 * taken.get(name, 0)
            taken[name] = taken.get(name, 0) + 1
            kind = name.rstrip("012")
            col = COLS[kind] + (AG * int(name[2]) if kind in ("aq", "ak", "av") else 0)
            cols(name, w["w_in"], col + P * first, 2)
            out[-1]["m0"] = first + {"ak": 4, "av": 8}.get(kind, 0)
            out[-1]["phase"] = phase

    taken = {}
    for u in range(8):
        ada(u)
    cols("lr", w["w_in"], C_LR, 1)
    for u, name in enumerate(("gk", "gk", "gq", "gq", "gv", "gv", "gv", "gv")):
        add(name, "gla_in")
        ada(8 + u)
    add("aq0 gr aq0 gr ak0 gr ak0 gr av0 ga av0", "gla")
    add("aq1 aq1 ga ak1 ga ak1 av1 ga av1", "att0")
    add("aq2 aq2 ak2 ak2 av2 av2", "att1")
    add("gb gb gb gb", "att2")
    late = list(range(16, 23))
    for kind, src, n in (("bb", "w_branch_b", 2), ("ba", "w_branch_a", 4), ("wo", "w_out", 4)):
        for u in range(n):
            if kind == "bb":
                cols(kind, w[src], 512 * u, 4, kt=4)
            else:
                cols(kind, w[src], 256 * u, 2)
            if late:
                ada(late.pop(0))
    ada(23)
    for u in range(KF):
        out.append(dict(kind="up", src=up_sources(w, u * P), kt=KD, mt=2, block=lambda k, j: KD * j + k))
    for m in range(KD):
        for half in range(2):
            out.append(dict(kind="dn", src=down_sources(w, half, m * P), kt=KF // 2, mt=1, half=half,
                            block=lambda k, j: k))
    n = {"mm": 0, "ada": 0}
    tile = done = 0
    arrived = [0, 0]
    for u, x in enumerate(out):
        sort = "ada" if x["kind"] == "ada" else "mm"
        x["i"] = n[sort]
        n[sort] += 1
        arrived[u % 2] += 16 * len(x["src"])
        x["arrived"] = arrived[u % 2]
        x["words"] = x["kt"] * x["mt"] * P
        x["tile0"], x["pass0"] = tile, done
        if sort == "mm":
            done += x["mt"]
            tile += 0 if x.get("half") == 0 else x["mt"]
    return out


def program(nc, w, o, con):
    U = stream(w)
    MM = [u for u, x in enumerate(U) if x["kind"] != "ada"]
    ADA = [u for u, x in enumerate(U) if x["kind"] == "ada"]
    LAST = {"ba": "dve", "wo": "dve", "up": "dve", "dn": "dve"}
    owner, freed, passes = [], [], []
    count = {"act": 0, "dve": 0}
    for u in MM:
        x = U[u]
        if x.get("half") == 0:
            continue
        for m in range(x["mt"]):
            who = LAST.get(x["kind"], "act") if not (x["kind"] == "up" and m == 0) else "act"
            count[who] += 1
            owner.append(who)
            freed.append(count[who])
            passes.append(x["pass0"] + m + 1)

    def units(kind):
        return [u for u, x in enumerate(U) if x["kind"] == kind]

    ctx = ExitStack()
    with ctx:
        def sb(name, shape, dt=F32):
            return ctx.enter_context(nc.sbuf_tensor(name, shape, dt))

        def sem(name):
            return ctx.enter_context(nc.semaphore(name))

        actH = sb("actH", [P, KD, T], R32)
        actL = sb("actL", [P, KD, T], R32)
        wraw = sb("wraw", [P, 2, UW])
        whi = sb("whi", [P, 2, UW], R32)
        wlo = sb("wlo", [P, 2, UW], R32)
        cst = sb("cst", [P, 5 * P])
        mod = sb("mod", [P, 6 * KD, NC])
        vec = sb("vec", [P, NV1 + NV2])
        stT = sb("stT", [P, KF, NS * 2])
        modA = sb("modA", [P, KD, NC])
        scT = sb("scT", [P, NC * KD])
        ident, tri, gmask, flip, ones = (cst[:, P * i:P * i + P] for i in range(5))
        AW = 30720
        FX = 2 * KF * T
        FT = FX + KD * T
        with ExitStack() as e:
            e.enter_context(nc.sbuf_tensor("below_a2", [P, KD * T], F32))
            a2H = e.enter_context(nc.sbuf_tensor("a2H", [P, KD, T], R32))
            a2L = e.enter_context(nc.sbuf_tensor("a2L", [P, KD, T], R32))
            b2H = e.enter_context(nc.sbuf_tensor("b2H", [P, 4, T], R32))
            b2L = e.enter_context(nc.sbuf_tensor("b2L", [P, 4, T], R32))
        with ExitStack() as e:
            gH = e.enter_context(nc.sbuf_tensor("gH", [P, KF, T], R32))
            gL = e.enter_context(nc.sbuf_tensor("gL", [P, KF, T], R32))
        arena = sb("arena", [P, AW])
        ps = ctx.enter_context(nc.psum_tensor("ps", [P, 8, 512], F32))

        def at(off, *shape, parts=P):
            n = int(np.prod(shape))
            assert off + n <= AW, (off, shape)
            v = arena[0:parts, off:off + n]
            if len(shape) == 2:
                v = v.rearrange("p (a b) -> p a b", b=shape[1])
            return v

        def norm_temps(off, modulated=True):
            tmp = dict(sq=at(off, 2, T), v=at(off + 2 * T, T), y=at(off + 3 * T, T), t=at(off + 4 * T, T),
                       r=at(off + 5 * T, T))
            return dict(tmp, hf=at(off + 6 * T, 2, T)) if modulated else tmp

        def dram(name, *shape):
            return nc.dram_tensor(name, shape, F32, kind="Internal").ap()

        xd = dram("x_feature_major", P, KD * T)
        rawd = dram("raw_gates", P, 3 * KD * T)
        od = dram("gla_out", P, KD * T)
        bd = dram("bias_by_distance", NG * AH, BW)
        gd = dram("group_out", NG, TP, AH * BND)

        w_dma = [sem("w_dma0"), sem("w_dma1")]
        hi_ready, lo_ready, pass_done = sem("hi_ready"), sem("lo_ready"), sem("pass_done")
        ada_done, ada_tok, ada_turned, ada_read = (sem(n) for n in ("ada_done", "ada_tok", "ada_turned", "ada_read"))
        tile_read = {"act": sem("tile_read_act"), "dve": sem("tile_read_dve")}
        outs, caches_moved = sem("outs"), sem("caches_moved")
        n_outs = [0]
        S = {}

        def s(name):
            if name not in S:
                S[name] = sem(name)
            return S[name]

        class Chain:

            def __init__(self, name):
                self.sem, self.n = sem(name), 0

            def link(self, eng, ins):
                self.n += 1
                ins.then_inc(self.sem, 1)
                eng.wait_ge(self.sem, self.n)

        dch, ach = Chain("dve_chain"), Chain("act_chain")

        spill_order = [(u, m) for u, x in enumerate(U) if x["kind"] in SPILL for m in range(2)]
        spill = at(29448, 2, T)

        moves = [(o["conv_s"][:, 0, :], w["state_conv"][:, 1, :])]
        for g in range(NG):
            pieces = 2 if g == 2 else 1
            for b in range(NS):
                n = (WIN[g] - 1) * D // P
                src = w[f"cache_win{g + 1}"][b].rearrange("t n -> (t n)")[D:WIN[g] * D].rearrange("(p n) -> p n", n=n)
                dst = o[f"win{g + 1}_s"][b].rearrange("t n -> (t n)")[0:(WIN[g] - 1) * D].rearrange("(p n) -> p n", n=n)
                for i in range(pieces):
                    r = slice(P // pieces * i, P // pieces * (i + 1))
                    moves.append((dst[r], src[r]))
        n_moved = [0]

        def move_cache(act):
            if n_moved[0] < len(moves):
                act.dma_start(*moves[n_moved[0]]).then_inc(caches_moved, 16)
                n_moved[0] += 1

        def issue(sp, u):
            if u >= len(U):
                return
            x = U[u]
            if u >= 2:
                y = U[u - 2]
                sp.wait_ge(ada_done if y["kind"] == "ada" else lo_ready, y["i"] + 1)
            load(sp, u % 2, x["src"])

        def issue_all(sp, u0, u1):
            u = u0
            while u < u1:
                if U[u]["kind"] == "ada" and U[u + 1]["kind"] != "ada":
                    assert u + 1 < u1
                    issue(sp, u + 1)
                    issue(sp, u)
                    u += 2
                else:
                    issue(sp, u)
                    u += 1

        def load(sp, slot, sources):
            for block, src in sources:
                k, n = src.shape[1], src.shape[2]
                dst = wraw[:, slot, P * block:P * block + k * n].rearrange("p (k n) -> p k n", k=k)
                sp.dma_start(dst, src).then_inc(w_dma[slot], 16)

        def split_hi(act, v, part=0, parts=1):
            if v >= len(MM):
                return
            u = MM[v]
            if part == 0:
                act.wait_ge(w_dma[u % 2], U[u]["arrived"])
                if v >= 2:
                    y = U[MM[v - 2]]
                    act.wait_ge(pass_done, y["pass0"] + y["mt"])
            n = U[u]["words"] // parts
            c = slice(n * part, n * part + n)
            ins = act.activation(whi[:, v % 2, c], wraw[:, u % 2, c], ACT.Copy)
            if part == parts - 1:
                ins.then_inc(hi_ready, 1)

        def split_lo(dve, v, part=0, parts=1):
            if v >= len(MM):
                return
            u = MM[v]
            n = U[u]["words"] // parts
            c = slice(n * part, n * part + n)
            if part == 0:
                dve.wait_ge(hi_ready, v + 1)
            ins = dve.tensor_tensor(wlo[:, v % 2, c], wraw[:, u % 2, c], whi[:, v % 2, c].bitcast(F32), ALU.subtract)
            if part == parts - 1:
                ins.then_inc(lo_ready, 1)

        def banks(n):
            return ps[:, 2 * (n % 2):2 * (n % 2) + 2, 0:HT]

        def halves(v):
            return v.rearrange("p (a b) -> p a b", a=2)

        def three_pass(pe, n, slot, blocks, H, L, k0=0, begin=True, end=True):
            last = None
            for j, b in enumerate(blocks):
                hi, lo = whi[:, slot, b * P:b * P + P], wlo[:, slot, b * P:b * P + P]
                for a, wt, X in ((0, hi, H), (1, hi, H), (0, hi, L), (1, hi, L), (0, lo, H), (1, lo, H)):
                    last = pe.matmul(ps[:, 2 * (n % 2) + a, 0:HT], wt, X[:, k0 + j, a * HT:a * HT + HT],
                                     start=begin and j == 0 and wt is hi and X is H,
                                     stop=end and j == len(blocks) - 1 and wt is lo)
            return last

        def multiply(pe, u, H, L, between=None, arriving=None):
            x = U[u]
            pe.wait_ge(lo_ready, x["i"] + 1)
            for m in range(x["mt"]):
                n = x["tile0"] + m
                if n >= 2:
                    pe.wait_ge(tile_read[owner[n - 2]], freed[n - 2])
                parts = between.parts if between else 1
                for part in range(parts):
                    kn = x["kt"] // parts
                    for k in range(kn * part, kn * part + kn):
                        if arriving and m == 0:
                            pe.wait_ge(arriving[0], arriving[1] + k + 1)
                        last = three_pass(pe, n, x["i"] % 2, [x["block"](k, m)], H, L, k0=k, begin=k == 0,
                                          end=k == x["kt"] - 1)
                    if part == parts - 1:
                        last.then_inc(pass_done, 1)
                    if between:
                        between()

        def copy_tiles(act, u, dst, m0, between=None):
            x = U[u]
            fine = between and between.fine
            if not fine:
                split_hi(act, x["i"] + 1)
            for m in range(x["mt"]):
                n = x["tile0"] + m
                if between:
                    for part in range(between.parts):
                        if m == 0 and fine:
                            split_hi(act, x["i"] + 1, part, between.parts)
                        if part < between.parts - 1:
                            between()
                act.wait_ge(pass_done, passes[n])
                if x["kind"] in SPILL:
                    r = spill_order.index((u, m))
                    if r >= 2:
                        act.wait_ge(s(f"spill_out{r % 2}"), 16 * (r // 2))
                    to = spill[:, r % 2, :]
                else:
                    to = dst[:, m0 + m, :]
                act.activation(halves(to), banks(n), ACT.Copy).then_inc(tile_read["act"], 1)
                if between:
                    between()

        def store_spilled(sp, u):
            x = U[u]
            if x["kind"] not in SPILL:
                return
            for m in range(x["mt"]):
                r = spill_order.index((u, m))
                q = SPILL[x["kind"]] + x["m0"] + m
                sp.wait_ge(tile_read["act"], freed[x["tile0"] + m])
                sp.dma_start(rawd[:, T * q:T * q + T], spill[:, r % 2, :]).then_inc(s(f"spill_out{r % 2}"), 16)

        class Between:

            def __init__(self, work, steps, units, fine=False):
                self.fine, self.parts = fine, 4 if fine else 2
                self.work, self.steps, self.places = work, steps, 2 * self.parts * len(units)
                self.place = self.done = 0

            def __call__(self):
                self.place += 1
                while self.done < -(-self.steps * self.place // self.places):
                    next(self.work)
                    self.done += 1

            def finish(self):
                assert self.done == self.steps and next(self.work, None) is None

        def stream_pe(pe, us, work, steps, fine=False):
            between = Between(work, steps, us, fine)
            for u in us:
                multiply(pe, u, actH, actL, between)
            between.finish()

        def stream_act(act, us, dst, work, steps, fine=False):
            between = Between(work, steps, us, fine)
            for u in us:
                move_cache(act)
                copy_tiles(act, u, dst, U[u]["m0"], between)
            between.finish()

        def split_between(dve, u, between):
            if not between.fine:
                split_lo(dve, U[u]["i"] + 1)
            for place in range(2 * between.parts):
                piece = place - between.parts + 1
                if between.fine and 0 <= piece < between.parts:
                    split_lo(dve, U[u]["i"] + 1, piece, between.parts)
                between()

        def stream_dve(dve, us, work, steps, fine=False):
            between = Between(work, steps, us, fine)
            for u in us:
                split_between(dve, u, between)
            between.finish()

        def stream_sp(sp, us):
            for u in us:
                issue(sp, u + 3)
                store_spilled(sp, u)

        def wait_copied(eng, u):
            n = U[u]["tile0"] + U[u]["mt"] - 1
            eng.wait_ge(tile_read["act"], freed[n])

        def ada_pe(pe, a):
            u = ADA[a]
            pe.wait_ge(w_dma[u % 2], U[u]["arrived"])
            if a >= 1:
                pe.wait_ge(ada_tok, a)
            for k in range(KD):
                last = pe.matmul(ps[0:NC, 7, 0:2 * P], scT[:, k:NC * KD:KD],
                                 wraw[:, u % 2, 2 * k * P:2 * (k + 1) * P], start=k == 0, stop=k == KD - 1)
            last.then_inc(ada_done, 1)

        def ada_turn_pe(pe, a, rows):
            pe.wait_ge(ada_tok, a + 1)
            if a >= 1:
                pe.wait_ge(ada_read, a)
            for m in range(2):
                last = pe.transpose(ps[:, 6, 480 + NC * m:480 + NC * m + NC], rows[:, a % 2, P * m:P * m + P],
                                    ident[0:NC, 0:NC])
            last.then_inc(ada_turned, 1)

        def ada_dve(dve, a, rows):
            dve.wait_ge(ada_done, a + 1)
            if a >= 2:
                dve.wait_ge(ada_turned, a - 1)
            dve.tensor_copy(rows[:, a % 2, :], ps[0:NC, 7, 0:2 * P]).then_inc(ada_tok, 1)

        def ada_turn_dve(dve, a):
            dve.wait_ge(ada_turned, a + 1)
            dve.tensor_tensor(mod[:, 2 * a:2 * a + 2, :],
                              ps[:, 6, 480:480 + 2 * NC].rearrange("p (m c) -> p m c", m=2),
                              vec[:, V_BA + 2 * a:V_BA + 2 * a + 2].unsqueeze(2).to_broadcast([P, 2, NC]),
                              ALU.add).then_inc(ada_read, 1)

        def norm_pe(pe, i, tmp):
            pe.wait_ge(s("sq_added"), (KD - 1) * (i + 1))
            for a in range(2):
                last = pe.matmul(ps[:, 4 + a, 0:HT], ones, tmp["t"][:, a * HT:a * HT + HT], start=True, stop=True)
            last.then_inc(s("sq_summed"), 1)

        def newton(dve, v, y, t, r):
            dch.link(dve, dve.tensor_tensor(t, y, y, ALU.mult))
            dch.link(dve, dve.scalar_tensor_tensor(t, t, -0.5, v, ALU.mult, ALU.mult))
            return dve.scalar_tensor_tensor(r, t, 1.5, y, ALU.add, ALU.mult)

        def square_act(act, i, k, X, tmp):
            if k >= 2:
                act.wait_ge(s("sq_added"), (KD - 1) * i + max(1, k - 2))
            act.activation(tmp["sq"][:, k % 2, :], X[:, k, :], ACT.Square).then_inc(s("sq_ready"), 1)

        def square_dve(dve, i, k, tmp):
            if k < 1:
                return
            dve.wait_ge(s("sq_ready"), KD * i + k + 1)
            if k >= 2:
                dve.wait_ge(s("sq_added"), (KD - 1) * i + k - 1)
            dve.tensor_tensor(tmp["t"], tmp["sq"][:, 0, :] if k == 1 else tmp["t"], tmp["sq"][:, k % 2, :], ALU.add)\
               .then_inc(s("sq_added"), 1)

        def rstd_dve(dve, i, tmp):
            dve.wait_ge(s("sq_summed"), i + 1)
            dve.tensor_scalar(halves(tmp["v"]), ps[:, 4:6, 0:HT], 1.0 / D, EPS, ALU.mult, ALU.add)\
               .then_inc(s("ms_ready"), 1)
            dve.wait_ge(s("rs_ready"), i + 1)
            dch.link(dve, newton(dve, tmp["v"], tmp["y"], tmp["t"], tmp["r"]))

        def norm_act(act, i, tmp):
            act.wait_ge(s("ms_ready"), i + 1)
            ach.link(act, act.activation(tmp["y"], tmp["v"], ACT.Ln))
            act.activation(tmp["y"], tmp["y"], ACT.Exp, scale=-0.5).then_inc(s("rs_ready"), 1)

        def modulate_dve(dve, i, X, tmp, gcol, shift, scale):
            g = vec[:, gcol:gcol + KD].unsqueeze(2).to_broadcast([P, KD, NC])
            dch.link(dve, dve.scalar_tensor_tensor(modA[:, :, :], mod[:, scale:scale + KD, :], 1.0, g, ALU.add, ALU.mult))

            def low(k):
                dve.wait_ge(s("h_hi"), KD * i + k + 1)
                dve.tensor_tensor(actL[:, k, :], tmp["hf"][:, k % 2, :], actH[:, k, :].bitcast(F32), ALU.subtract)\
                   .then_inc(s("h_split"), 1)

            for k in range(KD):
                h = tmp["hf"][:, k % 2, :]
                if k >= 2:
                    dve.wait_ge(s("h_split"), KD * i + k - 1)
                dve.tensor_tensor(h, X[:, k, :], tmp["r"], ALU.mult).then_inc(s("h_normed"), 1)
                dve.wait_ge(s("h_normed"), KD * i + k + 1)
                dch.link(dve, dve.tensor_tensor(h[:, TP:T], h[:, TP:T], modA[:, k, 1:NC], ALU.mult))
                dve.tensor_tensor(h[:, TP:T], h[:, TP:T], mod[:, shift + k, 1:NC], ALU.add).then_inc(s("h_ready"), 1)
                if k >= 1:
                    low(k - 1)
            low(KD - 1)

        def modulate_act(act, i, tmp, shift):
            for k in range(KD):
                h = tmp["hf"][:, k % 2, :]
                act.wait_ge(s("h_normed"), KD * i + k + 1)
                ach.link(act, act.activation(h[:, 0:TP], h[:, 0:TP], ACT.Identity, scale=modA[:, k, 0:1],
                                             bias=mod[:, shift + k, 0:1]))
                act.wait_ge(s("h_ready"), KD * i + k + 1)
                act.activation(actH[:, k, :], h, ACT.Copy).then_inc(s("h_hi"), 1)

        xT1 = at(0, KD, T)
        xin = at(4160, 4, D)
        n1 = norm_temps(8256)
        csrow = at(12416, FH, parts=2 * NS)
        crow = at(15232, P, parts=NC * KD)
        v1row = at(15360, P, parts=NV1)
        v2row = at(15488, P, parts=NV2)
        xsin = at(15616, D, parts=NS)
        sig1 = at(16640, NC * KD)
        ada1 = at(16800, 2, 2 * P, parts=NC)

        with nc.Block() as block:
            @block.sync
            def _(sp):
                sp.dma_start(cst[:, 0:4 * P], con["cst"]).then_inc(s("early_in"), 16)
                sp.dma_start(crow[0:KD, :], w["c_prompt"].rearrange("b (k p) -> (b k) p", p=P)).then_inc(s("early_in"), 16)
                sp.dma_start(crow[KD:NC * KD, :], w["c_sample"].rearrange("b (k p) -> (b k) p", p=P)).then_inc(s("early_in"), 16)
                for name, r0, n in (("norm1_g", V_N1, KD), ("norm2_g", V_N2, KD), ("normf_g", V_NF, KD),
                                    ("gla_norm_g", V_GN, 2), ("b_ada", V_BA, 6 * KD)):
                    sp.dma_start(v1row[r0:r0 + n, :], w[name].rearrange("(k p) -> k p", p=P)).then_inc(s("early_in"), 16)
                issue(sp, 0)
                issue(sp, 1)
                for u in range(2, 8 + 2):
                    issue(sp, u)
                sp.wait_ge(s("x_all"), 1)
                sp.wait_ge(s("x_evac"), KD)
                sp.dma_start(xd, xT1.rearrange("p k t -> p (k t)")).then_inc(s("x_spilled"), 16)

            @block.gpsimd
            def _(pool):
                for t in range(4):
                    pool.dma_start(xin[:, t, :], w["x_prompt"][P * t:P * t + P, :]).then_inc(s("x_in"), 16)
                pool.dma_start(xsin, w["x_sample"]).then_inc(s("x_in"), 16)
                pool.dma_start(v2row[0:KF, :], w["conv_b"].rearrange("(k p) -> k p", p=P)).then_inc(s("late_in"), 16)
                pool.dma_start(v2row[KF:NV2, :], w["conv_w"].rearrange("j (k p) -> (j k) p", p=P)).then_inc(s("late_in"), 16)
                pool.dma_start(csrow, w["state_conv"].rearrange("b j n -> (b j) n")).then_inc(s("late_in"), 16)

            @block.scalar
            def _(act):
                act.wait_ge(s("prep_T"), 1)
                act.activation(sig1, ps[:, 4, 0:NC * KD], ACT.Sigmoid).then_inc(s("c_sig"), 1)
                for k in range(KD):
                    act.wait_ge(s("x_T"), k + 1)
                    act.activation(xT1[:, k, 0:TP], ps[:, k % 4, :], ACT.Copy).then_inc(s("x_evac"), 1)
                    if k == 1:
                        act.wait_ge(s("prep_T"), 3)
                        act.activation(xT1[:, :, TP:T], ps[:, 5, 0:NS * KD].rearrange("p (k b) -> p k b", b=NS), ACT.Copy)\
                           .then_inc(s("x_all"), 1)
                act.wait_ge(s("x_all"), 1)
                act.wait_ge(s("x_evac"), KD)
                for k in range(KD):
                    square_act(act, 0, k, xT1, n1)
                norm_act(act, 0, n1)
                split_hi(act, 0)

            @block.vector
            def _(dve):
                dve.memset(ones, 1.0)
                dve.wait_ge(s("c_sig"), 1)
                dve.tensor_tensor(scT[:, :], ps[:, 4, 0:NC * KD], sig1, ALU.mult).then_inc(s("c_silu"), 1)
                dve.wait_ge(s("prep_T"), 2)
                dve.tensor_copy(vec[:, 0:NV1], ps[:, 6, 0:NV1]).then_inc(s("vec_ready"), 1)
                dve.wait_ge(s("vec_ready"), 1)
                for a in range(8):
                    ada_dve(dve, a, ada1)
                    if a >= 1:
                        ada_turn_dve(dve, a - 1)
                    if a == 3:
                        dve.wait_ge(s("prep_T"), 4)
                        dve.tensor_copy(vec[:, NV1:NV1 + NV2], ps[:, 4, NV1:NV1 + NV2])
                        dve.wait_ge(s("prep_T"), 5)
                        dve.tensor_copy(stT[:, :, :], ps[:, 5, 0:KF * 16].rearrange("p (k b) -> p k b", b=16))\
                           .then_inc(s("vec_ready"), 1)
                    if a == 4:
                        for k in range(KD):
                            square_dve(dve, 0, k, n1)
                    if a == 6:
                        rstd_dve(dve, 0, n1)
                ada_turn_dve(dve, 7)
                split_lo(dve, 0)

            @block.tensor
            def _(pe):
                pe.wait_ge(s("early_in"), 128)
                pe.transpose(ps[:, 4, 0:NC * KD], crow, ident[0:NC * KD, 0:NC * KD]).then_inc(s("prep_T"), 1)
                pe.transpose(ps[:, 6, 0:NV1], v1row, ident[0:NV1, 0:NV1]).then_inc(s("prep_T"), 1)
                pe.wait_ge(s("c_silu"), 1)
                for a in range(8):
                    ada_pe(pe, a)
                    if a >= 1:
                        if a == 1:
                            pe.wait_ge(s("vec_ready"), 1)
                        ada_turn_pe(pe, a - 1, ada1)
                    if a < 4:
                        for k in (2 * a, 2 * a + 1):
                            if k >= 4:
                                pe.wait_ge(s("x_evac"), k - 3)
                            for t in range(4):
                                if k == 0 and t == 0:
                                    pe.wait_ge(s("x_in"), 80)
                                last = pe.transpose(ps[:, k % 4, P * t:P * t + P], xin[:, t, P * k:P * k + P], ident)
                            last.then_inc(s("x_T"), 1)
                    if a == 0:
                        for k in range(KD):
                            last = pe.transpose(ps[:, 5, NS * k:NS * k + NS], xsin[:, P * k:P * k + P], ident[0:NS, 0:NS])
                        last.then_inc(s("prep_T"), 1)
                    if a == 3:
                        pe.wait_ge(s("late_in"), 48)
                        pe.wait_ge(s("x_all"), 1)
                        pe.transpose(ps[:, 4, NV1:NV1 + NV2], v2row, ident[0:NV2, 0:NV2]).then_inc(s("prep_T"), 1)
                        for k in range(KF):
                            last = pe.transpose(ps[:, 5, 16 * k:16 * k + 16], csrow[:, P * k:P * k + P], ident[0:16, 0:16])
                        last.then_inc(s("prep_T"), 1)
                    if a == 5:
                        pe.wait_ge(s("vec_ready"), 2)
                        norm_pe(pe, 0, n1)
                ada_turn_pe(pe, 7, ada1)

        gk, gq, gv = at(0, 4, T), at(2080, 4, T), at(4160, KD, T)
        vtok = at(10400, 4, D)
        oT2 = at(14496, KD, T)
        gtok = at(18656, 4, 512)
        Bt, X1, X2, X3, X4, X5, kdtok, aTm = (at(20704 + 512 * i, 512) for i in range(8))
        Sall = at(24800, 8, GDV)
        sq2 = at(21216, 2, 512)
        ktS, vtS = at(26848, 512, parts=NS), at(27360, D, parts=NS)
        ebS = at(28384, 4, NS)
        ada2 = at(22240, 2, 2 * P, parts=NC)
        lrT = at(28416, T)
        wg2 = at(28936, 512, parts=GR + 1)
        za, zb = Bt, X1
        Sring = at(18656, 2, 4 * GDV)
        kmask = at(10400, 2, 512, parts=NS)
        qS, gS, oS = at(20704, 4, NS), at(20736, 4 * NS), at(20768, 8, NS)
        sqS, rsS, rsT, rsV, rsR = at(20832, 8, NS), at(20896, 4 * NS), at(20928, 4 * NS), at(20960, 4 * NS), at(20992, 4 * NS)
        QSC = GDK ** -0.5
        U_K, U_Q, U_V, U_LR = units("gk"), units("gq"), units("gv"), units("lr")
        AQKV = [at(4160, 12, T), at(10400, 12, T)]

        def update_bank(c):
            return ps[:, 4 + 2 * (c % 2) + c // 4, GDV * (c // 2 % 2):GDV * (c // 2 % 2) + GDV]

        def phase(name):
            return [u for u, x in enumerate(U) if x.get("phase") == name]

        def logsig_act(act, z, ta, tb, name, i):
            ach.link(act, act.activation(ta, z, ACT.Abs))
            ach.link(act, act.activation(ta, ta, ACT.Exp, scale=-1.0))
            act.activation(tb, ta, ACT.Ln, bias=1.0).then_inc(s(name), 1)

        GLA_IN, GLA = phase("gla_in"), phase("gla")
        DESTS = {"gk": gk, "gq": gq, "gv": gv}
        V_TILE0 = U[U_V[0]]["tile0"]
        V_LAG = 19
        IN_STEPS = 4 * len(GLA_IN)
        GLA_STEPS = 1 + 7 * GH + 2 + NS + 2

        def v_pe(pe, m):
            if m == 0:
                pe.wait_ge(s("g_ready"), 4)
            if m >= 2:
                pe.wait_ge(s("v_tok"), m - 1)
            pe.wait_ge(tile_read["act"], freed[V_TILE0 + m])
            for t in range(4):
                last = pe.transpose(ps[:, 4 + m % 2, P * t:P * t + P], gv[:, m, P * t:P * t + P], ident)
            last.then_inc(s("v_T"), 1)

        def v_act(act, m):
            act.wait_ge(s("v_T"), m + 1)
            act.activation(vtok[:, :, P * m:P * m + P], ps[:, 4 + m % 2, :].rearrange("p (t i) -> p t i", t=4), ACT.Copy)\
               .then_inc(s("v_tok"), 1)

        def gla_in_pe(pe):
            for p in range(IN_STEPS):
                if p == 0:
                    pe.wait_ge(s("wg2_in"), 32)
                    wait_copied(pe, U_LR[0])
                if p < 4:
                    if p >= 2:
                        pe.wait_ge(s("g_ready"), p - 1)
                    pe.matmul(ps[:, 4 + p % 2, :], lrT[0:GR + 1, P * p:P * p + P], wg2, start=True, stop=True)\
                      .then_inc(s("z_ready"), 1)
                elif p >= V_LAG and p % 2 == V_LAG % 2:
                    v_pe(pe, (p - V_LAG) // 2)
                yield

        def gla_in_act(act):
            for p in range(IN_STEPS):
                if p < 4:
                    act.wait_ge(s("z_ready"), p + 1)
                    if p >= 1:
                        act.wait_ge(s("g_ready"), p)
                    logsig_act(act, ps[:, 4 + p % 2, :], za, zb, "ln_ready", p)
                elif p >= V_LAG and p % 2 == V_LAG % 2:
                    v_act(act, (p - V_LAG) // 2)
                yield

        def gla_in_dve(dve):
            for p in range(IN_STEPS):
                if p < 4:
                    dve.wait_ge(s("ln_ready"), p + 1)
                    dve.scalar_tensor_tensor(gtok[:, p, :], ps[:, 4 + p % 2, :], 0.0, zb, ALU.min, ALU.subtract)\
                       .then_inc(s("g_ready"), 1)
                yield

        def gla_pe(pe):
            v_pe(pe, KD - 1)
            pe.wait_ge(s("v_tok"), KD - 1)
            pe.wait_ge(ada_read, 16)
            for m in range(4):
                last = pe.transpose(ps[0:NS, 4, P * m:P * m + P], gk[:, m, TP:T], ident)
            for m in range(KD):
                last = pe.transpose(ps[0:NS, 6 + m // 4, P * (m % 4):P * (m % 4) + P], gv[:, m, TP:T], ident)
            last.then_inc(s("kvs_T"), 1)
            yield
            for h in range(GH):
                if h == 0:
                    pe.wait_ge(s("kvs"), 1)
                else:
                    pe.wait_ge(s("o_v"), h)
                    pe.wait_ge(s("o_sq"), h)
                for t in range(4):
                    last = pe.matmul(ps[:, 4, P * t:P * t + P], gtok[:, t, GDK * h:GDK * h + GDK], tri, start=True, stop=True)
                last.then_inc(s("B_ready"), 1)
                for _ in range(3):
                    yield
                pe.wait_ge(s("kd"), h + 1)
                for t in range(4):
                    last = pe.transpose(ps[:, 6, P * t:P * t + P], X4[:, P * t:P * t + P], ident)
                last.then_inc(s("kd_T"), 1)
                pe.wait_ge(s("qe"), h + 1)
                for t in range(4):
                    last = pe.matmul(ps[:, 5, P * t:P * t + P], X2[:, P * t:P * t + P], X1[:, P * t:P * t + P],
                                     start=True, stop=True)
                last.then_inc(s("A_ready"), 1)
                yield
                pe.wait_ge(s("kd_tok"), h + 1)
                pe.wait_ge(s("aT"), h + 1)
                for c in range(NCH):
                    t, r = c // 2, CH * (c % 2)
                    last = pe.matmul(update_bank(c), kdtok[r:r + CH, P * t:P * t + P], vtok[r:r + CH, t, GDV * h:GDV * h + GDV],
                                     start=True, stop=True)
                last.then_inc(s("U_ready"), 1)
                yield
                pe.wait_ge(s("gla_state"), NCH * (h + 1))
                pe.wait_ge(s("qb"), h + 1)
                for vt in range(2):
                    for t in range(4):
                        col = GDV * h + P * vt
                        last = pe.matmul(ps[:, 4 + vt, P * t:P * t + P], vtok[:, t, col:col + P],
                                         aTm[:, P * t:P * t + P], start=True, stop=False)
                        for c in (2 * t, 2 * t + 1):
                            if c >= 1:
                                last = pe.matmul(ps[:, 4 + vt, CH * c:CH * c + CH], Sall[:, c - 1, P * vt:P * vt + P],
                                                 X5[:, CH * c:CH * c + CH], start=False, stop=c % 2 == 1)
                last.then_inc(s("o_ready"), 1)
                yield
                pe.wait_ge(s("o_sq"), h + 1)
                for vt in range(2):
                    last = pe.matmul(ps[:, 6, :], ones, sq2[:, vt, :], start=vt == 0, stop=vt == 1)
                last.then_inc(s("o_summed"), 1)
                yield
            yield
            pe.wait_ge(s("o_done"), GH)
            for h in range(GH):
                last = pe.matmul(ps[:, 4, NS * h:NS * h + NS], wg2[:, GDK * h:GDK * h + GDK], lrT[0:GR + 1, TP:T],
                                 start=True, stop=True)
            last.then_inc(s("z_ready"), 1)
            yield

            def read_out(b):
                pe.wait_ge(s("gs_new"), b + 1)
                for h in range(GH):
                    for vt in range(2):
                        col = (2 * h + vt) * NS + b
                        last = pe.matmul(ps[:, 6, col:col + 1], Sring[:, b % 2, GDV * h + P * vt:GDV * h + P * vt + P],
                                         qS[:, h, b:b + 1], start=True, stop=True)
                last.then_inc(s("gs_read"), 1)

            pe.wait_ge(s("g_ready"), 5)
            for b in range(NS):
                if b >= 1:
                    read_out(b - 1)
                pe.wait_ge(s("kmask"), b + 1)
                for h in range(GH):
                    last = pe.matmul(ps[:, 4 + h // 2, GDV * (h % 2):GDV * (h % 2) + GDV],
                                     kmask[:, b % 2, GDK * h:GDK * h + GDK], vtS[:, GDV * h:GDV * h + GDV],
                                     start=True, stop=True)
                last.then_inc(s("kv_outer"), 1)
                yield
            read_out(NS - 1)
            yield
            pe.wait_ge(s("o_sq"), 5)
            for vt in range(2):
                last = pe.matmul(ps[:, 7, 0:32], ones, sqS[:, vt:KD:2, :], start=vt == 0, stop=vt == 1)
            last.then_inc(s("o_summed"), 1)
            yield

        def gla_act(act):
            v_act(act, KD - 1)
            act.wait_ge(s("kvs_T"), 1)
            ach.link(act, act.activation(ktS, ps[0:NS, 4, :], ACT.Copy))
            act.activation(vtS.rearrange("p (a b) -> p a b", a=2), ps[0:NS, 6:8, :], ACT.Copy).then_inc(s("kvs"), 1)
            yield
            for h in range(GH):
                act.wait_ge(s("b_ready"), 2 * h + 1)
                act.activation(X3, Bt, ACT.Exp)
                act.wait_ge(s("b_ready"), 2 * h + 2)
                act.activation(X2, X1, ACT.Exp, scale=-1.0)
                act.activation(X4, X4, ACT.Exp).then_inc(s("e24"), 1)
                act.activation(X5, X1, ACT.Exp).then_inc(s("e5"), 1)
                for _ in range(3):
                    yield
                act.wait_ge(s("kd_T"), h + 1)
                act.activation(kdtok, ps[:, 6, :], ACT.Copy).then_inc(s("kd_tok"), 1)
                yield
                yield
                act.wait_ge(s("o_ready"), h + 1)
                act.activation(oT2[:, 2 * h:2 * h + 2, 0:TP], ps[:, 4:6, :], ACT.Copy)
                act.activation(sq2, ps[:, 4:6, :], ACT.Square).then_inc(s("o_sq"), 1)
                yield
                act.wait_ge(s("o_v"), h + 1)
                ach.link(act, act.activation(Bt, aTm, ACT.Ln))
                act.activation(Bt, Bt, ACT.Exp, scale=-0.5).then_inc(s("o_rs"), 1)
                yield
            yield
            act.wait_ge(s("z_ready"), 5)
            logsig_act(act, ps[:, 4, 0:32], gS, rsS, "ln_ready", 0)
            act.wait_ge(s("g_ready"), 5)
            act.activation(ebS.rearrange("p h b -> p (h b)"), gS, ACT.Exp, scale=1.0 / 16).then_inc(s("ebs"), 1)
            yield
            for _ in range(NS + 1):
                yield
            act.wait_ge(s("o_v"), 5)
            ach.link(act, act.activation(rsT, rsV, ACT.Ln))
            act.activation(rsT, rsT, ACT.Exp, scale=-0.5).then_inc(s("o_rs"), 1)
            yield

        def gla_dve(dve):
            yield
            for h in range(GH):
                dve.wait_ge(s("B_ready"), h + 1)
                if h >= 1:
                    dve.wait_ge(s("o_done"), h)
                dve.tensor_copy(Bt, ps[:, 4, :]).then_inc(s("b_ready"), 1)
                dve.wait_ge(s("b_ready"), 2 * h + 1)
                B3 = Bt.rearrange("p (c i) -> p c i", i=CH)
                dve.tensor_tensor(X1.rearrange("p (c i) -> p c i", i=CH), B3,
                                  B3[:, :, CH // 2:CH // 2 + 1].to_broadcast([P, NCH, CH]), ALU.subtract)
                dve.tensor_tensor(X4.rearrange("p (c i) -> p c i", i=CH),
                                  B3[:, :, CH - 1:CH].to_broadcast([P, NCH, CH]), B3, ALU.subtract)\
                   .then_inc(s("b_ready"), 1)
                dve.wait_ge(s("e24"), h + 1)
                dve.tensor_tensor(X2, gk[:, h, 0:TP], X2, ALU.mult)
                dve.tensor_tensor(X4, gk[:, h, 0:TP], X4, ALU.mult).then_inc(s("kd"), 1)
                dve.wait_ge(s("e5"), h + 1)
                dve.scalar_tensor_tensor(X1, gq[:, h, 0:TP], QSC, X5, ALU.mult, ALU.mult).then_inc(s("qe"), 1)
                dve.wait_ge(s("qe"), h + 1)
                dve.scalar_tensor_tensor(X5, gq[:, h, 0:TP], QSC, X3, ALU.mult, ALU.mult).then_inc(s("qb"), 1)
                for _ in range(3):
                    yield
                dve.wait_ge(s("A_ready"), h + 1)
                dve.tensor_tensor(aTm.rearrange("p (t i) -> p t i", i=P), ps[:, 5, :].rearrange("p (t i) -> p t i", i=P),
                                  gmask.unsqueeze(1).to_broadcast([P, 4, P]), ALU.mult).then_inc(s("aT"), 1)
                yield
                dve.wait_ge(s("U_ready"), h + 1)
                if h >= 1:
                    dve.wait_ge(s("gla_p_out"), 16 * h)
                for c in range(NCH):
                    add = update_bank(c)
                    if c == 0:
                        ins = dve.tensor_copy(Sall[:, 0, :], add)
                    else:
                        ins = dve.scalar_tensor_tensor(Sall[:, c, :], Sall[:, c - 1, :],
                                                       X3[:, CH * c + CH - 1:CH * c + CH], add, ALU.mult, ALU.add)
                    ins.then_inc(s("gla_state"), 1)
                    dve.wait_ge(s("gla_state"), NCH * h + c + 1)
                yield
                yield
                dve.wait_ge(s("o_summed"), h + 1)
                dve.tensor_scalar(aTm, ps[:, 6, :], 1.0 / GDV, EPS, ALU.mult, ALU.add).then_inc(s("o_v"), 1)
                dve.wait_ge(s("o_rs"), h + 1)
                dch.link(dve, newton(dve, aTm, Bt, X2, X4))
                for vt in range(2):
                    last = dve.scalar_tensor_tensor(oT2[:, 2 * h + vt, 0:TP], oT2[:, 2 * h + vt, 0:TP],
                                                    vec[:, V_GN + vt:V_GN + vt + 1], X4, ALU.mult, ALU.mult)
                last.then_inc(s("o_done"), 1)
                yield
            yield
            dve.wait_ge(s("o_done"), GH)
            dve.tensor_scalar(qS, gq[:, :, TP:T], QSC, None, ALU.mult)
            dve.wait_ge(s("kvs"), 1)
            dve.tensor_scalar(kmask[:, 0, :], ktS, ident[0:NS, 0:1], None, ALU.mult).then_inc(s("kmask"), 1)
            dve.wait_ge(s("ln_ready"), 5)
            dve.scalar_tensor_tensor(gS, ps[:, 4, 0:32], 0.0, rsS, ALU.min, ALU.subtract).then_inc(s("g_ready"), 1)
            yield
            dve.wait_ge(s("ebs"), 1)
            for b in range(NS):
                dve.wait_ge(s("kv_outer"), b + 1)
                if b + 1 < NS:
                    dve.tensor_scalar(kmask[:, (b + 1) % 2, :], ktS, ident[0:NS, b + 1:b + 2], None, ALU.mult)\
                       .then_inc(s("kmask"), 1)
                dve.wait_ge(s(f"gs_in{b % 2}"), 16 * (b // 2 + 1))
                for h in range(GH):
                    st = Sring[:, b % 2, GDV * h:GDV * h + GDV]
                    last = dve.scalar_tensor_tensor(st, st, ebS[:, h, b:b + 1],
                                                    ps[:, 4 + h // 2, GDV * (h % 2):GDV * (h % 2) + GDV], ALU.mult, ALU.add)
                last.then_inc(s("gs_new"), 1)
                yield
            dve.wait_ge(s("gs_read"), NS)
            dch.link(dve, dve.tensor_copy(oS.rearrange("p a b -> p (a b)"), ps[:, 6, 0:64]))
            dve.tensor_tensor(sqS.rearrange("p a b -> p (a b)"), oS.rearrange("p a b -> p (a b)"),
                              oS.rearrange("p a b -> p (a b)"), ALU.mult).then_inc(s("o_sq"), 1)
            yield
            dve.wait_ge(s("o_summed"), 5)
            dve.tensor_scalar(rsV, ps[:, 7, 0:32], 1.0 / GDV, EPS, ALU.mult, ALU.add).then_inc(s("o_v"), 1)
            dve.wait_ge(s("o_rs"), 5)
            dch.link(dve, newton(dve, rsV, rsT, rsS, rsR))
            for vt in range(2):
                last = dve.scalar_tensor_tensor(oT2[:, vt:KD:2, TP:T], oS[:, vt:KD:2, :],
                                                vec[:, V_GN + vt:V_GN + vt + 1],
                                                rsR.rearrange("p (h b) -> p h b", b=NS), ALU.mult, ALU.mult)
            last.then_inc(s("o_all"), 1)
            yield

        with nc.Block() as block:
            @block.sync
            def _(sp):
                issue_all(sp, 10, GLA[0] + 3)
                stream_sp(sp, GLA)

            @block.gpsimd
            def _(pool):
                pool.dma_start(wg2[0:GR, :], w["gla_wg2"]).then_inc(s("wg2_in"), 16)
                pool.dma_start(wg2[GR:GR + 1, :], w["gla_bg"].rearrange("(a n) -> a n", a=1)).then_inc(s("wg2_in"), 16)
                for h in range(GH):
                    pool.wait_ge(s("gla_state"), 8 * (h + 1))
                    pool.dma_start(o["gla_p"][h], Sall[:, 7, :]).then_inc(s("gla_p_out"), 16)
                    pool.wait_ge(s("gla_p_out"), 16 * (h + 1))

                def store_state(b):
                    pool.wait_ge(s("gs_new"), b + 1)
                    pool.dma_start(o["gla_s"][b].rearrange("h p v -> p h v"),
                                   Sring[:, b % 2, :].rearrange("p (h v) -> p h v", h=GH)).then_inc(s(f"gs_out{b % 2}"), 16)

                pool.wait_ge(s("o_done"), GH)
                for b in range(NS):
                    if b >= 2:
                        store_state(b - 2)
                        pool.wait_ge(s(f"gs_out{b % 2}"), 16 * (b // 2))
                        pool.wait_ge(s("gs_read"), b - 1)
                    pool.dma_start(Sring[:, b % 2, :].rearrange("p (h v) -> p h v", h=GH),
                                   w["state_gla"][b].rearrange("h p v -> p h v")).then_inc(s(f"gs_in{b % 2}"), 16)
                store_state(NS - 2)
                store_state(NS - 1)

            @block.scalar
            def _(act):
                modulate_act(act, 0, n1, 0)
                x = U[U_LR[0]]
                split_hi(act, x["i"] + 1)
                act.wait_ge(pass_done, passes[x["tile0"]])
                act.activation(halves(lrT[0:GR, :]), ps[0:GR, 2 * (x["tile0"] % 2):2 * (x["tile0"] % 2) + 2, 0:HT], ACT.Copy).then_inc(tile_read["act"], 1)
                act.wait_ge(s("x_spilled"), 16)
                between = Between(gla_in_act(act), IN_STEPS, GLA_IN)
                for u in GLA_IN:
                    copy_tiles(act, u, DESTS[U[u]["kind"]], U[u]["m0"], between)
                between.finish()
                stream_act(act, GLA, AQKV[0], gla_act(act), GLA_STEPS)

            @block.vector
            def _(dve):
                dve.memset(lrT[0:32, :], 1.0)
                modulate_dve(dve, 0, xT1, n1, V_N1, 0, KD)
                split_lo(dve, U[U_LR[0]]["i"] + 1)
                between = Between(gla_in_dve(dve), IN_STEPS, GLA_IN)
                for j, u in enumerate(GLA_IN):
                    split_between(dve, u, between)
                    ada_dve(dve, 8 + j, ada2)
                    if j >= 1:
                        ada_turn_dve(dve, 7 + j)
                ada_turn_dve(dve, 15)
                between.finish()
                stream_dve(dve, GLA, gla_dve(dve), GLA_STEPS)

            @block.tensor
            def _(pe):
                multiply(pe, U_LR[0], actH, actL, arriving=(s("h_split"), 0))
                between = Between(gla_in_pe(pe), IN_STEPS, GLA_IN)
                for j, u in enumerate(GLA_IN):
                    multiply(pe, u, actH, actL, between)
                    ada_pe(pe, 8 + j)
                    if j >= 1:
                        ada_turn_pe(pe, 7 + j, ada2)
                ada_turn_pe(pe, 15, ada2)
                between.finish()
                stream_pe(pe, GLA, gla_pe(pe), GLA_STEPS)

        hank = at(0, AH, 512)
        qkS = at(0, NG, AG, parts=NS)
        vnew = at(1536, NG, AG, parts=NS)
        kring = at(3072, 2, AG)
        biasT = at(16640, AH, 512)
        avt = at(20736, 4, AG)
        kst = at(22784, 2, AG)
        sq_ = at(23808, 2, 512)
        PT = at(24832, 2, 512)
        bnd = at(25856, 2, AH * BND)
        sc = at(26912, NG, NS * AH)
        snew = at(27104, NG, AH, parts=NS)
        SS = at(27128, NG, SK, parts=NS * AH)
        sbias = at(27515, NG, SK, parts=NS * AH)
        pT = at(27902, NG, NS * AH)
        small = at(28094, 32)
        snd = at(28126, NG, AH, parts=NS * AH)
        snr = at(28150, NG, 1, parts=NS * AH)
        prod = at(28190, AG)
        relb = at(28702, NG * AH, parts=33)
        relbS = at(28726, NG, NS * AH, parts=33)
        onehot = at(23808, NG * (BW + SK), parts=33)
        bvec = at(0, NG, BW, parts=AH)
        BC = ((0, 2 * P), (2 * P, 3 * P), (3 * P, 4 * P))

        def rows(g, c):
            return slice(P * c, P * c + P) if g == 0 else slice(c, TP, 4)

        def steps(g):
            if g == 0:
                return [(c, slice(h, h + 3, 2), [c] if c == 0 else [c - 1, c]) for c in range(4) for h in (0, 4, 1, 5)]
            return [(c, slice(h, AH, 2), [c]) for c in range(4) for h in (0, 1)]

        J0 = [0, 16, 24]
        FLIP_GAP = 0
        KOUT = [[3], [0, 1, 2, 3], [0, 1, 2, 3]]
        K0 = [0, 1, 5]
        NK = (P, P, P // 2)

        def win_rows(g, c, kv):
            v = o[f"win{g + 1}_p"]
            v = v[:, :] if g == 0 else v.rearrange("(i c) n -> c i n", c=4)[c]
            return v[:, AG * kv:AG * kv + AG]

        def cache_rows(g, b, kv):
            v = w[f"cache_win{g + 1}"][b].rearrange("(i c) n -> c i n", c=DIL[g])[0]
            return v[:, AG * kv:AG * kv + AG]

        def bias_sp(sp):
            sp.dma_start(relb[0:32, :], w["rel_bias"]).then_inc(s("relb_in"), 16)
            sp.dma_start(onehot, con["onehot"]).then_inc(s("relb_in"), 16)
            sp.wait_ge(s("bvec_ready"), NG)
            sp.dma_start(bd.rearrange("(g h) n -> h g n", g=NG), bvec).then_inc(s("bias_spilled"), 16)
            sp.wait_ge(s("bias_spilled"), 16)
            for g in range(NG):
                lo, hi = BC[g]
                src = bass.AP(bd.tensor, g * AH * BW, [[1, P], [BW, AH], [1, hi - lo]])
                sp.dma_start(hank[:, :, lo:hi], src).then_inc(s("hank_in"), 16)

        def bias_pe(pe):
            pe.wait_ge(s("relb_in"), 32)
            pe.wait_ge(s("relb_ready"), 1)
            for g in range(NG):
                pe.matmul(ps[0:AH, 4 + g, 0:BW], relb[:, AH * g:AH * g + AH], onehot[:, BW * g:BW * g + BW],
                          start=True, stop=True).then_inc(s("bvec_T"), 1)
                last = pe.matmul(ps[0:NS * AH, 7, SK * g:SK * g + SK], relbS[:, g, :],
                                 onehot[:, NG * BW + SK * g:NG * BW + SK * g + SK], start=True, stop=True)
            last.then_inc(s("sbias_T"), 1)

        def flip_pe(pe, h):
            if h == 0:
                pe.wait_ge(s("hank_in"), 16 * NG)
                pe.wait_ge(s("av_tok"), 4)
            if h >= 2:
                pe.wait_ge(s("bias_ready"), h - 1)
            pe.matmul(ps[:, 4 + h % 2, :], flip, hank[:, h, :], start=True, stop=True).then_inc(s("flipped"), 1)

        def flip_act(act, h):
            act.wait_ge(s("flipped"), h + 1)
            act.activation(biasT[:, h, :], ps[:, 4 + h % 2, :], ACT.Copy).then_inc(s("bias_ready"), 1)

        def bias_dve(dve):
            dve.memset(relb[32:33, :], 1.0)
            dch.link(dve, dve.memset(sc[:, NG - 1, :], 0.0))
            dve.wait_ge(s("relb_in"), 32)
            for g in range(NG):
                last = dve.tensor_copy(relbS[:, g, :].rearrange("p (b h) -> p b h", h=AH),
                                       relb[:, AH * g:AH * g + AH].unsqueeze(1).to_broadcast([33, NS, AH]))
            last.then_inc(s("relb_ready"), 1)
            for g in range(NG):
                dve.wait_ge(s("bvec_T"), g + 1)
                dve.tensor_copy(bvec[:, g, :], ps[0:AH, 4 + g, 0:BW]).then_inc(s("bvec_ready"), 1)
            dve.wait_ge(s("sbias_T"), 1)
            dve.tensor_copy(sbias.rearrange("p g n -> p (g n)"), ps[0:NS * AH, 7, 0:NG * SK]).then_inc(s("sbias"), 1)

        def heads_tok_pe(pe, g, A):
            for c in range(4):
                if g == 0 and c == 2:
                    pe.wait_ge(s("av_tok"), 2)
                    bias_pe(pe)
                    yield
                    pe.wait_ge(s("bvec_ready"), NG)
                if c >= 2:
                    pe.wait_ge(s("av_tok"), 4 * g + c - 1)
                for m in range(4):
                    last = pe.transpose(ps[:, 4 + c % 2, P * m:P * m + P], A[:, 8 + m, rows(g, c)], ident)
                last.then_inc(s("av_T"), 1)
                yield
            if g == 0:
                pe.wait_ge(s("sbias"), 1)
            for i, c in enumerate(KOUT[g]):
                if i >= 2:
                    pe.wait_ge(s("k_tok"), K0[g] + i - 1)
                for m in range(4):
                    last = pe.transpose(ps[:, 6 + i % 2, P * m:P * m + P], A[:, 4 + m, rows(g, c)], ident)
                last.then_inc(s("ak_T"), 1)
                yield
            if g == 0:
                for _ in range(FLIP_GAP):
                    yield
                for h in range(AH):
                    flip_pe(pe, h)
                    yield
                pe.wait_ge(s("bias_ready"), AH)
            pe.wait_ge(s("av_tok"), 4 * g + 4)
            pe.wait_ge(s("k_tok"), K0[g] + len(KOUT[g]))
            for a in range(3):
                for m in range(4):
                    last = pe.transpose(ps[0:NS, 4 + a, P * m:P * m + P], A[:, 4 * a + m, TP:T], ident)
            last.then_inc(s("new_T"), 1)
            yield

        def heads_tok_act(act, g):
            for c in range(4):
                if g == 0 and c == 2:
                    yield
                act.wait_ge(s("av_T"), 4 * g + c + 1)
                act.activation(avt[:, c, :], ps[:, 4 + c % 2, :], ACT.Copy).then_inc(s("av_tok"), 1)
                yield
            for c in KOUT[g]:
                yield
            if g == 0:
                act.wait_ge(s("o_spilled"), 16)
                for d in range(2):
                    act.wait_ge(s(f"gs_out{d}"), 16 * (NS // 2))
                for _ in range(FLIP_GAP):
                    yield
                for h in range(AH):
                    flip_act(act, h)
                    yield
            act.wait_ge(s("new_T"), g + 1)
            act.activation(qkS[:, 0:2, :], ps[0:NS, 4:6, :], ACT.Copy)
            act.activation(vnew[:, g, :], ps[0:NS, 6, :], ACT.Copy).then_inc(s("new_tok"), 1)
            yield

        def heads_tok_dve(dve, g):
            for c in range(4):
                if g == 0 and c == 2:
                    bias_dve(dve)
                    yield
                yield
            for i in range(len(KOUT[g])):
                n = K0[g] + i
                dve.wait_ge(s("ak_T"), n + 1)
                if n >= 2:
                    dve.wait_ge(s(f"k_out{n % 2}"), 16 * (n // 2))
                dve.tensor_copy(kst[:, n % 2, :], ps[:, 6 + i % 2, :]).then_inc(s("k_tok"), 1)
                yield
            if g == 0:
                for h in range(FLIP_GAP + AH):
                    yield
            dve.wait_ge(s("new_tok"), g + 1)
            dch.link(dve, dve.tensor_tensor(qkS[:, 2, :], qkS[:, 0, :], qkS[:, 1, :], ALU.mult))
            dve.tensor_reduce(snew[:, g, :], qkS[:, 2, :].rearrange("p (h e) -> p h e", e=AE), AX.X, ALU.add)
            yield

        def attention_steps(g):
            return 4 + len(KOUT[g]) + 1 + (1 + FLIP_GAP + AH if g == 0 else 0) + len(steps(g)) + 2 + NS

        def heads_tok_sp(sp, g):
            for i, c in enumerate(KOUT[g]):
                n = K0[g] + i
                sp.wait_ge(s("k_tok"), n + 1)
                sp.dma_start(win_rows(g, c, 0), kst[:, n % 2, :]).then_inc(s(f"k_out{n % 2}"), 16)
                sp.wait_ge(s("av_tok"), 4 * g + c + 1)
                sp.dma_start(win_rows(g, c, 1), avt[:, c, :]).then_inc(outs, 16)
                n_outs[0] += 16
            sp.wait_ge(s("new_tok"), g + 1)
            last = WIN[g] - 1
            sp.dma_start(o[f"win{g + 1}_s"][:, last, 0:AG], qkS[:, 1, :]).then_inc(outs, 16)
            sp.dma_start(o[f"win{g + 1}_s"][:, last, AG:2 * AG], vnew[:, g, :]).then_inc(outs, 16)
            n_outs[0] += 32

        def attend_pe(pe, g, A):
            st = steps(g)
            pe.wait_ge(s("new_tok"), g + 1)
            for j in range(len(st) + 2):
                if j < len(st):
                    c, hs, keys = st[j]
                    nh, h0 = AH // 4 if g == 0 else AH // 2, hs.start
                    n = J0[g] + j
                    J = P * len(keys)
                    if n >= 2:
                        pe.wait_ge(s("s_read"), n - 1)
                    for i in range(nh):
                        h = h0 + 2 * i
                        r = AE * (h % 2)
                        kt = slice(P * keys[0], P * keys[0] + J) if g == 0 else rows(g, c)
                        last = pe.matmul(ps[:, 4 + n % 2, J * i:J * i + J], A[r:r + AE, h // 2, rows(g, c)],
                                         A[r:r + AE, 4 + h // 2, kt], start=True, stop=True)
                    last.then_inc(s("s_ready"), 1)
                if 1 <= j <= len(st):
                    c, hs, keys = st[j - 1]
                    nh, h0 = AH // 4 if g == 0 else AH // 2, hs.start
                    n = J0[g] + j - 1
                    pe.wait_ge(s("p_ready"), n + 1)
                    if n >= 1:
                        pe.wait_ge(s("pT_ready"), n)
                    for i in range(nh * len(keys)):
                        last = pe.transpose(ps[:, 6, P * i:P * i + P], sq_[:, n % 2, P * i:P * i + P], ident)
                    last.then_inc(s("p_T"), 1)
                if j >= 2:
                    c, hs, keys = st[j - 2]
                    nh, h0 = AH // 4 if g == 0 else AH // 2, hs.start
                    n = J0[g] + j - 2
                    pe.wait_ge(s("pT_ready"), n + 1)
                    if h0 == 0 and 4 * g + c >= 1:
                        pe.wait_ge(s("o_read"), 4 * g + c)
                    for i in range(nh):
                        h = h0 + 2 * i
                        for kb, kt in enumerate(keys):
                            x = i * len(keys) + kb
                            last = pe.matmul(ps[:, 7, AE * h:AE * h + AE], PT[:, n % 2, P * x:P * x + P],
                                             avt[:, kt, AE * h:AE * h + AE], start=kb == 0, stop=kb == len(keys) - 1)
                    last.then_inc(s("pv"), 1)
                yield

        def attend_dve(dve, g):
            st = steps(g)

            def gather(c, n):
                dve.wait_ge(s("pv"), n + 1)
                out = bnd[:, c % 2, :].rearrange("p (h f) -> p h f", f=BND)[:, :, 0:AE]
                dve.tensor_copy(out, ps[:, 7, :].rearrange("p (h e) -> p h e", e=AE)).then_inc(s("o_read"), 1)

            due = []
            for j, (c, hs, keys) in enumerate(st):
                nh, h0 = AH // 4 if g == 0 else AH // 2, hs.start
                n = J0[g] + j
                J = P * len(keys)
                lo, hi = BC[g]
                lo = hi - J
                dve.wait_ge(s("s_ready"), n + 1)
                if n >= 2:
                    dve.wait_ge(s("p_T"), n - 1)
                sv = sq_[:, n % 2, 0:nh * J].rearrange("p (h k) -> p h k", k=J)
                dve.scalar_tensor_tensor(sv, ps[:, 4 + n % 2, 0:nh * J].rearrange("p (h k) -> p h k", k=J), SCALE,
                                         biasT[:, hs, lo:hi], ALU.mult, ALU.add).then_inc(s("s_read"), 1)
                dve.wait_ge(s("s_read"), n + 1)
                if h0 == 0 and 4 * g + c >= 2:
                    dve.wait_ge(s(f"g_out{c % 2}"), 16 * ((4 * g + c) // 2))
                nm = bnd[:, c % 2, :].rearrange("p (h f) -> p h f", f=BND)[:, hs, AE]
                dve.tensor_reduce(nm, sv, AX.X, ALU.max, negate=True).then_inc(s("m_ready"), 1)
                if due and due[0][0] == j:
                    gather(*due.pop(0)[1:])
                if j + 1 == len(st) or st[j + 1][0] != c:
                    due.append((j + 2, c, n))
                yield
            yield
            for _, c, n in due:
                gather(c, n)
            yield

        def attend_act(act, g):
            st = steps(g)
            for j in range(len(st) + 1):
                if j < len(st):
                    c, hs, keys = st[j]
                    nh, h0 = AH // 4 if g == 0 else AH // 2, hs.start
                    n = J0[g] + j
                    J = P * len(keys)
                    act.wait_ge(s("m_ready"), n + 1)
                    for i in range(nh):
                        b0 = BND * (h0 + 2 * i)
                        sv = sq_[:, n % 2, J * i:J * i + J]
                        last = act.activation(sv, sv, ACT.Exp, bias=bnd[:, c % 2, b0 + AE:b0 + AE + 1],
                                              accum_out=bnd[:, c % 2, b0 + AE + 1:b0 + AE + 2])
                    last.then_inc(s("p_ready"), 1)
                if j >= 1:
                    c, hs, keys = st[j - 1]
                    nh, h0 = AH // 4 if g == 0 else AH // 2, hs.start
                    n = J0[g] + j - 1
                    act.wait_ge(s("p_T"), n + 1)
                    if n >= 2:
                        act.wait_ge(s("pv"), n - 1)
                    k = P * nh * len(keys)
                    act.activation(PT[:, n % 2, 0:k], ps[:, 6, 0:k], ACT.Copy).then_inc(s("pT_ready"), 1)
                yield
            yield

        def attend_sp(sp, g):
            for c in range(4):
                sp.wait_ge(s("o_read"), 4 * g + c + 1)
                sp.wait_ge(s("p_ready"), J0[g] + (4 if g == 0 else 2) * (c + 1))
                dst = gd[g][P * c:P * c + P, :] if g == 0 else gd[g].rearrange("(i c) n -> c i n", c=4)[c]
                sp.dma_start(dst, bnd[:, c % 2, :]).then_inc(s(f"g_out{c % 2}"), 16)

        def sample_sp(sp, g, samples):
            for b in samples:
                n = NS * g + b
                if n >= 2:
                    sp.wait_ge(s("sc_mul"), n - 1)
                sp.dma_start(kring[0:NK[g], b % 2, :], cache_rows(g, b, 0)).then_inc(s(f"kc_in{b % 2}"), 16)

        def sample_pe(pe, g):
            for b in range(NS):
                n = NS * g + b
                if b == 0:
                    pe.wait_ge(s("s_read"), J0[g] + len(steps(g)))
                if n >= 2:
                    pe.wait_ge(s("sc_mul"), n - 1)
                pe.matmul(ps[:, 4 + b % 2, :], ident[0:NS, b:b + 1].to_broadcast([NS, P]), qkS[:, 0, :],
                          start=True, stop=True).then_inc(s("q_wide"), 1)
                yield

        def sample_dve(dve, g):
            k = NK[g]
            for b in range(NS):
                n = NS * g + b
                dve.wait_ge(s("q_wide"), n + 1)
                dve.wait_ge(s(f"kc_in{b % 2}"), 16 * (n // 2 + 1))
                dve.tensor_tensor(prod[0:k, :], kring[0:k, b % 2, :], ps[0:k, 4 + b % 2, :], ALU.mult)\
                   .then_inc(s("sc_mul"), 1)
                dve.wait_ge(s("sc_mul"), n + 1)
                dch.link(dve, dve.tensor_reduce(sc[0:k, g, AH * b:AH * b + AH],
                                                prod[0:k, :].rearrange("p (h e) -> p h e", e=AE), AX.X, ALU.add))
                yield

        def attention_pe(pe, g, A, join=None):
            yield from heads_tok_pe(pe, g, A)
            yield from attend_pe(pe, g, A)
            yield from turns(sample_pe(pe, g), join)

        def attention_act(act, g, join=None):
            yield from heads_tok_act(act, g)
            yield from attend_act(act, g)
            yield from turns((None for _ in range(NS)), join)

        def attention_dve(dve, g, join=None):
            yield from heads_tok_dve(dve, g)
            yield from attend_dve(dve, g)
            yield from turns(sample_dve(dve, g), join)

        def turns(samples, join):
            for b in range(NS):
                next(samples)
                yield
                if join and b >= NS // 2 - 1:
                    next(join)
                    yield
            assert next(samples, None) is None
            if join:
                yield from join

        def attention_pool(pool, g):
            if g == 0:
                bias_sp(pool)
            heads_tok_sp(pool, g)
            sample_sp(pool, g, range(2))
            attend_sp(pool, g)
            if g < NG - 1:
                sample_sp(pool, g, range(2, NS))
            nk = K0[g] + len(KOUT[g])
            for d in range(2):
                pool.wait_ge(s(f"g_out{d}"), 32 * (g + 1))
                if nk > d:
                    pool.wait_ge(s(f"k_out{d}"), 16 * ((nk + 1 - d) // 2))

        for g in range(NG - 1):
            with nc.Block() as block:
                us, here, there = phase(f"att{g}"), AQKV[g], AQKV[1 - g]
                n_steps = attention_steps(g)

                @block.sync
                def _(sp):
                    stream_sp(sp, us[:1])
                    if g == 0:
                        sp.wait_ge(s("o_all"), 1)
                        sp.dma_start(od, oT2.rearrange("p k t -> p (k t)")).then_inc(s("o_spilled"), 16)
                    stream_sp(sp, us[1:])

                @block.gpsimd
                def _(pool):
                    attention_pool(pool, g)

                @block.scalar
                def _(act):
                    stream_act(act, us, there, attention_act(act, g), n_steps, fine=g > 0)

                @block.vector
                def _(dve):
                    stream_dve(dve, us, attention_dve(dve, g), n_steps, fine=g > 0)

                @block.tensor
                def _(pe):
                    stream_pe(pe, us, attention_pe(pe, g, here), n_steps, fine=g > 0)

        diag = at(10400, NG, NS * AH, parts=NS * AH)
        pn = at(10592, NG, NS * AH, parts=NS)
        sel8 = at(10784, NS * AH, parts=NS)
        sel64 = at(10848, NS, parts=NS * AH)
        hmask = at(10856, AH, parts=NS * AH)
        cmb = at(16640, 2, NG * AH * BND)
        cw = [at(20736 + 32 * i, NG, AH) for i in range(4)]
        cw8 = [at(20864 + 8 * i, AH) for i in range(4)]
        of = at(20896, 2, AG)
        NR = NS * AH
        VSTEPS = 6
        VB = NG * NS // VSTEPS
        vring = at(4160, 3 * VB, AG)
        JOIN_STEPS = 5 + 2 + 1 + VSTEPS

        def join_pe(pe):
            for j in range(5):
                if j >= 1:
                    c = j - 1
                    pe.wait_ge(s("joined"), c + 1)
                    if c >= 2:
                        pe.wait_ge(s("oj_lo"), c - 1)
                    for f in range(4):
                        last = pe.transpose(ps[:, 6 + c % 2, P * f:P * f + P], of[:, c % 2, P * f:P * f + P], ident)
                    last.then_inc(s("oj_T"), 1)
                yield
            pe.wait_ge(s("relb_in"), 80)
            pe.wait_ge(s("oj_lo"), 4)
            for g in range(NG):
                last = pe.transpose(ps[0:NR, 6, P * g:P * g + P], sc[:, g, :], ident)
            last = pe.matmul(ps[0:NR, 7, 0:NG * AH], sel8, snew.rearrange("p g h -> p (g h)"), start=True, stop=True)
            last.then_inc(s("sn_T"), 1)
            yield
            pe.wait_ge(s("sm_m"), 2)
            for g in range(NG):
                last = pe.transpose(ps[:, 6, NR * g:NR * g + NR], SS[:, g, 0:P], ident[0:NR, 0:NR])
            last.then_inc(s("sn_T"), 1)
            pe.wait_ge(s("sm_m"), 3)
            pe.matmul(ps[0:NS, 7, 0:NG * NR], sel64, diag.rearrange("p g n -> p (g n)"), start=True, stop=True)\
              .then_inc(s("sn_T"), 1)
            yield
            pe.wait_ge(s("spT"), 2)
            pe.wait_ge(s("sc_mul"), NG * NS)
            for g in range(NG):
                for f in range(4):
                    pe.matmul(ps[:, 4, 16 * f:16 * f + 16], vnew[:, g, P * f:P * f + P],
                              pn[:, g, :].rearrange("p (b h) -> p b h", h=AH)[:, :, 2 * f:2 * f + 2],
                              start=g == 0 and f == 0, stop=False, skip_group_check=True)
            yield
            for n in range(NG * NS):
                g, b = n // NS, n % NS
                k = NK[g]
                if n % VB == 0:
                    pe.wait_ge(s(f"vc_in{n // VB % 3}"), 16 * (n // VB // 3 + 1))
                for f in range(4):
                    last = pe.matmul(ps[:, 4, 16 * f + 2 * b:16 * f + 2 * b + 2], vring[0:k, n % (3 * VB), P * f:P * f + P],
                                     pT[0:k, g, AH * b + 2 * f:AH * b + 2 * f + 2], start=False,
                                     stop=n == NG * NS - 1 and f == 3, skip_group_check=True)
                last.then_inc(s("vc_used"), 1)
                if (n + 1) % (NG * NS // VSTEPS) == 0:
                    yield

        def join_act(act):
            for j in range(5):
                if j < 4:
                    act.wait_ge(s("join_d"), j + 1)
                    act.activation(cw[1], cw[0], ACT.Exp).then_inc(s("join_e"), 1)
                if j >= 1:
                    c = j - 1
                    act.wait_ge(s("oj_T"), c + 1)
                    act.activation(b2H[:, 0:4, c:TP:4], ps[:, 6 + c % 2, :].rearrange("p (f i) -> p f i", f=4), ACT.Copy)\
                       .then_inc(s("oj_hi"), 1)
                yield
            act.wait_ge(s("sm_m"), 1)
            act.activation(SS, SS, ACT.Exp, bias=small[0:NR, 0:1], accum_out=small[0:NR, 1:2]).then_inc(s("sm_p"), 1)
            for _ in range(2 + VSTEPS):
                yield
            act.wait_ge(s("vc_used"), NG * NS)
            for r in range(2):
                q = slice(AE * r, AE * r + AE)
                last = act.activation(b2H[q, 0:4, TP:T],
                                      ps[q, 4, 0:NR].rearrange("p (f b r) -> p f b r", f=4, r=2)[:, :, :, r], ACT.Copy)
            last.then_inc(s("os_hi"), 1)
            yield

        def join_dve(dve):
            d, e, wd, al = cw
            mn, den, rd, _ = cw8
            for j in range(5):
                if j < 4:
                    c = j
                    dve.wait_ge(s(f"cmb_in{c % 2}"), 16 * (c // 2 + 1))
                    C = cmb[:, c % 2, :].rearrange("p (g h f) -> p g h f", g=NG, f=BND)
                    dch.link(dve, dve.tensor_tensor(mn, C[:, 0, :, AE], C[:, 1, :, AE], ALU.min))
                    dch.link(dve, dve.tensor_tensor(mn, mn, C[:, 2, :, AE], ALU.min))
                    dve.tensor_tensor(d, mn.unsqueeze(1).to_broadcast([P, NG, AH]), C[:, :, :, AE], ALU.subtract)\
                       .then_inc(s("join_d"), 1)
                    dve.wait_ge(s("join_e"), c + 1)
                    dch.link(dve, dve.tensor_tensor(wd, e, C[:, :, :, AE + 1], ALU.mult))
                    dch.link(dve, dve.tensor_tensor(den, wd[:, 0, :], wd[:, 1, :], ALU.add))
                    dch.link(dve, dve.tensor_tensor(den, den, wd[:, 2, :], ALU.add))
                    dch.link(dve, dve.reciprocal(rd, den))
                    dch.link(dve, dve.tensor_tensor(al, e, rd.unsqueeze(1).to_broadcast([P, NG, AH]), ALU.mult))
                    for g in range(NG):
                        ins = dve.tensor_tensor(C[:, g, :, 0:AE], C[:, g, :, 0:AE],
                                                al[:, g, :].unsqueeze(2).to_broadcast([P, AH, AE]), ALU.mult)
                    dch.link(dve, ins)
                    if c >= 2:
                        dve.wait_ge(s("oj_T"), c - 1)
                    ov = of[:, c % 2, :].rearrange("p (h e) -> p h e", e=AE)
                    dch.link(dve, dve.tensor_tensor(ov, C[:, 0, :, 0:AE], C[:, 1, :, 0:AE], ALU.add))
                    dve.tensor_tensor(ov, ov, C[:, 2, :, 0:AE], ALU.add).then_inc(s("joined"), 1)
                if j >= 1:
                    c = j - 1
                    dve.wait_ge(s("oj_hi"), c + 1)
                    dve.tensor_tensor(b2L[:, 0:4, c:TP:4], ps[:, 6 + c % 2, :].rearrange("p (f i) -> p f i", f=4),
                                      b2H[:, 0:4, c:TP:4].bitcast(F32), ALU.subtract).then_inc(s("oj_lo"), 1)
                yield
            dve.wait_ge(s("sn_T"), 1)
            dve.wait_ge(s("relb_in"), 80)
            dch.link(dve, dve.tensor_tensor(snd, ps[0:NR, 7, 0:NG * AH].rearrange("p (g h) -> p g h", g=NG),
                                            hmask.unsqueeze(1).to_broadcast([NR, NG, AH]), ALU.mult))
            dch.link(dve, dve.tensor_reduce(snr[:, :, 0], snd, AX.X, ALU.add))
            dve.scalar_tensor_tensor(SS[:, :, 0:P], ps[0:NR, 6, 0:NG * P].rearrange("p (g k) -> p g k", g=NG), SCALE,
                                     sbias[:, :, 0:P], ALU.mult, ALU.add)
            dch.link(dve, dve.scalar_tensor_tensor(SS[:, :, P:SK], snr, SCALE, sbias[:, :, P:SK], ALU.mult, ALU.add))
            dve.tensor_reduce(small[0:NR, 0:1], SS, AX.XY, ALU.max, negate=True).then_inc(s("sm_m"), 1)
            dve.wait_ge(s("sm_p"), 1)
            dch.link(dve, dve.reciprocal(small[0:NR, 2:3], small[0:NR, 1:2]))
            dve.tensor_scalar(SS, SS, small[0:NR, 2:3], None, ALU.mult).then_inc(s("sm_m"), 1)
            dve.wait_ge(s("sm_m"), 2)
            dve.tensor_tensor(diag, ident[0:NR, 0:NR].unsqueeze(1).to_broadcast([NR, NG, NR]),
                              SS[:, :, P:SK].to_broadcast([NR, NG, NR]), ALU.mult).then_inc(s("sm_m"), 1)
            yield
            dve.wait_ge(s("sn_T"), 2)
            dve.tensor_copy(pT.rearrange("p g n -> p (g n)"), ps[:, 6, 0:NG * NR]).then_inc(s("spT"), 1)
            dve.wait_ge(s("sn_T"), 3)
            dve.tensor_copy(pn.rearrange("p g n -> p (g n)"), ps[0:NS, 7, 0:NG * NR]).then_inc(s("spT"), 1)
            for _ in range(1 + VSTEPS):
                yield
            dve.wait_ge(s("os_hi"), 1)
            for r in range(2):
                q = slice(AE * r, AE * r + AE)
                last = dve.tensor_tensor(b2L[q, 0:4, TP:T],
                                         ps[q, 4, 0:NR].rearrange("p (f b r) -> p f b r", f=4, r=2)[:, :, :, r],
                                         b2H[q, 0:4, TP:T].bitcast(F32), ALU.subtract)
            last.then_inc(s("oj_lo"), 1)
            yield

        with nc.Block() as block:
            g_last = NG - 1
            us, here = phase("att2"), AQKV[g_last % 2]
            n_steps = attention_steps(g_last) + JOIN_STEPS

            @block.sync
            def _(sp):
                stream_sp(sp, us)
                for d in range(2):
                    sp.wait_ge(s(f"spill_out{d}"), 8 * len(spill_order))

            @block.gpsimd
            def _(pool):
                pool.dma_start(sel8, con["sel8"]).then_inc(s("relb_in"), 16)
                pool.dma_start(sel64, con["sel64"]).then_inc(s("relb_in"), 16)
                pool.dma_start(hmask, con["hmask"]).then_inc(s("relb_in"), 16)
                attention_pool(pool, g_last)
                def load_values(i):
                    if i >= 3:
                        pool.wait_ge(s("vc_used"), VB * (i - 2))
                    g, b = VB * i // NS, VB * i % NS
                    src = w[f"cache_win{g + 1}"].rearrange("b (i c) n -> c i b n", c=DIL[g])[0][:, b:b + VB, AG:2 * AG]
                    slot = VB * (i % 3)
                    pool.dma_start(vring[0:NK[g], slot:slot + VB, :], src).then_inc(s(f"vc_in{i % 3}"), 16)

                def load_group_outputs(c):
                    if c >= 2:
                        pool.wait_ge(s("joined"), c - 1)
                    pool.dma_start(cmb[:, c % 2, :].rearrange("p (g n) -> p g n", g=NG),
                                   gd.rearrange("g (i c) n -> c i g n", c=4)[c]).then_inc(s(f"cmb_in{c % 2}"), 16)

                half = NS // 2
                sample_sp(pool, g_last, range(2, half))
                pool.wait_ge(s("s_read"), J0[g_last] + len(steps(g_last)))
                load_group_outputs(0)
                load_group_outputs(1)
                sample_sp(pool, g_last, range(half, half + 2))
                for i in range(3):
                    load_values(i)
                load_group_outputs(2)
                sample_sp(pool, g_last, range(half + 2, NS))
                load_group_outputs(3)
                for i in range(3, VSTEPS):
                    load_values(i)

            @block.scalar
            def _(act):
                stream_act(act, us, None, attention_act(act, g_last, join_act(act)), n_steps, fine=True)

            @block.vector
            def _(dve):
                stream_dve(dve, us, attention_dve(dve, g_last, join_dve(dve)), n_steps, fine=True)

            @block.tensor
            def _(pe):
                stream_pe(pe, us, attention_pe(pe, g_last, here, join_pe(pe)), n_steps, fine=True)

        oT4 = at(0, KD, T)
        ya, yb = at(12480, KD, T), at(16640, KD, T)
        raw4 = at(20800, 4, T)
        f4 = at(FT, 4, T)
        sg4 = at(29120, 2, T)
        gated = at(30160, NS)
        ada4 = at(30200, 2, 2 * P, parts=NC)
        xT = at(FX, KD, T)
        n2 = norm_temps(0)
        G = {k: units(k) for k in ("bb", "ba", "wo", "up", "dn")}
        RAW = list(range(KD)) + [q + k * KD for q in range(KD) for k in (1, 2)]

        def residual_dve(dve, n, q, gate):
            a, b = ps[:, 2 * (n % 2), 0:HT], ps[:, 2 * (n % 2) + 1, 0:HT]
            g = mod[:, gate + q, 0:1]
            dve.scalar_tensor_tensor(xT[:, q, 0:HT], a, g, xT[:, q, 0:HT], ALU.mult, ALU.add)
            dve.scalar_tensor_tensor(xT[:, q, HT:TP], b[:, 0:TP - HT], g, xT[:, q, HT:TP], ALU.mult, ALU.add)
            dve.tensor_tensor(gated, b[:, TP - HT:HT], mod[:, gate + q, 1:NC], ALU.mult).then_inc(tile_read["dve"], 1)
            dve.wait_ge(tile_read["dve"], freed[n])
            dve.tensor_tensor(xT[:, q, TP:T], xT[:, q, TP:T], gated, ALU.add).then_inc(s("x_new"), 1)
            dve.wait_ge(s("x_new"), (0 if gate == 2 * KD else KD) + q + 1)

        def sigmoid_act(act, r):
            act.wait_ge(s(f"raw_in{r % 4}"), 16 * (r // 4 + 1))
            q = (r - KD) // 2
            if 2 <= r < KD + 2:
                act.wait_ge(s("sg_used"), r - 1)
            elif r >= KD + 2 and r % 2 == 0:
                act.wait_ge(tile_read["dve"], freed[U[G["ba"][0]]["tile0"] + q - 1])
            elif r >= KD + 2:
                act.wait_ge(s("sg_used"), KD + q)
            act.activation(sg4[:, r % 2, :], raw4[:, r % 4, :], ACT.Sigmoid).then_inc(s("sg_ready"), 1)

        def ada_after(u):
            x = U[u + 1]
            return x["i"] if x["kind"] == "ada" and x["i"] < 23 else None

        def late_ada_pe(pe, a):
            if a is not None:
                ada_pe(pe, a)
                if a > 16:
                    ada_turn_pe(pe, a - 1, ada4)
                if a == len(ADA) - 1:
                    ada_turn_pe(pe, a, ada4)

        def late_ada_dve(dve, a):
            if a is not None:
                ada_dve(dve, a, ada4)
                if a > 16:
                    ada_turn_dve(dve, a - 1)
                if a == len(ADA) - 1:
                    ada_turn_dve(dve, a)

        with nc.Block() as block:
            @block.sync
            def _(sp):
                issue_all(sp, G["bb"][0] + 3, G["up"][0] + 2)

            @block.gpsimd
            def _(pool):
                for r, q in enumerate(RAW):
                    if r >= 4:
                        pool.wait_ge(s("sg_ready"), r - 3)
                        if r - 4 < KD:
                            pool.wait_ge(s("sg_used"), r - 3)
                    pool.dma_start(raw4[:, r % 4, :], rawd[:, T * q:T * q + T]).then_inc(s(f"raw_in{r % 4}"), 16)
                    if r == 1:
                        pool.dma_start(oT4.rearrange("p k t -> p (k t)"), od).then_inc(s("o_back"), 16)
                    if r == 16:
                        pool.dma_start(xT.rearrange("p k t -> p (k t)"), xd).then_inc(s("x_back"), 16)

            @block.scalar
            def _(act):
                def gate(q):
                    act.wait_ge(s("a2_f"), q + 1)
                    act.activation(a2H[:, q, :], f4[:, q % 4, :], ACT.Copy).then_inc(s("a2_hi"), 1)

                for j, u in enumerate(G["bb"]):
                    split_hi(act, U[u]["i"] + 1)
                    for m in range(4):
                        q = 4 * j + m
                        sigmoid_act(act, q)
                        if q >= 1:
                            gate(q - 1)
                        n = U[u]["tile0"] + m
                        act.wait_ge(pass_done, passes[n])
                        act.activation(halves(yb[:, q, :]), banks(n), ACT.Copy).then_inc(tile_read["act"], 1)
                gate(KD - 1)
                for j, u in enumerate(G["ba"]):
                    split_hi(act, U[u]["i"] + 1)
                    for m in range(2):
                        q = 2 * j + m
                        sigmoid_act(act, KD + 2 * q)
                        sigmoid_act(act, KD + 2 * q + 1)
                        if q >= 1:
                            act.wait_ge(s("mixed"), q)
                            act.activation(actH[:, q - 1, :], ya[:, q - 1, :], ACT.Copy).then_inc(s("mix_hi"), 1)
                act.wait_ge(s("mixed"), KD)
                act.activation(actH[:, KD - 1, :], ya[:, KD - 1, :], ACT.Copy).then_inc(s("mix_hi"), 1)
                for j, u in enumerate(G["wo"]):
                    split_hi(act, U[u]["i"] + 1)
                    for m in range(2):
                        act.wait_ge(s("x_new"), 2 * j + m + 1)
                        square_act(act, 1, 2 * j + m, xT, n2)
                norm_act(act, 1, n2)

            @block.vector
            def _(dve):
                def low(q):
                    dve.wait_ge(s("a2_hi"), q + 1)
                    dve.tensor_tensor(a2L[:, q, :], f4[:, q % 4, :], a2H[:, q, :].bitcast(F32), ALU.subtract)\
                       .then_inc(s("a2_lo"), 1)

                def mix_low(q):
                    dve.wait_ge(s("mix_hi"), q + 1)
                    dve.tensor_tensor(actL[:, q, :], ya[:, q, :], actH[:, q, :].bitcast(F32), ALU.subtract)\
                       .then_inc(s("mix_lo"), 1)

                for j, u in enumerate(G["bb"]):
                    split_lo(dve, U[u]["i"] + 1)
                    for m in range(4):
                        q = 4 * j + m
                        f = f4[:, q % 4, :]
                        dve.wait_ge(s("sg_ready"), q + 1)
                        if q >= 4:
                            dve.wait_ge(s("a2_lo"), q - 3)
                        dve.tensor_tensor(f, sg4[:, q % 2, :], raw4[:, q % 4, :], ALU.mult).then_inc(s("sg_used"), 1)
                        dve.wait_ge(s("sg_used"), q + 1)
                        dve.wait_ge(s("o_back"), 16)
                        dve.tensor_tensor(f, f, oT4[:, q, :], ALU.mult).then_inc(s("a2_f"), 1)
                        if q >= 1:
                            low(q - 1)
                    if j == 1:
                        low(KD - 1)
                    late_ada_dve(dve, ada_after(u))
                for j, u in enumerate(G["ba"]):
                    split_lo(dve, U[u]["i"] + 1)
                    for m in range(2):
                        q, n = 2 * j + m, U[u]["tile0"] + m
                        r = KD + 2 * q
                        dve.wait_ge(tile_read["act"], freed[U[G["bb"][1]]["tile0"] + 3])
                        dve.wait_ge(s("sg_ready"), r + 1)
                        dve.wait_ge(pass_done, passes[n])
                        dve.tensor_tensor(halves(ya[:, q, :]), halves(sg4[:, 0, :]), banks(n), ALU.mult)\
                           .then_inc(tile_read["dve"], 1)
                        dve.wait_ge(tile_read["dve"], freed[n])
                        dve.wait_ge(s("sg_ready"), r + 2)
                        dve.tensor_tensor(yb[:, q, :], yb[:, q, :], sg4[:, 1, :], ALU.mult).then_inc(s("sg_used"), 1)
                        dve.wait_ge(s("sg_used"), KD + q + 1)
                        dve.tensor_tensor(ya[:, q, :], ya[:, q, :], yb[:, q, :], ALU.add).then_inc(s("mixed"), 1)
                        if q >= 1:
                            mix_low(q - 1)
                    late_ada_dve(dve, ada_after(u))
                dve.wait_ge(s("mixed"), KD)
                mix_low(KD - 1)
                dve.wait_ge(s("x_back"), 16)
                for j, u in enumerate(G["wo"]):
                    split_lo(dve, U[u]["i"] + 1)
                    for m in range(2):
                        n = U[u]["tile0"] + m
                        dve.wait_ge(pass_done, passes[n])
                        residual_dve(dve, n, 2 * j + m, 2 * KD)
                        square_dve(dve, 1, 2 * j + m - 1, n2)
                    late_ada_dve(dve, ada_after(u))
                square_dve(dve, 1, KD - 1, n2)
                late_ada_dve(dve, 23)
                rstd_dve(dve, 1, n2)

            @block.tensor
            def _(pe):
                for u in G["bb"]:
                    multiply(pe, u, b2H, b2L)
                    late_ada_pe(pe, ada_after(u))
                for j, u in enumerate(G["ba"]):
                    multiply(pe, u, a2H, a2L, arriving=(s("a2_lo"), 0) if j == 0 else None)
                    late_ada_pe(pe, ada_after(u))
                for j, u in enumerate(G["wo"]):
                    multiply(pe, u, actH, actL, arriving=(s("mix_lo"), 0) if j == 0 else None)
                    late_ada_pe(pe, ada_after(u))
                late_ada_pe(pe, 23)
                norm_pe(pe, 1, n2)

        abuf = at(FT, 2, T + 2)
        acc, sg5 = at(FT + 1044, T), at(FT + 1564, T)
        ast = at(FT + 2084, 2, P, parts=NS + 2)
        n3 = norm_temps(FT, modulated=False)
        yst = at(0, 4, D)
        ysst = at(4 * D, D, parts=NS)
        tok = {k: at(FT + 6 * T + 8 * i + 8, 5) for i, k in enumerate("vytr")}
        YB = (4, 6, 0, 2, 4)
        up0, dn0 = G["up"][0], G["dn"][0]
        v0, vd0 = U[up0]["i"], U[dn0]["i"]
        p0, t0 = U[up0]["pass0"], U[up0]["tile0"]
        td0 = U[dn0]["tile0"]
        FA, FD = freed[t0], freed[t0 + 1]

        with nc.Block() as block:
            @block.sync
            def _(sp):
                with sp.Fori(0, KF // 2 - 1) as i:
                    for d in range(2):
                        u = up0 + 2 + d
                        sp.wait_ge(lo_ready, v0 + 1 + d + 2 * i)
                        load(sp, u % 2, up_sources(w, P * (2 + d) + 2 * P * i))
                with sp.Fori(0, KD) as m:
                    for half in range(2):
                        u = dn0 + half
                        sp.wait_ge(lo_ready, vd0 - 1 + half + 2 * m)
                        load(sp, u % 2, down_sources(w, half, P * m))
                for n in range(4):
                    sp.wait_ge(s("y_tok_dve" if n % 2 else "y_tok"), n // 2 + 1)
                    sp.dma_start(o["y_prompt"][P * n:P * n + P, :], yst[:, n, :]).then_inc(s("y_out"), 16)
                sp.wait_ge(s("y_tok"), 3)
                sp.dma_start(o["y_sample"], ysst).then_inc(s("y_out"), 16)
                sp.wait_ge(s("y_out"), 80)
                sp.wait_ge(outs, n_outs[0])

            @block.gpsimd
            def _(pool):
                def store(u, col):
                    pool.wait_ge(s("tail_tok"), u + 1)
                    pool.dma_start(o["conv_p"][:, col], ast[0:2, store.slot, :]).then_inc(s(f"conv_out{store.slot}"), 16)
                    pool.dma_start(o["conv_s"][:, 1, col], ast[2:NS + 2, store.slot, :])\
                        .then_inc(s(f"conv_out{store.slot}"), 16)

                with pool.Fori(0, KF // 2) as i:
                    for d in range(2):
                        store.slot = d
                        store(2 * i + d, bass.ds(P * d + 2 * P * i, P))
                for d in range(2):
                    pool.wait_ge(s(f"conv_out{d}"), 32 * (KF // 2))

            @block.scalar
            def _(act):
                def unit(i, d, first):
                    vn = v0 + 1 + d
                    act.wait_ge(w_dma[(up0 + 1 + d) % 2], U[up0 + 1 + d]["arrived"] + 32 * i)
                    act.wait_ge(pass_done, p0 + 2 * d + 4 * i)
                    act.activation(whi[:, vn % 2, :], wraw[:, (up0 + 1 + d) % 2, :], ACT.Copy).then_inc(hi_ready, 1)
                    act.wait_ge(pass_done, p0 + 2 * d + 1 + 4 * i)
                    if not first:
                        act.wait_ge(s("conv_done"), 2 * i + d - 1)
                        act.wait_ge(s("tail_T"), 2 * i + d - 1)
                    act.activation(halves(abuf[:, d, 2:T + 2]), banks(t0), ACT.Copy).then_inc(tile_read["act"], 1)
                    act.wait_ge(s("conv_done"), 2 * i + d + 1)
                    act.activation(sg5, acc, ACT.Sigmoid).then_inc(s("ffn_sig"), 1)
                    act.wait_ge(tile_read["dve"], FD + d + 2 * i)
                    act.activation(gH[:, bass.ds(2 * i + d, 1), :].rearrange("p a t -> p (a t)"), acc, ACT.Copy)\
                       .then_inc(s("g_hi"), 1)

                modulate_act(act, 1, n2, 3 * KD)
                for d in range(2):
                    unit(0, d, True)
                with act.Fori(1, KF // 2) as i:
                    for d in range(2):
                        unit(i, d, False)
                for m in range(KD):
                    for half in range(2):
                        move_cache(act)
                        split_hi(act, vd0 + 2 * m + half + 1)
                    if m >= 1:
                        act.wait_ge(s("x_new"), KD + m)
                        if m == 1:
                            act.wait_ge(s("conv_out0"), 32 * (KF // 2))
                            act.wait_ge(s("conv_out1"), 32 * (KF // 2))
                        square_act(act, 2, m - 1, xT, n3)
                act.wait_ge(s("x_new"), 2 * KD)
                square_act(act, 2, KD - 1, xT, n3)
                act.wait_ge(s("ms_ready"), 3)
                ach.link(act, act.activation(tok["y"], tok["v"], ACT.Ln))
                act.activation(tok["y"], tok["y"], ACT.Exp, scale=-0.5).then_inc(s("rs_ready"), 1)
                act.wait_ge(s("y_ready"), 1)
                for n in (0, 2, 4):
                    act.wait_ge(s("y_T"), n + 1)
                    parts, b0 = (P if n < 4 else NS), YB[n]
                    dst = yst[:, n, :] if n < 4 else ysst
                    act.activation(dst.rearrange("p (a b) -> p a b", a=2), ps[0:parts, b0:b0 + 2, :], ACT.Identity,
                                   scale=tok["r"][0:parts, n:n + 1]).then_inc(s("y_tok"), 1)
                act.wait_ge(caches_moved, 16 * len(moves))
                assert n_moved[0] == len(moves)

            @block.vector
            def _(dve):
                dve.memset(tok["v"], 1.0)
                dch.link(dve, dve.memset(abuf[:, :, 0:2], 0.0))
                conv = sem("conv_chain")
                one = lambda c, j: vec[:, bass.ds(c + j, 1)]

                def unit(i, d, first):
                    vn = v0 + 1 + d
                    f = 2 * i + d
                    dve.wait_ge(hi_ready, vn + 1 + 2 * i)
                    dve.tensor_tensor(wlo[:, vn % 2, :], wraw[:, (up0 + 1 + d) % 2, :], whi[:, vn % 2, :].bitcast(F32),
                                      ALU.subtract).then_inc(lo_ready, 1)
                    dve.wait_ge(tile_read["act"], FA + d + 2 * i)
                    ab = abuf[:, d, :]
                    carried = stT[:, bass.ds(f, 1), :].rearrange("p a (b j) -> p (a b) j", j=2)
                    wj = [one(V_CW + KF * j, f) for j in range(3)]
                    cb = one(V_CB, f)
                    if not (first and d == 0):
                        dve.wait_ge(s("g_lo"), f)
                    dve.tensor_scalar(acc[:, 0:TP], ab[:, 0:TP], wj[0], cb, ALU.mult, ALU.add)
                    dve.tensor_scalar(acc[:, TP:T], carried[:, :, 0], wj[0], cb, ALU.mult, ALU.add).then_inc(conv, 1)
                    dve.wait_ge(conv, 4 * i + 2 * d + 1)
                    dve.scalar_tensor_tensor(acc[:, 0:TP], ab[:, 1:TP + 1], wj[1], acc[:, 0:TP], ALU.mult, ALU.add)
                    dve.scalar_tensor_tensor(acc[:, TP:T], carried[:, :, 1], wj[1], acc[:, TP:T], ALU.mult, ALU.add)\
                       .then_inc(conv, 1)
                    dve.wait_ge(conv, 4 * i + 2 * d + 2)
                    dve.scalar_tensor_tensor(acc, ab[:, 2:T + 2], wj[2], acc, ALU.mult, ALU.add).then_inc(s("conv_done"), 1)
                    dve.wait_ge(s("ffn_sig"), f + 1)
                    dve.tensor_tensor(acc, acc, sg5, ALU.mult).then_inc(s("silu"), 1)
                    dve.wait_ge(s("silu"), f + 1)
                    dve.wait_ge(pass_done, p0 + 2 * d + 2 + 4 * i)
                    dve.tensor_tensor(halves(acc), halves(acc), banks(t0 + 1), ALU.mult).then_inc(tile_read["dve"], 1)
                    dve.wait_ge(s("g_hi"), f + 1)
                    dve.tensor_tensor(gL[:, bass.ds(f, 1), :].rearrange("p a t -> p (a t)"), acc,
                                      gH[:, bass.ds(f, 1), :].rearrange("p a t -> p (a t)").bitcast(F32), ALU.subtract)\
                       .then_inc(s("g_lo"), 1)

                modulate_dve(dve, 1, xT, n2, V_N2, 3 * KD, 4 * KD)

                def gain(k):
                    dve.wait_ge(s("sq_ready"), 2 * KD + k + 1)
                    dve.tensor_scalar(xT[:, k, :], xT[:, k, :], vec[:, V_NF + k:V_NF + k + 1], None, ALU.mult)\
                       .then_inc(s("gained"), 1)

                def tail(i, d, first):
                    dve.wait_ge(s("tail_T"), 2 * i + d + 1)
                    if not first:
                        dve.wait_ge(s(f"conv_out{d}"), 32 * i)
                    dve.tensor_copy(ast[:, d, :], ps[0:NS + 2, 6 + d, 0:P]).then_inc(s("tail_tok"), 1)

                unit(0, 0, True)
                unit(0, 1, True)
                tail(0, 0, True)
                with dve.Fori(1, KF // 2) as i:
                    unit(i, 0, False)
                    dve.wait_ge(s("tail_T"), 2 * i)
                    dve.wait_ge(s("conv_out1"), 32 * i - 32)
                    dve.tensor_copy(ast[:, 1, :], ps[0:NS + 2, 7, 0:P]).then_inc(s("tail_tok"), 1)
                    unit(i, 1, False)
                    tail(i, 0, False)
                tail(KF // 2 - 1, 1, False)
                dve.wait_ge(s("g_lo"), KF)
                for m in range(KD):
                    for half in range(2):
                        split_lo(dve, vd0 + 2 * m + half + 1)
                    n = td0 + m
                    dve.wait_ge(pass_done, passes[n])
                    residual_dve(dve, n, m, 5 * KD)
                    square_dve(dve, 2, m - 1, n3)
                    if m >= 1:
                        gain(m - 1)
                square_dve(dve, 2, KD - 1, n3)
                gain(KD - 1)
                dve.wait_ge(s("sq_summed"), 3)
                dve.tensor_scalar(tok["v"][:, 0:4], ps[:, 3, 0:4], 1.0 / D, EPS, ALU.mult, ALU.add)
                dve.tensor_scalar(tok["v"][0:NS, 4:5], ps[0:NS, 3, 4:5], 1.0 / D, EPS, ALU.mult, ALU.add)\
                   .then_inc(s("ms_ready"), 1)
                dve.wait_ge(s("rs_ready"), 3)
                newton(dve, tok["v"], tok["y"], tok["t"], tok["r"]).then_inc(s("y_ready"), 1)
                dve.wait_ge(s("y_ready"), 1)
                for n in (1, 3):
                    dve.wait_ge(s("y_T"), n + 1)
                    dve.tensor_scalar(yst[:, n, :].rearrange("p (a b) -> p a b", a=2), ps[:, YB[n]:YB[n] + 2, :],
                                      tok["r"][:, n:n + 1], None, ALU.mult).then_inc(s("y_tok_dve"), 1)

            @block.tensor
            def _(pe):
                def unit(i, d, first):
                    f = 2 * i + d
                    pe.wait_ge(lo_ready, v0 + d + 1 + 2 * i)
                    for m in range(2):
                        n = t0 + 2 * d + m
                        if first:
                            pe.wait_ge(tile_read[owner[n - 2]], freed[n - 2])
                        else:
                            pe.wait_ge(tile_read["act" if m == 0 else "dve"], (FA if m == 0 else FD) + d - 1 + 2 * i)
                        for k in range(KD):
                            if first and d == 0 and m == 0:
                                pe.wait_ge(s("h_split"), KD + k + 1)
                            last = three_pass(pe, n, (v0 + d) % 2, [KD * m + k], actH, actL, k0=k, begin=k == 0,
                                              end=k == KD - 1)
                        last.then_inc(pass_done, 1)

                def tail(i, d, first):
                    pe.wait_ge(tile_read["act"], FA + d + 2 * i)
                    if not first:
                        pe.wait_ge(s("tail_tok"), 2 * i + d - 1)
                    pe.transpose(ps[0:NS + 2, 6 + d, 0:P], abuf[:, d, TP:T + 2], ident).then_inc(s("tail_T"), 1)

                unit(0, 0, True)
                unit(0, 1, True)
                tail(0, 0, True)
                with pe.Fori(1, KF // 2) as i:
                    unit(i, 0, False)
                    pe.wait_ge(tile_read["act"], FA - 1 + 2 * i)
                    pe.wait_ge(s("tail_tok"), 2 * i - 1)
                    pe.transpose(ps[0:NS + 2, 7, 0:P], abuf[:, 1, TP:T + 2], ident).then_inc(s("tail_T"), 1)
                    unit(i, 1, False)
                    tail(i, 0, False)
                pe.wait_ge(tile_read["act"], FA + KF - 1)
                pe.wait_ge(s("tail_tok"), KF - 1)
                pe.transpose(ps[0:NS + 2, 7, 0:P], abuf[:, 1, TP:T + 2], ident).then_inc(s("tail_T"), 1)
                pe.wait_ge(s("g_lo"), KF)

                def down(m, i, first):
                    n = td0 + m
                    for half in range(2):
                        pe.wait_ge(lo_ready, vd0 + 2 * m + half + 1 + 4 * i)
                        if half == 0 and first:
                            pe.wait_ge(tile_read[owner[n - 2]], freed[n - 2])
                        elif half == 0:
                            pe.wait_ge(tile_read["dve"], freed[td0] + m - 2 + 2 * i)
                        three_pass(pe, n, (vd0 + half) % 2, list(range(KF // 2)), gH, gL, k0=half * (KF // 2),
                                   begin=half == 0, end=half == 1).then_inc(pass_done, 1)

                for m in range(2):
                    down(m, 0, True)
                with pe.Fori(0, KD // 2 - 1) as i:
                    for m in range(2):
                        down(2 + m, i, False)
                def turn(n, tiles):
                    m = P if n < 4 else NS
                    for k in tiles:
                        last = pe.transpose(ps[0:m, YB[n] + k // 4, P * (k % 4):P * (k % 4) + P],
                                            xT[:, k, P * n:P * n + m], ident)
                    return last

                pe.wait_ge(s("gained"), KD - 1)
                for n in range(3):
                    turn(n, range(KD - 1))
                pe.wait_ge(s("sq_added"), 3 * (KD - 1))
                for n in range(5):
                    m = P if n < 4 else NS
                    last = pe.matmul(ps[0:m, 3, n:n + 1], n3["t"][:, P * n:P * n + m], ones[:, 0:1], start=True, stop=True)
                last.then_inc(s("sq_summed"), 1)
                pe.wait_ge(s("gained"), KD)
                for n in range(3):
                    turn(n, [KD - 1]).then_inc(s("y_T"), 1)
                pe.wait_ge(s("ms_ready"), 3)
                turn(3, range(KD)).then_inc(s("y_T"), 1)
                pe.wait_ge(s("y_tok"), 1)
                turn(4, range(KD)).then_inc(s("y_T"), 1)


def bucket(dist):
    d = np.maximum(dist, 1).astype(np.float32)
    large = 16 + (np.log(d / 16) / np.log(2048 / 16) * 16).astype(np.int32)
    return np.where(dist < 16, dist, np.minimum(large, 31)).astype(np.int32)


def constants():
    i = np.arange(P)
    same = (i[:, None] // CH == i[None, :] // CH) & (i[:, None] <= i[None, :])
    cst = np.concatenate([np.eye(P), same / 16.0, same, np.eye(P)[::-1]], axis=1).astype(np.float32)
    x = np.arange(BW)
    hot = np.zeros((33, NG * (BW + SK)), np.float32)

    def fill(c0, dist, valid):
        b = bucket(np.where(valid, dist, 0))
        cols = c0 + np.arange(len(dist))
        hot[b[valid], cols[valid]] = 1.0
        hot[32, cols[~valid]] = NEG

    d = 2 * P - 1 - x
    fill(0, d, (d >= 0) & (d <= P))
    d = P - 1 - x
    fill(BW, 4 * d, d >= 0)
    fill(2 * BW, 4 * d, (d >= 0) & (d % 4 == 0))
    r = np.arange(SK)
    for g, (dil, reach) in enumerate(((1, P), (4, P), (16, P // 2))):
        m = np.where(r == P, 0, reach - r)
        fill(NG * BW + SK * g, dil * m, m >= 0 if reach == P else (r == P) | (r < reach))
    rows = np.arange(NS * AH)
    sel64 = (rows[:, None] // AH == np.arange(NS)[None, :]).astype(np.float32)
    hmask = (rows[:, None] % AH == np.arange(AH)[None, :]).astype(np.float32)
    return {"cst": cst, "onehot": hot, "sel8": np.ascontiguousarray(sel64.T), "sel64": sel64, "hmask": hmask}


_INS = {
    "x_prompt": (TP, D), "x_sample": (NS, D), "state_gla": (NS, GH, GDK, GDV),
    "cache_win1": (NS, WIN[0], 2 * AG), "cache_win2": (NS, WIN[1], 2 * AG), "cache_win3": (NS, WIN[2], 2 * AG),
    "state_conv": (NS, 2, FH), "c_prompt": (1, D), "c_sample": (NS, D), "w_ada": (D, 6 * D), "b_ada": (6 * D,),
    "norm1_g": (D,), "w_in": (D, C_GB + D), "gla_wg2": (GR, GH * GDK), "gla_bg": (GH * GDK,), "gla_norm_g": (GDV,),
    "w_branch_a": (D, D), "w_branch_b": (AG, D), "w_out": (D, D), "rel_bias": (32, NG * AH), "norm2_g": (D,),
    "w_up": (D, 2 * FH), "conv_w": (3, FH), "conv_b": (FH,), "w_down": (FH, D), "normf_g": (D,),
}
_OUTS = {
    "y_prompt": ((TP, D), (1, TP, D)), "y_sample": ((NS, D), (NS, 1, D)),
    "gla_p": ((GH, GDK, GDV), (1, 1, GH, GDK, GDV)), "gla_s": ((NS, GH, GDK, GDV), (1, NS, GH, GDK, GDV)),
    "win1_p": ((P, 2 * AG), (1, 1, P, 2, AH, AE)), "win1_s": ((NS, WIN[0], 2 * AG), (1, NS, WIN[0], 2, AH, AE)),
    "win2_p": ((TP, 2 * AG), (1, 1, TP, 2, AH, AE)), "win2_s": ((NS, WIN[1], 2 * AG), (1, NS, WIN[1], 2, AH, AE)),
    "win3_p": ((TP, 2 * AG), (1, 1, TP, 2, AH, AE)), "win3_s": ((NS, WIN[2], 2 * AG), (1, NS, WIN[2], 2, AH, AE)),
    "conv_p": ((2, FH), (1, 1, 2, FH)), "conv_s": ((NS, 2, FH), (1, NS, 2, FH)),
}


def kernel(**inputs):
    import numpy as _np
    import concourse.bacc as _bacc
    from concourse.bass_utils import run_bass_kernel_spmd as _run

    nc = _bacc.Bacc("TRN2", target_bir_lowering=False, num_devices=1)
    arrays, w, con, o = {}, {}, {}, {}
    for name, shape in _INS.items():
        arrays[f"in_{name}"] = _np.ascontiguousarray(_np.asarray(inputs[name]).reshape(shape))
        w[name] = nc.dram_tensor(f"in_{name}", shape, F32, kind="ExternalInput").ap()
    for name, a in constants().items():
        arrays[f"in_{name}"] = a
        con[name] = nc.dram_tensor(f"in_{name}", a.shape, F32, kind="ExternalInput").ap()
    for name, (shape, _) in _OUTS.items():
        o[name] = nc.dram_tensor(f"out_{name}", shape, F32, kind="ExternalOutput").ap()
    program(nc, w, o, con)
    r = _run(nc, [arrays], core_ids=[0])
    return tuple(r.results[0][f"out_{name}"].reshape(full) for name, (_, full) in _OUTS.items())
```
